# Optimizing a Trainium2 kernel written in Bass

```python
import math
import jax, jax.numpy as jnp
from jax import lax
import numpy as np

D_MODEL = 1024
BATCH = 1
SEQ = 1024
DEPTH = 2
DEC_BATCH = 8
DEC_SEQ = 4
PAST_LEN = 1024
PAGE_SIZE = 128

N_A = DEPTH // 2
N_B = DEPTH - N_A
H_A = 8
DH_A = D_MODEL // H_A
D_A = H_A * DH_A
MLSTM_CHUNK = 64
F_BIAS_LO = 3.0
F_BIAS_HI = 6.0
H_B = 8
DK_B = D_MODEL // (2 * H_B)
DV_B = 2 * DK_B
D_B = H_B * DV_B
QK_B = H_B * 2 * DK_B
Q_BLOCK = 128
ATTN_SCALE = DK_B ** -0.5
ROPE_THETA = 10000.0
EPS = 1e-6
A_IN = 5 * D_A + 2 * H_A
B_IN = QK_B + D_B
KV_OUT = QK_B + D_B

kernel_name = 'yoco_mlstm_diffattn_step'

F32 = jnp.float32

def rmsnorm(x, g):
    xf = x.astype(F32)
    y = xf * lax.rsqrt(jnp.mean(xf * xf, axis=-1, keepdims=True) + EPS)
    return (y * g.astype(F32)).astype(x.dtype)

def head_rmsnorm(h, g):
    hf = h.astype(F32)
    return hf * lax.rsqrt(jnp.mean(hf * hf, axis=-1, keepdims=True) + EPS) * g.astype(F32)

def rope(x, pos):
    half = DK_B // 2
    inv = ROPE_THETA ** (-(jnp.arange(half, dtype=F32) / half))
    ang = pos[:, None] * inv[None, :]
    cos = jnp.cos(ang)[None, :, None, None, :]
    sin = jnp.sin(ang)[None, :, None, None, :]
    xf = x.astype(F32)
    x1, x2 = xf[..., :half], xf[..., half:]
    return jnp.concatenate([x1 * cos - x2 * sin, x2 * cos + x1 * sin], axis=-1).astype(x.dtype)

def mlstm_cell(q, k, v, i_pre, log_f, c0, n0, m0):
    bsz, t_, h_, d_ = q.shape
    L = MLSTM_CHUNK if t_ % MLSTM_CHUNK == 0 else t_
    nc = t_ // L

    def to_chunks(a):
        a = a.reshape((bsz, nc, L, h_) + a.shape[3:])
        return jnp.moveaxis(a, (1, 3), (0, 2))

    tril = jnp.tril(jnp.ones((L, L), dtype=bool))

    def body(carry, xs):
        c, n, m = carry
        qc, kc, vc, ic, fc = xs
        bcum = jnp.cumsum(fc, axis=-1)
        d = bcum[..., :, None] - bcum[..., None, :] + ic[..., None, :]
        d = jnp.where(tril, d, -jnp.inf)
        inter = bcum + m[..., None]
        mj = jnp.maximum(inter, jnp.max(d, axis=-1))
        w_inter = jnp.exp(inter - mj)
        a = jnp.exp(d - mj[..., None]) * jnp.einsum('bhjd,bhsd->bhjs', qc, kc)
        num = w_inter[..., None] * jnp.einsum('bhvk,bhjk->bhjv', c, qc) + jnp.einsum('bhjs,bhsv->bhjv', a, vc)
        den = w_inter * jnp.einsum('bhk,bhjk->bhj', n, qc) + jnp.sum(a, axis=-1)
        h = num / jnp.maximum(jnp.abs(den), jnp.exp(-mj))[..., None]
        b_last = bcum[..., -1]
        g = b_last[..., None] - bcum + ic
        m_new = jnp.maximum(b_last + m, jnp.max(g, axis=-1))
        decay = jnp.exp(b_last + m - m_new)
        wg = jnp.exp(g - m_new[..., None])
        c_new = decay[..., None, None] * c + jnp.einsum('bhs,bhsv,bhsk->bhvk', wg, vc, kc)
        n_new = decay[..., None] * n + jnp.einsum('bhs,bhsk->bhk', wg, kc)
        return (c_new, n_new, m_new), h

    xs = (to_chunks(q), to_chunks(k), to_chunks(v), to_chunks(i_pre), to_chunks(log_f))
    (c1, n1, m1), hs = lax.scan(body, (c0, n0, m0), xs)
    hs = jnp.moveaxis(hs, (0, 2), (1, 3)).reshape(bsz, t_, h_, d_)
    return hs, c1, n1, m1

def mlstm_layer(x, g, w_in, b_i, b_f, hnorm, w_out, c0, n0, m0):
    bsz, t_, _ = x.shape
    p = rmsnorm(x, g) @ w_in
    q, k, v, o, z, gi, gf = jnp.split(p, [D_A, 2 * D_A, 3 * D_A, 4 * D_A, 5 * D_A, 5 * D_A + H_A], axis=-1)
    heads = lambda a: a.reshape(bsz, t_, H_A, DH_A).astype(F32)
    i_pre = gi.astype(F32) + b_i.astype(F32)
    log_f = jax.nn.log_sigmoid(gf.astype(F32) + b_f.astype(F32))
    hc, c1, n1, m1 = mlstm_cell(heads(q), heads(k) * (DH_A ** -0.5), heads(v), i_pre, log_f,
                                c0.astype(F32), n0.astype(F32), m0.astype(F32))
    hc = jax.nn.sigmoid(heads(o)) * hc
    hc = head_rmsnorm(hc, hnorm.reshape(H_A, DH_A))
    y = (hc.reshape(bsz, t_, D_A).astype(x.dtype) * jax.nn.silu(z)) @ w_out
    return x + y, c1, n1, m1

def shared_kv(x, g, w_kv, pos):
    bsz, t_, _ = x.shape
    p = rmsnorm(x, g) @ w_kv
    k = rope(p[..., :QK_B].reshape(bsz, t_, H_B, 2, DK_B), pos)
    v = p[..., QK_B:].reshape(bsz, t_, H_B, DV_B)
    return k, v

def diff_mix(q, k_parts, v_parts, masks, lam):
    scores = []
    for kp, mk in zip(k_parts, masks):
        s = jnp.einsum('bqhcd,bkhcd->bhcqk', q, kp).astype(F32) * ATTN_SCALE
        if mk is not None:
            s = jnp.where(mk, s, -jnp.inf)
        scores.append(s)
    p = jax.nn.softmax(jnp.concatenate(scores, axis=-1), axis=-1)
    w = p[:, :, 0] - lam * p[:, :, 1]
    out = None
    start = 0
    for vp in v_parts:
        s_len = vp.shape[1]
        o = jnp.einsum('bhqk,bkhe->bqhe', w[..., start:start + s_len].astype(vp.dtype), vp)
        out = o if out is None else out + o
        start += s_len
    return out

def make_attend(k_new, v_new, past):
    if past is None:
        def attend(q, lam):
            bsz, t_ = q.shape[:2]
            nb = t_ // Q_BLOCK
            qb = jnp.moveaxis(q.reshape(bsz, nb, Q_BLOCK, H_B, 2, DK_B), 1, 0)
            kpos = jnp.arange(t_)

            def one(args):
                qi, start = args
                qpos = start + jnp.arange(Q_BLOCK)
                mask = qpos[:, None] >= kpos[None, :]
                return diff_mix(qi, (k_new,), (v_new,), (mask,), lam)

            out = lax.map(one, (qb, jnp.arange(nb) * Q_BLOCK))
            return jnp.moveaxis(out, 0, 1).reshape(bsz, t_, H_B, DV_B)
        return attend
    k_past, v_past = past

    def attend(q, lam):
        t_ = q.shape[1]
        causal = jnp.tril(jnp.ones((t_, t_), dtype=bool))
        return diff_mix(q, (k_past, k_new), (v_past, v_new), (None, causal), lam)
    return attend

def diff_layer(x, g, w_in, lq1, lk1, lq2, lk2, subln, w_out, pos, attend, lam_init):
    bsz, t_, _ = x.shape
    p = rmsnorm(x, g) @ w_in
    q = rope(p[..., :QK_B].reshape(bsz, t_, H_B, 2, DK_B), pos)
    z = p[..., QK_B:]
    lam = (jnp.exp(jnp.sum(lq1.astype(F32) * lk1.astype(F32)))
           - jnp.exp(jnp.sum(lq2.astype(F32) * lk2.astype(F32))) + lam_init)
    o = head_rmsnorm(attend(q, lam), subln) * (1.0 - lam_init)
    y = (o.reshape(bsz, t_, D_B).astype(x.dtype) * jax.nn.silu(z)) @ w_out
    return x + y

def trunk(x, pos, c_in, n_in, m_in, past, norm_g, w_in_a, b_i_a, b_f_a, hnorm_a, w_out_a,
          kv_norm_g, w_kv, w_in_b, lam_q1, lam_k1, lam_q2, lam_k2, subln_b, w_out_b, final_norm_g):
    cs, ns, ms = [], [], []
    k_new = v_new = attend = None
    for l in range(DEPTH):
        if l < N_A:
            x, c1, n1, m1 = mlstm_layer(x, norm_g[l], w_in_a[l], b_i_a[l], b_f_a[l], hnorm_a[l], w_out_a[l],
                                        c_in[l], n_in[l], m_in[l])
            cs.append(c1)
            ns.append(n1)
            ms.append(m1)
            if l == N_A - 1:
                k_new, v_new = shared_kv(x, kv_norm_g, w_kv, pos)
                attend = make_attend(k_new, v_new, past)
        else:
            j = l - N_A
            lam_init = 0.8 - 0.6 * math.exp(-0.3 * l)
            x = diff_layer(x, norm_g[l], w_in_b[j], lam_q1[j], lam_k1[j], lam_q2[j], lam_k2[j],
                           subln_b[j], w_out_b[j], pos, attend, lam_init)
    y = rmsnorm(x, final_norm_g)
    return y, k_new, v_new, jnp.stack(cs), jnp.stack(ns), jnp.stack(ms)

def setup_inputs(seed: int = 0) -> dict:
    key = jax.random.key(seed)
    ks = jax.random.split(key, 24)
    n_pages = PAST_LEN // PAGE_SIZE
    n_used = DEC_BATCH * n_pages
    n_pool = n_used + max(1, n_used // 4)
    nrm = lambda k, shape, s: jax.random.normal(k, shape, F32) * s
    return {
        'x_prompt': nrm(ks[0], (BATCH, SEQ, D_MODEL), 1.0),
        'x_sample': nrm(ks[1], (DEC_BATCH, DEC_SEQ, D_MODEL), 1.0),
        'cache_k': nrm(ks[2], (n_pool, PAGE_SIZE, H_B, 2, DK_B), 1.0),
        'cache_v': nrm(ks[3], (n_pool, PAGE_SIZE, H_B, DV_B), 1.0),
        'state_C': nrm(ks[4], (N_A, DEC_BATCH, H_A, DH_A, DH_A), 0.5),
        'state_n': nrm(ks[5], (N_A, DEC_BATCH, H_A, DH_A), 0.5),
        'state_m': nrm(ks[6], (N_A, DEC_BATCH, H_A), 1.0),
        'page_table': jax.random.permutation(ks[7], n_pool)[:n_used].reshape(DEC_BATCH, n_pages).astype(jnp.int32),
        'norm_g': 1.0 + nrm(ks[8], (DEPTH, D_MODEL), 0.02),
        'w_in_a': nrm(ks[9], (N_A, D_MODEL, A_IN), D_MODEL ** -0.5),
        'b_i_a': nrm(ks[10], (N_A, H_A), 0.1),
        'b_f_a': jnp.linspace(F_BIAS_LO, F_BIAS_HI, H_A, dtype=F32)[None, :] + nrm(ks[11], (N_A, H_A), 0.1),
        'hnorm_a': 1.0 + nrm(ks[12], (N_A, D_A), 0.02),
        'w_out_a': nrm(ks[13], (N_A, D_A, D_MODEL), D_A ** -0.5),
        'kv_norm_g': 1.0 + nrm(ks[14], (D_MODEL,), 0.02),
        'w_kv': nrm(ks[15], (D_MODEL, KV_OUT), D_MODEL ** -0.5),
        'w_in_b': nrm(ks[16], (N_B, D_MODEL, B_IN), D_MODEL ** -0.5),
        'lam_q1': nrm(ks[17], (N_B, DK_B), 0.1),
        'lam_k1': nrm(ks[18], (N_B, DK_B), 0.1),
        'lam_q2': nrm(ks[19], (N_B, DK_B), 0.1),
        'lam_k2': nrm(ks[20], (N_B, DK_B), 0.1),
        'subln_b': 1.0 + nrm(ks[21], (N_B, DV_B), 0.02),
        'w_out_b': nrm(ks[22], (N_B, D_B, D_MODEL), D_B ** -0.5),
        'final_norm_g': 1.0 + nrm(ks[23], (D_MODEL,), 0.02),
    }

def reference(x_prompt, x_sample, cache_k, cache_v, state_C, state_n, state_m, page_table,
              norm_g, w_in_a, b_i_a, b_f_a, hnorm_a, w_out_a, kv_norm_g, w_kv, w_in_b,
              lam_q1, lam_k1, lam_q2, lam_k2, subln_b, w_out_b, final_norm_g):
    bp, tp, _ = x_prompt.shape
    c0 = jnp.zeros((N_A, bp, H_A, DH_A, DH_A), F32)
    n0 = jnp.zeros((N_A, bp, H_A, DH_A), F32)
    m0 = jnp.zeros((N_A, bp, H_A), F32)
    pos_p = jnp.arange(tp, dtype=F32)
    y_p, k_p, v_p, c_p, n_p, m_p = trunk(
        x_prompt, pos_p, c0, n0, m0, None, norm_g, w_in_a, b_i_a, b_f_a, hnorm_a, w_out_a,
        kv_norm_g, w_kv, w_in_b, lam_q1, lam_k1, lam_q2, lam_k2, subln_b, w_out_b, final_norm_g)
    db, ts, _ = x_sample.shape
    past_len = page_table.shape[1] * PAGE_SIZE
    k_past = cache_k[page_table].reshape((db, past_len) + cache_k.shape[2:])
    v_past = cache_v[page_table].reshape((db, past_len) + cache_v.shape[2:])
    pos_s = past_len + jnp.arange(ts, dtype=F32)
    y_s, k_s, v_s, c_s, n_s, m_s = trunk(
        x_sample, pos_s, state_C, state_n, state_m, (k_past, v_past), norm_g, w_in_a, b_i_a, b_f_a,
        hnorm_a, w_out_a, kv_norm_g, w_kv, w_in_b, lam_q1, lam_k1, lam_q2, lam_k2, subln_b, w_out_b,
        final_norm_g)
    sd = state_C.dtype
    xd = x_prompt.dtype
    return (y_p, y_s, k_p, v_p, c_p.astype(xd), n_p.astype(xd), m_p.astype(xd),
            k_s, v_s, c_s.astype(sd), n_s.astype(sd), m_s.astype(sd))


_drawn_inputs = setup_inputs


def setup_inputs(seed=0):
    import zlib

    import numpy as np

    out = dict(_drawn_inputs(seed))
    spreads = {}
    factors = {'hnorm_a': 4.908,
     'kv_norm_g': 2.875,
     'lam_q1': 3.192,
     'lam_k1': 6.492,
     'lam_q2': 7.235,
     'lam_k2': 8.0,
     'subln_b': 8.0,
     'final_norm_g': 2.912}
    for name, (base, spread) in spreads.items():
        noise = np.random.default_rng([zlib.crc32(name.encode()), seed]).standard_normal(out[name].shape)
        drawn = base * np.exp(spread * noise) if base else spread * noise
        out[name] = __import__('jax').numpy.asarray(drawn.astype(out[name].dtype))
    for name, factor in factors.items():
        out[name] = (out[name] * factor).astype(out[name].dtype)
    return out
```

```python
from contextlib import ExitStack

import numpy as np

import concourse.bass as bass
from concourse import mybir

ALU = mybir.AluOpType
ACT = mybir.ActivationFunctionType
F32 = mybir.dt.float32
F32R = mybir.dt.float32r
I32 = mybir.dt.int32
AX = mybir.AxisListType.X

P = 128
D = 1024
KT = D // P
H = 8
NT = 8
SEQ = NT * P
DB, DS = 8, 4
TS = DB * DS
TOK = SEQ + TS
NB = NT + 1
PAGES = 8
DK = 64
HALF = DK // 2
EPS = 1e-6
BIG = 1e30
LAM_INIT = 0.8 - 0.6 * float(np.exp(-0.3))
ATTN_SCALE = DK ** -0.5
K_SCALE = P ** -0.5

C_ID = 0
C_MA = C_ID + P
C_MB = C_MA + P
C_COS = C_MB + P
C_SIN = C_COS + NB * HALF
C_MS = C_SIN + NB * HALF
C_ONE = C_MS + TS
C_COMP = C_ONE + DB
C_NEW = C_COMP + 2
C_EXP = C_NEW + DB * TS
C_C1 = C_EXP + 2
C_N = C_C1 + 1


def constants():
    c = np.zeros((P, C_N), np.float32)
    r = np.arange(P)
    c[:, C_ID:C_ID + P] = np.eye(P)
    c[:, C_MA:C_MA + P] = np.where(r[:, None] <= r[None, :], 0.0, BIG)
    c[:, C_MB:C_MB + P] = np.where(r[None, :] <= r[:, None], 0.0, -BIG)
    inv = (np.float32(10000.0) ** (-(np.arange(HALF, dtype=np.float32) / np.float32(HALF)))).astype(np.float32)
    for t in range(NB):
        pos = (t * P + r if t < NT else PAGES * P + r % DS).astype(np.float32)
        ang = pos[:, None] * inv[None, :]
        c[:, C_COS + t * HALF:C_COS + (t + 1) * HALF] = np.cos(ang)
        c[:, C_SIN + t * HALF:C_SIN + (t + 1) * HALF] = np.sin(ang)
    s = np.arange(TS)
    own = (s[:, None] // DS == s[None, :] // DS)
    c[:TS, C_MS:C_MS + TS] = np.where(own & (s[:, None] <= s[None, :]), 0.0, BIG)
    c[:TS, C_ONE:C_ONE + DB] = s[:, None] // DS == np.arange(DB)[None, :]
    c[:, C_COMP:C_COMP + 2] = r[:, None] // DK == np.arange(2)[None, :]
    q = np.arange(64) % DS
    for b in range(DB):
        ok = (s[None, :] // DS == b) & (s[None, :] % DS <= q[:, None])
        c[:64, C_NEW + b * TS:C_NEW + (b + 1) * TS] = np.where(ok, 0.0, -BIG)
    c[:, C_EXP] = -0.5
    c[:, C_EXP + 1] = 1.0
    c[:, C_C1] = r // DS % 2
    return c


class Chain:

    def __init__(self, eng, sem):
        self.eng, self.sem, self.base, self.n = eng, sem, 0, 0

    def link(self, ins):
        ins.then_inc(self.sem, 1)
        self.n += 1
        self.eng.wait_ge(self.sem, self.base + self.n)

    def enter(self, i, per):
        self.start, self.base, self.n, self.per = self.base + self.n, self.base + self.n + i * per, 0, per

    def leave(self, times):
        assert self.n == self.per, f"links in a turn: {self.n}"
        self.base, self.n = self.start + times * self.per, 0


def trunk_step(
    nc: bass.Bass,
    x_prompt, x_sample, cache_k, cache_v, state_C, state_n, state_m, page_table,
    norm_g, w_in_a, b_i_a, b_f_a, hnorm_a, w_out_a, kv_norm_g, w_kv, w_in_b,
    lam_q1, lam_k1, lam_q2, lam_k2, subln_b, w_out_b, final_norm_g, consts,
    y_p, y_s, k_p, v_p, c_p, n_p, m_p, k_s, v_s, c_s, n_s, m_s,
):
    ctx = ExitStack()

    def sb(name, shape, dt=F32):
        return ctx.enter_context(nc.sbuf_tensor(name, shape, dt))

    held = []

    def sem(name):
        held.append(nc.alloc_semaphore(name=name))
        return held[-1]

    scratch = []

    def phase_tensor(name, shape, dt=F32):
        return scratch[-1].enter_context(nc.sbuf_tensor(name, shape, dt))

    def run(program, *args):
        scratch.append(ExitStack())
        program(*args)
        scratch.pop().close()
        nc.clear_and_free_semaphores(list(held))
        held.clear()
        nc.all_engine_barrier()

    def two(name):
        return [sem(f"{name}{k}") for k in range(2)]

    consts_in = nc.alloc_semaphore(name="consts_in")

    passed = nc.alloc_semaphore(name="passed")

    def apart(eng):
        eng.sem_inc(passed, 1)

    def dram(name, shape):
        return nc.dram_tensor(name, shape, F32, kind="Internal").ap()

    with ctx:
        cst = sb("cst", [P, C_N])
        ident = cst[:, C_ID:C_ID + P]
        XH = sb("XH", [P, KT, TOK], F32R)
        XL = sb("XL", [P, KT, TOK], F32R)
        YX = sb("YX", [P, NB * D])
        YT = YX[:, 0:KT * TOK].rearrange("p (k t) -> p k t", k=KT)
        X1 = YX[:, :].rearrange("p (b n) -> p b n", b=NB)
        WH = sb("WH", [P, KT * 640], F32R)
        WL = sb("WL", [P, KT * 640], F32R)
        RAW = sb("RAW", [P, KT * 640])
        gA = sb("gA", [P, KT])
        gB = sb("gB", [P, KT])
        gKV = sb("gKV", [P, KT])
        one_row = cst[:, C_EXP + 1:C_EXP + 2]
        neg_half = cst[:, C_EXP:C_EXP + 1]
        PS = [ctx.enter_context(nc.psum_tensor(f"PS{k}", [P, 512], F32)) for k in range(4)]
        PD = [ctx.enter_context(nc.psum_tensor(f"PD{k}", [P, 2, 512], F32)) for k in range(2)]
        BK = [PS[0][:, :], PS[1][:, :], PS[2][:, :], PS[3][:, :],
              PD[0][:, 0, :], PD[0][:, 1, :], PD[1][:, 0, :], PD[1][:, 1, :]]

        AREA = 9430
        areas = []

        def area(size=AREA):
            areas.append(size)
            work = phase_tensor(f"WORK{len(areas)}", [P, size])
            at = [0]

            def take(*shape):
                n = int(np.prod(shape))
                v = work[:, at[0]:at[0] + n]
                at[0] += n
                assert at[0] <= size, at[0]
                if len(shape) == 1:
                    return v
                if len(shape) == 2:
                    return v.rearrange("p (a b) -> p a b", a=shape[0])
                return v.rearrange("p (a b c) -> p a b c", a=shape[0], b=shape[1])
            return take

        d_G = dram("d_G", [H, TOK])
        d_dec = dram("d_dec", [H, 2 * NT])
        d_smA = dram("d_smA", [TS, 5, D])
        d_smB = dram("d_smB", [TS, 4, D])
        d_x1 = dram("d_x1", [TOK, D])
        d_av = dram("d_av", [DB, 64, D])

        COL = sb("COL", [P, NB, 4, H])
        LAM = sb("LAM", [P, 1])
        PT = sb("PT", [1, DB * PAGES], I32)
        DEC = sb("DEC", [P, H * 2 * NT])

        def tok(j, n):
            return bass.ds(j * P, n)

        def norm_phase(tag, first):
            take = area()
            if first:
                take(2600)
            xin = take(2, D)
            xn = take(2, D)
            junk = take(2, D)
            ss = take(2)
            var = take(2)
            rs = take(2)
            ld, sq, rr, xs, tp, hi, lo, st = (two(f"{tag}_{s}") for s in ("ld", "sq", "rs", "xn", "tp", "hi", "lo", "st"))
            pch = sem(f"{tag}_pool")

            def each_pair(eng, body):
                with eng.Fori(0, NT // 2) as i:
                    body(i, ((0, P), (1, P)))
                body(NT // 2, ((0, TS),))

            def source(i, b, n):
                return xin[0:n, b, :] if first else X1[0:n, bass.ds(2 * i + b, 1), :].rearrange("p a n -> p (a n)")

            with nc.Block() as block:
                @block.sync
                def _(sp):
                    if first:
                        sp.dma_start(cst[:, :], consts).then_inc(consts_in, 16)

                    def load(i, slots):
                        for b, n in slots:
                            if first:
                                sp.wait_ge(xs[b], i)
                                src = x_prompt[0, bass.ds((2 * i + b) * P, P), :] if n == P else \
                                    x_sample.rearrange("b s n -> (b s) n")
                                sp.dma_start(xin[0:n, b, :], src).then_inc(ld[b], 16)
                            else:
                                sp.dma_start(d_x1[tok(2 * i + b, n), :], source(i, b, n)).then_inc(st[b], 16)
                                sp.wait_ge(st[b], 16 * (i + 1))
                                apart(sp)
                    each_pair(sp, load)

                @block.scalar
                def _(act):
                    if first:
                        with nc.allow_non_contiguous_dma("gains by contraction row"):
                            for g, v in ((gA, norm_g[0, :]), (gB, norm_g[1, :]), (gKV, kv_norm_g)):
                                act.dma_start(g[:, :], v.rearrange("(k p) -> p k", p=P)).then_inc(consts_in, 16)

                    def body(i, slots):
                        for b, n in slots:
                            if first:
                                act.wait_ge(ld[b], 16 * (i + 1))
                            act.activation(junk[0:n, b, :], source(i, b, n), ACT.Square,
                                           accum_out=ss[0:n, b:b + 1]).then_inc(sq[b], 1)
                        for b, n in slots:
                            for half in range(2):
                                act.wait_ge(tp[b], 2 * i + half + 1)
                                act.activation(XH[:, 4 * half:4 * half + 4, tok(2 * i + b, n)],
                                               BK[2 * b + half].rearrange("p (k t) -> p k t", k=4)[:, :, 0:n],
                                               ACT.Copy).then_inc(hi[b], 1)
                    each_pair(act, body)

                @block.gpsimd
                def _(pool):
                    links = Chain(pool, pch)
                    pool.wait_ge(consts_in, 64) if first else None

                    def body(i, slots):
                        for b, n in slots:
                            pool.wait_ge(sq[b], i + 1)
                            apart(pool)
                            links.link(nc.gpsimd.tensor_scalar(var[0:n, b:b + 1], ss[0:n, b:b + 1], 1.0 / D, EPS,
                                                               ALU.mult, ALU.add))
                            nc.gpsimd.tensor_tensor(rs[0:n, b:b + 1], var[0:n, b:b + 1], neg_half[0:n, :],
                                                    ALU.pow).then_inc(rr[b], 1)
                    with pool.Fori(0, NT // 2) as i:
                        links.enter(i, 2)
                        body(i, ((0, P), (1, P)))
                    links.leave(NT // 2)
                    body(NT // 2, ((0, TS),))

                @block.vector
                def _(dve):
                    def body(i, slots):
                        for b, n in slots:
                            dve.wait_ge(rr[b], i + 1)
                            dve.wait_ge(tp[b], 2 * i)
                            nc.vector.tensor_scalar(xn[0:n, b, :], source(i, b, n), rs[0:n, b:b + 1], None,
                                                    ALU.mult).then_inc(xs[b], 1)
                        for b, n in slots:
                            for half in range(2):
                                dve.wait_ge(hi[b], 2 * i + half + 1)
                                cols = (slice(None), slice(4 * half, 4 * half + 4), tok(2 * i + b, n))
                                nc.vector.tensor_tensor(XL[cols],
                                                        BK[2 * b + half].rearrange("p (k t) -> p k t", k=4)[:, :, 0:n],
                                                        XH[cols].bitcast(F32), ALU.subtract).then_inc(lo[b], 1)
                    each_pair(dve, body)

                @block.tensor
                def _(pe):
                    pe.wait_ge(consts_in, 64) if first else None

                    def body(i, slots):
                        for b, n in slots:
                            pe.wait_ge(xs[b], i + 1)
                            pe.wait_ge(lo[b], 2 * i)
                            for k in range(KT):
                                out = BK[2 * b + k // 4].rearrange("p (k t) -> p k t", k=4)[:, k % 4, 0:n]
                                last = nc.tensor.transpose(out, xn[0:n, b, k * P:(k + 1) * P], ident[0:n, 0:n])
                                if k % 4 == 3:
                                    last.then_inc(tp[b], 1)
                    each_pair(pe, body)

        def gates_phase():
            take = area()
            gi, gf, t1, t2, bc, G = (take(TOK) for _ in range(6))
            QTT = take(TOK)
            gw = take(KT, 2 * H)
            bi, bf = take(1), take(1)
            m = take(NT + 1)
            M0 = take(DB)
            mS = take(DB)
            decE = take(2 * NT)
            onesr = take(P)
            GH = WH[:, 0:KT * 64].rearrange("p (k c) -> p k c", k=KT)
            GL = WL[:, 0:KT * 64].rearrange("p (k c) -> p k c", k=KT)
            g_ld, g_zero, g_hi, g_lo, g_mm, g_ev, g_ab, g_ln, g_arg, g_exp, g_row, g_tp, g_col, g_st, dch, g_dec, g_m = (
                sem(s) for s in ("g_ld", "g_zero", "g_hi", "g_lo", "g_mm", "g_ev", "g_ab", "g_ln", "g_arg", "g_exp",
                                 "g_row", "g_tp", "g_col", "g_st", "g_dve", "g_dec", "g_m"))
            ach = sem("g_act")
            TH = TOK // 3

            def smp(t, d):
                return t[0:H, SEQ:TOK].rearrange("h (b s) -> h b s", s=DS)[:, :, d]

            with nc.Block() as block:
                @block.sync
                def _(sp):
                    with nc.allow_non_contiguous_dma("gate columns"):
                        sp.dma_start(gw, w_in_a[0, :, 5 * D:].rearrange("(k p) c -> p k c", p=P)).then_inc(g_ld, 16)
                        sp.dma_start(bi[0:H, :], b_i_a.rearrange("a h -> h a")).then_inc(g_ld, 16)
                        sp.dma_start(bf[0:H, :], b_f_a.rearrange("a h -> h a")).then_inc(g_ld, 16)
                        sp.dma_start(M0[0:H, :], state_m[0, :, :].rearrange("b h -> h b")).then_inc(g_ld, 16)
                        sp.wait_ge(g_row, 1)
                        sp.dma_start(d_G, G[0:H, :]).then_inc(g_st, 16)
                        sp.dma_start(m_p.rearrange("a b h -> h (a b)"), m[0:H, NT:NT + 1]).then_inc(g_st, 16)
                        sp.dma_start(m_s[0, :, :].rearrange("b h -> h b"), mS[0:H, :]).then_inc(g_st, 16)
                        sp.wait_ge(g_exp, 1)
                        sp.dma_start(d_dec, decE[0:H, :]).then_inc(g_dec, 16)
                        sp.wait_ge(g_dec, 16)
                        sp.dma_start(DEC[:, :], d_dec.rearrange("h c -> (h c)").partition_broadcast(P)).then_inc(g_st, 16)
                        sp.wait_ge(g_st, 64)

                @block.scalar
                def _(act):
                    act.wait_ge(g_ld, 64)
                    act.wait_ge(g_zero, 3)
                    for k in range(KT):
                        for f in range(2):
                            last = act.activation(GH[:, k, 32 * f:32 * f + H], gw[:, k, H * f:H * f + H], ACT.Copy,
                                                  scale=gA[:, k:k + 1])
                    last.then_inc(g_hi, 1)
                    act.wait_ge(g_mm, 1)
                    for c in range(3):
                        for f, t in ((0, gi), (1, gf)):
                            last = act.activation(t[0:H, c * TH:(c + 1) * TH], BK[c][32 * f:32 * f + H, 0:TH], ACT.Copy)
                    last.then_inc(g_ev, 1)
                    act.wait_ge(g_ab, 1)
                    links = Chain(act, ach)
                    links.link(act.activation(t2[0:H, :], t1[0:H, :], ACT.Exp, scale=-1.0))
                    act.activation(bc[0:H, :], t2[0:H, :], ACT.Ln, bias=one_row[0:H, :]).then_inc(g_ln, 1)
                    act.wait_ge(g_arg, 1)
                    act.activation(decE[0:H, 0:NT], t1[0:H, P - 1:SEQ:P], ACT.Exp)
                    links.link(act.activation(decE[0:H, NT:2 * NT], smp(t1, DS - 1), ACT.Exp))
                    act.activation(QTT[32:32 + H, :], t1[0:H, :], ACT.Exp).then_inc(g_exp, 1)
                    act.activation(QTT[64:64 + H, :], t2[0:H, :], ACT.Exp, scale=-1.0).then_inc(g_exp, 1)
                    act.wait_ge(g_arg, 2)
                    act.activation(QTT[96:96 + H, :], gf[0:H, :], ACT.Exp).then_inc(g_exp, 1)

                @block.vector
                def _(dve):
                    links = Chain(dve, dch)
                    v = nc.vector
                    v.memset(GH.bitcast(F32), 0.0).then_inc(g_zero, 1)
                    v.memset(GL.bitcast(F32), 0.0).then_inc(g_zero, 1)
                    v.memset(onesr[0:H, :], 1.0)
                    v.memset(m[0:H, 0:1], 0.0)
                    v.memset(QTT, 0.0).then_inc(g_zero, 1)
                    dve.wait_ge(g_zero, 3)
                    dve.wait_ge(g_hi, 1)
                    for k in range(KT):
                        for f in range(2):
                            cols = slice(32 * f, 32 * f + H)
                            last = v.scalar_tensor_tensor(GL[:, k, cols], gw[:, k, H * f:H * f + H], gA[:, k:k + 1],
                                                          GH[:, k, cols].bitcast(F32), ALU.mult, ALU.subtract)
                    last.then_inc(g_lo, 1)
                    dve.wait_ge(g_ev, 1)
                    v.tensor_scalar(gi[0:H, :], gi[0:H, :], bi[0:H, :], None, ALU.add)
                    links.link(v.tensor_scalar(gf[0:H, :], gf[0:H, :], bf[0:H, :], None, ALU.add))
                    v.scalar_tensor_tensor(t1[0:H, :], gf[0:H, :], -1.0, gf[0:H, :], ALU.mult, ALU.max).then_inc(g_ab, 1)
                    dve.wait_ge(g_ln, 1)
                    links.link(v.scalar_tensor_tensor(t1[0:H, :], gf[0:H, :], 0.0, bc[0:H, :], ALU.min, ALU.subtract))
                    for c in range(NT):
                        cc = slice(c * P, (c + 1) * P)
                        v.tensor_tensor_scan(bc[0:H, cc], onesr[0:H, :], t1[0:H, cc], 0.0, ALU.mult, ALU.add)
                    links.link(v.tensor_copy(smp(bc, 0), smp(t1, 0)))
                    for d in range(1, DS):
                        links.link(v.tensor_tensor(smp(bc, d), smp(bc, d - 1), smp(t1, d), ALU.add))
                    links.link(v.tensor_tensor(gi[0:H, :], gi[0:H, :], bc[0:H, :], ALU.subtract))
                    v.tensor_copy(QTT[0:H, :], gi[0:H, :])
                    for c in range(NT):
                        cc = slice(c * P, (c + 1) * P)
                        last = slice((c + 1) * P - 1, (c + 1) * P)
                        links.link(v.tensor_tensor_scan(G[0:H, cc], gi[0:H, cc], gi[0:H, cc], m[0:H, c:c + 1],
                                                        ALU.max, ALU.max))
                        links.link(v.tensor_tensor(m[0:H, c + 1:c + 2], bc[0:H, last], G[0:H, last], ALU.add))
                    links.link(v.tensor_tensor(smp(G, 0), M0[0:H, :], smp(gi, 0), ALU.max))
                    for d in range(1, DS):
                        links.link(v.tensor_tensor(smp(G, d), smp(G, d - 1), smp(gi, d), ALU.max))
                    v.tensor_tensor(mS[0:H, :], smp(bc, DS - 1), smp(G, DS - 1), ALU.add).then_inc(g_row, 1)
                    for c in range(NT):
                        cc = slice(c * P, (c + 1) * P)
                        v.tensor_scalar(t1[0:H, cc], G[0:H, cc], -1.0, m[0:H, c:c + 1], ALU.mult, ALU.add)
                    for d in range(DS):
                        v.tensor_tensor(smp(t1, d), M0[0:H, :], smp(G, d), ALU.subtract)
                    v.tensor_tensor(t2[0:H, :], bc[0:H, :], G[0:H, :], ALU.add).then_inc(g_arg, 1)
                    for c in range(NT):
                        cc = slice(c * P, (c + 1) * P)
                        last = slice((c + 1) * P - 1, (c + 1) * P)
                        v.tensor_scalar(gf[0:H, cc], gi[0:H, cc], G[0:H, last], None, ALU.subtract)
                    for d in range(DS):
                        last = v.tensor_tensor(smp(gf, d), smp(gi, d), smp(G, DS - 1), ALU.subtract)
                    last.then_inc(g_arg, 1)
                    for c in range(NB):
                        n = P if c < NT else TS
                        if c % 4 == 0:
                            dve.wait_ge(g_tp, c // 4 + 1)
                        src = BK[3 + c // 4].rearrange("p (c q r) -> p c q r", c=4, q=4)[0:n, c % 4, :, 0:H]
                        last = v.tensor_copy(COL[0:n, c, :, :], src)
                    links.link(last)
                    v.tensor_scalar(COL[:, 0:NT, 3, :], COL[:, 0:NT, 3, :], K_SCALE, None, ALU.mult)
                    links.link(v.tensor_scalar(COL[0:TS, NT, 3, :], COL[0:TS, NT, 3, :], K_SCALE, None, ALU.mult))

                @block.tensor
                def _(pe):
                    pe.wait_ge(g_hi, 1)
                    pe.wait_ge(g_lo, 1)
                    for c in range(3):
                        cc = slice(c * TH, (c + 1) * TH)
                        n = 0
                        for k in range(KT):
                            for w, x in ((GH, XH), (GH, XL), (GL, XH)):
                                last = nc.tensor.matmul(BK[c][0:64, 0:TH], w[:, k, :], x[:, k, cc],
                                                        start=(n == 0), stop=(n == 3 * KT - 1))
                                n += 1
                    last.then_inc(g_mm, 1)
                    pe.wait_ge(g_exp, 3)
                    pe.wait_ge(g_arg, 2)
                    for c in range(NB):
                        n = P if c < NT else TS
                        out = BK[3 + c // 4].rearrange("p (c r) -> p c r", c=4)[0:n, c % 4, :]
                        last = nc.tensor.transpose(out, QTT[:, c * P:c * P + n], ident)
                        if c % 4 == 3 or c == NB - 1:
                            last.then_inc(g_tp, 1)

                @block.gpsimd
                def _(pool):
                    pass

        def mlstm_phase():
            take = area()
            QK = take(2, 2, P)
            QKT = take(NT, 2, P)
            KW = take(NT, P)
            GB = take(SEQ)
            DM, EX, AT = take(2, P), take(2, P), take(2, P)
            VA = take(2, P + 2)
            SG = take(2, 2, P)
            ZC, GZ = take(2, P), take(2, P)
            IS, NU = take(2, P + 2), take(2, P + 2)
            U, Y = take(2, P), take(2, P)
            dn, rd, ssq, var, rs = (take(2) for _ in range(5))
            JK = take(2, P)
            CA = take(P + 2)
            CS = take(P + 2)
            SS = take(5, P)
            HN = take(P)
            N1, N2 = 2 * P, 3 * P
            r0 = lambda w: w[:, 0:KT * N1].rearrange("p (k c) -> p k c", k=KT)
            r1 = lambda w: w[:, KT * N1:KT * (N1 + N2)].rearrange("p (k c) -> p k c", k=KT)
            a_w0, a_w1, a_g, a_hn, a_sst, a_cst = (sem(f"a_{s}") for s in ("w0", "w1", "g", "hn", "sst", "cst"))
            hi0, lo0, hi1, lo1 = (sem(f"a_{s}") for s in ("hi0", "lo0", "hi1", "lo1"))
            pj_mm, qk, voz, kw, dd, ee, s_mm, at, cell, ca, num, isc, uu, sq, rr, sg, gz, yy, ss, ct, cev = (
                sem(f"a_{s}") for s in ("pj", "qk", "voz", "kw", "dm", "ex", "s", "at", "cell", "ca", "num", "is",
                                        "u", "sq", "rs", "sg", "gz", "y", "ss", "ct", "cev"))
            pj_free, tr_mm, tr_free = two("a_pjf"), two("a_tr"), two("a_trf")
            dch, pch, ones_set = sem("a_dve"), sem("a_pool"), sem("a_ones")
            B_S, B_IN, B_X, B_C = BK[4], BK[5], BK[6], BK[7]

            def heads(eng, body, links=None, per=0):
                with eng.Fori(0, H - 1) as h:
                    if links:
                        links.enter(h, per)
                    body(h, False)
                if links:
                    links.leave(H - 1)
                body(H - 1, True)

            def w_cols(group, h):
                return w_in_a[0, :, bass.ds(group * D + h * P, P)].rearrange("(k p) c -> p k c", p=P)

            with nc.Block() as block:
                @block.sync
                def _(sp):
                    def load0(h):
                        for j in range(2):
                            sp.dma_start(r0(RAW)[:, :, j * P:(j + 1) * P], w_cols(j, h)).then_inc(a_w0, 16)

                    def load1(h):
                        for j in range(3):
                            sp.dma_start(r1(RAW)[:, :, j * P:(j + 1) * P], w_cols(2 + j, h)).then_inc(a_w1, 16)

                    load0(0)
                    load1(0)

                    def body(h, last):
                        if not last:
                            sp.wait_ge(lo0, KT * (h + 1))
                            load0(h + 1)
                        sp.wait_ge(dd, NT * h)
                        sp.dma_start(GB, d_G[bass.ds(h, 1), 0:SEQ].rearrange("a n -> (a n)").partition_broadcast(P))\
                          .then_inc(a_g, 16)
                        sp.wait_ge(gz, NT * h)
                        sp.dma_start(HN, hnorm_a[0, bass.ds(h * P, P)].partition_broadcast(P)).then_inc(a_hn, 16)
                        if not last:
                            sp.wait_ge(lo1, KT * (h + 1))
                            load1(h + 1)
                        sp.wait_ge(ss, h + 1)
                        sp.dma_start(d_smA[:, :, bass.ds(h * P, P)], SS[0:TS, :, :]).then_inc(a_sst, 16)
                        sp.wait_ge(cev, h + 1)
                        sp.dma_start(c_p[0, 0, bass.ds(h, 1), :, :].rearrange("a v k -> (a v) k"), CS[:, 0:P])\
                          .then_inc(a_cst, 16)
                        sp.dma_start(n_p[0, 0, bass.ds(h, 1), :].rearrange("a k -> k a"), CS[:, P:P + 1])\
                          .then_inc(a_cst, 16)
                    heads(sp, body)
                    sp.wait_ge(a_sst, 16 * H)
                    sp.wait_ge(a_cst, 32 * H)

                @block.scalar
                def _(act):
                    def cut0(h, k):
                        act.activation(r0(WH)[:, k, :], r0(RAW)[:, k, :], ACT.Copy, scale=gA[:, k:k + 1])\
                           .then_inc(hi0, 1)

                    act.wait_ge(a_w0, 32)
                    for k in range(KT):
                        cut0(0, k)

                    def body(h, last):
                        act.wait_ge(a_w1, 48 * (h + 1))
                        act.wait_ge(pj_mm, 2 * NB * h)
                        for t in range(NB):
                            if t < KT:
                                act.activation(r1(WH)[:, t, :], r1(RAW)[:, t, :], ACT.Copy, scale=gA[:, t:t + 1])\
                                   .then_inc(hi1, 1)
                            act.wait_ge(pj_mm, 2 * NB * h + t + 1)
                            src = BK[t % 2][:, 0:N1].rearrange("p (j c) -> p j c", j=2)
                            if t < NT:
                                act.wait_ge(tr_mm[t % 2], 8 * h + t // 2)
                                act.wait_ge(kw, NT * h + max(t - 1, 0))
                                act.activation(QK[:, t % 2, :, :], src, ACT.Copy).then_inc(qk, 1)
                            else:
                                act.wait_ge(a_sst, 16 * h)
                                act.activation(SS[0:TS, 0:2, :], src[0:TS, :, :], ACT.Copy).then_inc(qk, 1)
                            act.wait_ge(qk, NB * h + t + 1)
                            act.sem_inc(pj_free[t % 2], 1)
                        if not last:
                            act.wait_ge(a_w0, 32 * (h + 2))
                            act.wait_ge(pj_mm, 2 * NB * h + NB)
                        for t in range(NB):
                            if t < NT:
                                act.wait_ge(dd, NT * h + t + 1)
                                act.activation(EX[:, t % 2, :], DM[:, t % 2, :], ACT.Exp, scale=-1.0,
                                               bias=COL[:, t, 0, bass.ds(h, 1)]).then_inc(ee, 1)
                                if not last:
                                    cut0(h + 1, t)

                            def chunk(c):
                                act.wait_ge(cell, NT * h + c + 1)
                                act.activation(IS[:, c % 2, 0:P + 1], B_X[:, 0:P + 1], ACT.Copy,
                                               scale=COL[:, c, 1, bass.ds(h, 1)]).then_inc(isc, 1)
                                act.wait_ge(uu, NT * h + c + 1)
                                act.activation(JK[:, c % 2, :], U[:, c % 2, :], ACT.Square,
                                               accum_out=ssq[:, c % 2:c % 2 + 1]).then_inc(sq, 1)
                            if t == NT:
                                chunk(t - 1)
                            u = NB + t
                            act.wait_ge(pj_mm, 2 * NB * h + u + 1)
                            src = BK[u % 2][:, 0:N2].rearrange("p (j c) -> p j c", j=3)
                            if t < NT:
                                act.wait_ge(cell, NT * h + max(t - 1, 0))
                                act.wait_ge(yy, NT * h + max(t - 1, 0))
                                act.activation(VA[:, t % 2, 0:P], src[:, 0, :], ACT.Copy)
                                act.activation(SG[:, t % 2, :, :], src[:, 1:3, :], ACT.Tanh, scale=0.5)
                                act.activation(ZC[:, t % 2, :], src[:, 2, :], ACT.Copy).then_inc(voz, 1)
                                act.wait_ge(voz, NT * h + t + 1)
                            else:
                                act.activation(SS[0:TS, 2:5, :], src[0:TS, :, :], ACT.Copy).then_inc(ss, 1)
                                act.wait_ge(ss, h + 1)
                            act.sem_inc(pj_free[u % 2], 1)
                            if 1 <= t < NT:
                                chunk(t - 1)
                        act.wait_ge(ct, h + 1)
                        act.wait_ge(a_cst, 32 * h)
                        act.activation(CS[:, 0:P], B_X[:, 0:P], ACT.Copy)
                        act.activation(CS[:, P:P + 1], CA[:, P:P + 1], ACT.Copy).then_inc(cev, 1)
                    heads(act, body)

                @block.gpsimd
                def _(pool):
                    links = Chain(pool, pch)
                    g = nc.gpsimd
                    def body(h, last):
                        pool.wait_ge(cell, NT * h)
                        for t in range(NT):
                            pool.wait_ge(qk, NB * h + t + 1)
                            g.tensor_tensor(KW[:, t, :], QK[:, t % 2, 1, :],
                                            COL[:, t, 3, bass.ds(h, 1)].to_broadcast([P, P]), ALU.mult)\
                             .then_inc(kw, 1)
                        pool.wait_ge(a_hn, 16 * (h + 1))
                        for t in range(NB):
                            if t >= 1:
                                b = (t - 1) % 2
                                pool.wait_ge(sq, NT * h + t)
                                apart(pool)
                                links.link(g.tensor_scalar(var[:, b:b + 1], ssq[:, b:b + 1], 4.0 / P, 16 * EPS,
                                                           ALU.mult, ALU.add))
                                g.tensor_tensor(rs[:, b:b + 1], var[:, b:b + 1], neg_half, ALU.pow).then_inc(rr, 1)
                            if t < NT:
                                b = t % 2
                                pool.wait_ge(sg, NT * h + t + 1)
                                links.link(g.tensor_tensor(GZ[:, b, :], ZC[:, b, :], SG[:, b, 1, :], ALU.mult))
                                g.tensor_tensor(GZ[:, b, :], GZ[:, b, :], HN, ALU.mult)\
                                 .then_inc(gz, 1)
                    heads(pool, body, links, 16)

                @block.vector
                def _(dve):
                    v = nc.vector
                    links = Chain(dve, dch)

                    def cut0(h, k):
                        dve.wait_ge(hi0, KT * h + k + 1)
                        v.scalar_tensor_tensor(r0(WL)[:, k, :], r0(RAW)[:, k, :], gA[:, k:k + 1],
                                               r0(WH)[:, k, :].bitcast(F32), ALU.mult, ALU.subtract).then_inc(lo0, 1)

                    v.memset(VA[:, :, P:P + 1], 1.0).then_inc(ones_set, 1)
                    for k in range(KT):
                        cut0(0, k)

                    def body(h, last):
                        dve.wait_ge(cev, h)
                        v.memset(CA, 0.0).then_inc(ca, 1)
                        for t in range(NB):
                            if t < KT:
                                dve.wait_ge(hi1, KT * h + t + 1)
                                v.scalar_tensor_tensor(r1(WL)[:, t, :], r1(RAW)[:, t, :], gA[:, t:t + 1],
                                                       r1(WH)[:, t, :].bitcast(F32), ALU.mult, ALU.subtract)\
                                 .then_inc(lo1, 1)
                            if t >= 1:
                                b = (t - 1) % 2
                                dve.wait_ge(tr_mm[b], 8 * h + (t - 1) // 2 + 1)
                                v.tensor_copy(QKT[:, t - 1, :, :],
                                              BK[2 + b][:, 0:N1].rearrange("p (j c) -> p j c", j=2))\
                                 .then_inc(tr_free[b], 1)

                        def y_transposed(c):
                            dve.wait_ge(tr_mm[c % 2], 8 * h + 4 + c // 2 + 1)
                            v.tensor_copy(YT[:, bass.ds(h, 1), c * P:(c + 1) * P].rearrange("p a c -> p (a c)"),
                                          BK[2 + c % 2][:, 0:P]).then_inc(tr_free[c % 2], 1)

                        dve.wait_ge(a_g, 16 * (h + 1))
                        for t in range(NB):
                            if t < NT:
                                v.tensor_tensor(DM[:, t % 2, :], GB[:, t * P:(t + 1) * P], cst[:, C_MA:C_MA + P],
                                                ALU.add).then_inc(dd, 1)
                                dve.wait_ge(ee, NT * h + t + 1)
                                dve.wait_ge(s_mm, NT * h + t + 1)
                                v.scalar_tensor_tensor(AT[:, t % 2, :], B_S[:, 0:P], K_SCALE, EX[:, t % 2, :],
                                                       ALU.mult, ALU.mult).then_inc(at, 1)
                                if not last:
                                    cut0(h + 1, t)
                            if t >= 1:
                                c = t - 1
                                b = c % 2
                                dve.wait_ge(cell, NT * h + c + 1)
                                v.scalar_tensor_tensor(CA[:, 0:P + 1], CA[:, 0:P + 1],
                                                       DEC[:, bass.ds(h * 2 * NT + c, 1)], B_C[:, 0:P + 1],
                                                       ALU.mult, ALU.add).then_inc(ca, 1)
                                dve.wait_ge(isc, NT * h + c + 1)
                                v.tensor_tensor(NU[:, b, 0:P + 1], B_IN[:, 0:P + 1], IS[:, b, 0:P + 1], ALU.add)\
                                 .then_inc(num, 1)
                                dve.wait_ge(num, NT * h + c + 1)
                                den = NU[:, b, P:P + 1]
                                links.link(v.scalar_tensor_tensor(dn[:, b:b + 1], den, -1.0, den, ALU.mult, ALU.max))
                                links.link(v.tensor_tensor(dn[:, b:b + 1], dn[:, b:b + 1],
                                                           COL[:, c, 2, bass.ds(h, 1)], ALU.max))
                                links.link(v.reciprocal(rd[:, b:b + 1], dn[:, b:b + 1]))
                                v.scalar_tensor_tensor(U[:, b, :], NU[:, b, 0:P], rd[:, b:b + 1], SG[:, b, 0, :],
                                                       ALU.mult, ALU.mult).then_inc(uu, 1)
                            if t >= 2:
                                y_transposed(t - 2)
                            if t < NT:
                                b = t % 2
                                dve.wait_ge(voz, NT * h + t + 1)
                                v.tensor_scalar(SG[:, b, :, :], SG[:, b, :, :], 1.0, None, ALU.add).then_inc(sg, 1)
                                dve.wait_ge(sg, NT * h + t + 1)
                            if t >= 1:
                                b = (t - 1) % 2
                                dve.wait_ge(rr, NT * h + t)
                                dve.wait_ge(gz, NT * h + t)
                                v.scalar_tensor_tensor(Y[:, b, :], U[:, b, :], rs[:, b:b + 1], GZ[:, b, :],
                                                       ALU.mult, ALU.mult).then_inc(yy, 1)
                        y_transposed(NT - 1)
                    heads(dve, body, links, 24)

                @block.tensor
                def _(pe):
                    def project(reg, n, t, bank):
                        rows = P if t < NT else TS
                        tt = slice(t * P, t * P + rows)
                        i = 0
                        for k in range(KT):
                            for x, w in ((XH, WH), (XH, WL), (XL, WH)):
                                last = nc.tensor.matmul(bank[0:rows, 0:n], x[:, k, tt], reg(w)[:, k, :],
                                                        start=(i == 0), stop=(i == 3 * KT - 1))
                                i += 1
                        last.then_inc(pj_mm, 1)

                    pe.wait_ge(ones_set, 1)

                    def body(h, last):
                        pe.wait_ge(hi0, KT * (h + 1))
                        pe.wait_ge(lo0, KT * (h + 1))
                        for t in range(NB):
                            pe.wait_ge(pj_free[t % 2], NB * h + t // 2)
                            project(r0, N1, t, BK[t % 2])
                            if t >= 1:
                                b = (t - 1) % 2
                                pe.wait_ge(qk, NB * h + t)
                                pe.wait_ge(tr_free[b], 8 * h + (t - 1) // 2)
                                for j in range(2):
                                    x = nc.tensor.transpose(BK[2 + b][:, j * P:(j + 1) * P], QK[:, b, j, :], ident)
                                x.then_inc(tr_mm[b], 1)
                        pe.wait_ge(hi1, KT * (h + 1))
                        pe.wait_ge(lo1, KT * (h + 1))

                        def run_cell(c):
                            b = c % 2
                            pe.wait_ge(at, NT * h + c + 1)
                            pe.wait_ge(voz, NT * h + c + 1)
                            pe.wait_ge(num, NT * h + c)
                            nc.tensor.matmul(B_IN[:, 0:P + 1], AT[:, b, :], VA[:, b, 0:P + 1], start=True, stop=True)
                            pe.wait_ge(ca, NB * h + c + 1)
                            pe.wait_ge(isc, NT * h + c)
                            nc.tensor.matmul(B_X[:, 0:P + 1], QKT[:, c, 0, :], CA[:, 0:P + 1], start=True, stop=True)
                            pe.wait_ge(kw, NT * h + c + 1)
                            nc.tensor.matmul(B_C[:, 0:P + 1], KW[:, c, :], VA[:, b, 0:P + 1], start=True, stop=True)\
                              .then_inc(cell, 1)

                        def y_transpose(c):
                            pe.wait_ge(yy, NT * h + c + 1)
                            pe.wait_ge(tr_free[c % 2], 8 * h + 4 + c // 2)
                            nc.tensor.transpose(BK[2 + c % 2][:, 0:P], Y[:, c % 2, :], ident).then_inc(tr_mm[c % 2], 1)

                        for t in range(NB):
                            u = NB + t
                            if t < NT:
                                pe.wait_ge(tr_free[t % 2], 8 * h + t // 2 + 1)
                                pe.wait_ge(at, NT * h + t)
                                nc.tensor.matmul(B_S[:, 0:P], QKT[:, t, 1, :], QKT[:, t, 0, :], start=True, stop=True)\
                                  .then_inc(s_mm, 1)
                                pe.wait_ge(pj_free[u % 2], NB * h + u // 2)
                                project(r1, N2, t, BK[u % 2])
                                if t >= 1:
                                    run_cell(t - 1)
                                if t >= 2:
                                    y_transpose(t - 2)
                            else:
                                run_cell(t - 1)
                                y_transpose(t - 2)
                                pe.wait_ge(pj_free[u % 2], NB * h + u // 2)
                                project(r1, N2, t, BK[u % 2])
                                y_transpose(t - 1)
                        pe.wait_ge(ca, NB * h + NB)
                        pe.wait_ge(isc, NT * h + NT)
                        nc.tensor.transpose(B_X[:, 0:P], CA[:, 0:P], ident).then_inc(ct, 1)
                    heads(pe, body)

        def mlstm_sample_phase():
            take = area()
            XS = RAW[:, 2 * DB * P:2 * DB * P + 10 * P].rearrange("p (s j c) -> p s j c", s=2, j=5)
            CI = RAW[:, 0:2 * DB * P].rearrange("p (s b k) -> p s b k", s=2, b=DB)
            CN = take(2, DB, P)
            GS = take(H, TS)
            CT = take(DB, P + 2)
            nN = take(P)
            nT = take(DB, H)
            nO = take(DB, H)
            nM = take(DB)
            QT2 = take(2, TS)
            QZ = take(DB * (TS + DS))
            VW = take(DB, P)
            WG = take(DB)
            VA = take(P + 2)
            DM, EX, AT = take(TS), take(TS), take(TS)
            SG = take(2, P)
            GZ, U, Y, JK = take(P), take(P), take(P), take(P)
            IS, NU = take(P + 2), take(P + 2)
            dn, rd, ssq, var, rs = (take(1) for _ in range(5))
            HN = take(D)
            b_x, b_c, b_st, cn = two("b_x"), two("b_c"), two("b_st"), two("b_cn")
            b_k, b_n = sem("b_k"), sem("b_n")
            ini, qt, ctp, s_mm, qe, cte, ee, dd, at, wg, qz, vw, cell, upd, isc, num, uu, sq, rr, ez, sg, gz, yy, yt, yte, nev = (
                sem(f"b_{s}") for s in ("ini", "qt", "ctp", "s", "qe", "cte", "ex", "dm", "at", "wg", "qz", "vw", "cell",
                                        "upd", "is", "num", "u", "sq", "rs", "ez", "sg", "gz", "y", "yt", "yte", "nev"))
            dch, pch, n_tp = sem("b_dve"), sem("b_pool"), sem("b_ntp")

            def heads(eng, body, links=None, per=0):
                with eng.Fori(0, H // 2) as i:
                    if links:
                        links.enter(i, per)
                    for b in range(2):
                        body(i, b, i * 2 + b)
                if links:
                    links.leave(H // 2)

            with nc.Block() as block:
                @block.sync
                def _(sp):
                    sp.dma_start(GS[0:TS, :, :], d_G[:, SEQ:TOK].partition_broadcast(TS)).then_inc(b_k, 16)
                    sp.dma_start(HN, hnorm_a[0, :].partition_broadcast(P)).then_inc(b_k, 16)
                    sp.dma_start(nN[0:DB * H, :], state_n[0, :, :, :].rearrange("b h k -> (b h) k")).then_inc(b_k, 16)

                    with sp.Fori(0, H // 2) as i:
                        for b in range(2):
                            h = i * 2 + b
                            sp.wait_ge(cn[b], i)
                            apart(sp)
                            sp.wait_ge(yy, i * 2)
                            sp.dma_start(XS[0:TS, b, :, :], d_smA[:, :, bass.ds(h * P, P)]).then_inc(b_x[b], 16)
                            sp.dma_start(CI[:, b, :, :],
                                         state_C[0, :, bass.ds(h, 1), :, :].rearrange("b a v k -> v (b a) k"))\
                              .then_inc(b_c[b], 16)

                @block.scalar
                def _(act):
                    def body(i, b, h):
                        act.wait_ge(b_x[b], 16 * (i + 1))
                        act.wait_ge(yy, h)
                        act.activation(SG[0:TS, :, :], XS[0:TS, b, 3:5, :], ACT.Tanh, scale=0.5).then_inc(ez, 1)
                        act.activation(VA[0:TS, 0:P], XS[0:TS, b, 2, :], ACT.Copy)
                        act.wait_ge(qt, h + 1)
                        act.activation(QT2, BK[0][:, 0:2 * TS].rearrange("p (a t) -> p a t", a=2), ACT.Copy)\
                           .then_inc(qe, 1)
                        act.wait_ge(dd, h + 1)
                        act.activation(EX[0:TS, :], DM[0:TS, :], ACT.Exp, scale=-1.0,
                                       bias=COL[0:TS, NT, 0, bass.ds(h, 1)]).then_inc(ee, 1)
                        act.wait_ge(ctp, h + 1)
                        for g in range(2):
                            last = act.activation(CT[:, 4 * g:4 * g + 4, 0:P],
                                                  BK[1 + g].rearrange("p (b v) -> p b v", b=4), ACT.Copy)
                        last.then_inc(cte, 1)
                        act.wait_ge(cell, h + 1)
                        act.activation(IS[0:TS, 0:P + 1], BK[5][0:TS, 0:P + 1], ACT.Copy,
                                       scale=COL[0:TS, NT, 1, bass.ds(h, 1)]).then_inc(isc, 1)
                        act.wait_ge(uu, h + 1)
                        act.activation(JK[0:TS, :], U[0:TS, :], ACT.Square, accum_out=ssq[0:TS, :]).then_inc(sq, 1)
                    heads(act, body)

                @block.gpsimd
                def _(pool):
                    g = nc.gpsimd
                    links = Chain(pool, pch)
                    pool.wait_ge(b_k, 48)

                    def body(i, b, h):
                        pool.wait_ge(sg, h + 1)
                        links.link(g.tensor_tensor(GZ[0:TS, :], XS[0:TS, b, 4, :], SG[0:TS, 1, :], ALU.mult))
                        g.tensor_tensor(GZ[0:TS, :], GZ[0:TS, :], HN[0:TS, bass.ds(h * P, P)], ALU.mult).then_inc(gz, 1)
                        pool.wait_ge(sq, h + 1)
                        apart(pool)
                        links.link(g.tensor_scalar(var[0:TS, :], ssq[0:TS, :], 4.0 / P, 16 * EPS, ALU.mult, ALU.add))
                        g.tensor_tensor(rs[0:TS, :], var[0:TS, :], neg_half[0:TS, :], ALU.pow).then_inc(rr, 1)
                        pool.wait_ge(cn[b], i + 1)
                        pool.dma_start(c_s[0, :, bass.ds(h, 1), :, :].rearrange("b a v k -> v (b a) k"), CN[:, b, :, :])\
                            .then_inc(b_st[b], 16)
                    heads(pool, body, links, 4)
                    pool.wait_ge(nev, 1)
                    pool.dma_start(n_s[0, :, :, :].rearrange("b h k -> (b h) k"), nN[0:DB * H, :]).then_inc(b_n, 16)
                    for b in range(2):
                        pool.wait_ge(b_st[b], 16 * (H // 2))
                    pool.wait_ge(b_n, 16)

                @block.vector
                def _(dve):
                    v = nc.vector
                    links = Chain(dve, dch)
                    v.memset(QZ, 0.0).then_inc(ini, 1)
                    v.memset(VA[:, P:P + 1], 1.0).then_inc(ini, 1)
                    dve.wait_ge(ini, 2)
                    dve.wait_ge(n_tp, 1)
                    links.link(v.tensor_copy(nT, BK[0][:, 0:DB * H].rearrange("p (b h) -> p b h", b=DB)))
                    dve.wait_ge(b_k, 48)

                    def body(i, b, h):
                        hh = bass.ds(h, 1)
                        v.tensor_tensor(DM[0:TS, :], GS[0:TS, hh, :].rearrange("p a t -> p (a t)"),
                                        cst[0:TS, C_MS:C_MS + TS], ALU.add).then_inc(dd, 1)
                        dve.wait_ge(upd, h)
                        v.tensor_tensor(WG[0:TS, :], cst[0:TS, C_ONE:C_ONE + DB],
                                        COL[0:TS, NT, 3, hh].to_broadcast([TS, DB]), ALU.mult).then_inc(wg, 1)
                        dve.wait_ge(wg, h + 1)
                        dve.wait_ge(b_x[b], 16 * (i + 1))
                        v.tensor_tensor(VW[0:TS, :, :],
                                        XS[0:TS, b, 2, :].unsqueeze(1).to_broadcast([TS, DB, P]),
                                        WG[0:TS, :].unsqueeze(2).to_broadcast([TS, DB, P]), ALU.mult).then_inc(vw, 1)
                        dve.wait_ge(qe, h + 1)
                        v.tensor_copy(QZ.rearrange("p (b s) -> p b s", s=TS + DS)[:, :, 0:DS],
                                      QT2[:, 0, :].rearrange("p (b s) -> p b s", s=DS))
                        v.tensor_copy(CT[:, :, P:P + 1].rearrange("p b a -> p (b a)"),
                                      nT[:, :, hh].rearrange("p b a -> p (b a)")).then_inc(qz, 1)
                        dve.wait_ge(ee, h + 1)
                        dve.wait_ge(s_mm, h + 1)
                        v.scalar_tensor_tensor(AT[0:TS, :], BK[3][0:TS, 0:TS], K_SCALE, EX[0:TS, :],
                                               ALU.mult, ALU.mult).then_inc(at, 1)
                        dve.wait_ge(ez, h + 1)
                        v.tensor_scalar(SG[0:TS, :, :], SG[0:TS, :, :], 1.0, None, ALU.add).then_inc(sg, 1)
                        dve.wait_ge(sg, h + 1)
                        dec = DEC[:, bass.ds(h * 2 * NT + NT, DB)]
                        links.link(v.tensor_tensor(nM, nT[:, :, hh].rearrange("p b a -> p (b a)"), dec, ALU.mult))
                        v.tensor_tensor(nO[:, :, hh].rearrange("p b a -> p (b a)"), nM, BK[3][:, 64:64 + DB], ALU.add)
                        dve.wait_ge(cell, h + 1)
                        dve.wait_ge(isc, h + 1)
                        links.link(v.tensor_tensor(NU[0:TS, 0:P + 1], BK[4][0:TS, 0:P + 1], IS[0:TS, 0:P + 1], ALU.add))
                        den = NU[0:TS, P:P + 1]
                        links.link(v.scalar_tensor_tensor(dn[0:TS, :], den, -1.0, den, ALU.mult, ALU.max))
                        links.link(v.tensor_tensor(dn[0:TS, :], dn[0:TS, :], COL[0:TS, NT, 2, hh], ALU.max))
                        links.link(v.reciprocal(rd[0:TS, :], dn[0:TS, :]))
                        v.scalar_tensor_tensor(U[0:TS, :], NU[0:TS, 0:P], rd[0:TS, :], SG[0:TS, 0, :],
                                               ALU.mult, ALU.mult).then_inc(uu, 1)
                        dve.wait_ge(upd, h + 1)
                        dve.wait_ge(b_st[b], 16 * i)
                        for s in range(DB):
                            last = v.scalar_tensor_tensor(CN[:, b, s, :], CI[:, b, s, :],
                                                          DEC[:, bass.ds(h * 2 * NT + NT + s, 1)],
                                                          BK[6 + s // 4].rearrange("p (b k) -> p b k", b=4)[:, s % 4, :],
                                                          ALU.mult, ALU.add)
                        last.then_inc(cn[b], 1)
                        dve.wait_ge(rr, h + 1)
                        dve.wait_ge(gz, h + 1)
                        v.scalar_tensor_tensor(Y[0:TS, :], U[0:TS, :], rs[0:TS, :], GZ[0:TS, :],
                                               ALU.mult, ALU.mult).then_inc(yy, 1)
                        dve.wait_ge(yt, h + 1)
                        v.tensor_copy(YT[:, hh, SEQ:TOK].rearrange("p a t -> p (a t)"), BK[0][:, 0:TS])\
                         .then_inc(yte, 1)
                    heads(dve, body, links, 10)
                    dve.wait_ge(n_tp, 2)
                    v.tensor_copy(nN[0:DB * H, :], BK[1][0:DB * H, 0:P]).then_inc(nev, 1)

                @block.tensor
                def _(pe):
                    pe.wait_ge(b_k, 48)
                    nc.tensor.transpose(BK[0][:, 0:DB * H], nN[0:DB * H, :], ident[0:DB * H, 0:DB * H]).then_inc(n_tp, 1)
                    pe.wait_ge(dch, 1)

                    def body(i, b, h):
                        pe.wait_ge(b_x[b], 16 * (i + 1))
                        pe.wait_ge(yte, h)
                        apart(pe)
                        for j in range(2):
                            last = nc.tensor.transpose(BK[0][:, j * TS:(j + 1) * TS], XS[0:TS, b, j, :],
                                                       ident[0:TS, 0:TS])
                        last.then_inc(qt, 1)
                        pe.wait_ge(b_c[b], 16 * (i + 1))
                        for s in range(DB):
                            out = BK[1 + s // 4].rearrange("p (b v) -> p b v", b=4)[:, s % 4, :]
                            last = nc.tensor.transpose(out, CI[:, b, s, :], ident)
                        last.then_inc(ctp, 1)
                        pe.wait_ge(qe, h + 1)
                        pe.wait_ge(wg, h + 1)
                        nc.tensor.matmul(BK[3][0:TS, 0:TS], QT2[:, 1, :], QT2[:, 0, :], start=True, stop=True)
                        nc.tensor.matmul(BK[3][:, 64:64 + DB], XS[0:TS, b, 1, :], WG[0:TS, :], start=True, stop=True)\
                          .then_inc(s_mm, 1)
                        pe.wait_ge(vw, h + 1)
                        pe.wait_ge(cn[1 - b], i + b)
                        for s in range(DB):
                            out = BK[6 + s // 4].rearrange("p (b k) -> p b k", b=4)[:, s % 4, :]
                            last = nc.tensor.matmul(out, VW[0:TS, s, :], XS[0:TS, b, 1, :], start=True, stop=True)
                        last.then_inc(upd, 1)
                        pe.wait_ge(at, h + 1)
                        apart(pe)
                        nc.tensor.matmul(BK[4][0:TS, 0:P + 1], AT[0:TS, :], VA[0:TS, 0:P + 1], start=True, stop=True)
                        pe.wait_ge(cte, h + 1)
                        pe.wait_ge(qz, h + 1)
                        for s in range(DB):
                            last = nc.tensor.matmul(BK[5][0:TS, 0:P + 1], QZ[:, s * TS:(s + 1) * TS], CT[:, s, 0:P + 1],
                                                    start=(s == 0), stop=(s == DB - 1))
                        last.then_inc(cell, 1)
                        pe.wait_ge(yy, h + 1)
                        apart(pe)
                        nc.tensor.transpose(BK[0][:, 0:TS], Y[0:TS, :], ident[0:TS, 0:TS]).then_inc(yt, 1)
                    heads(pe, body)
                    pe.wait_ge(yte, H)
                    nc.tensor.transpose(BK[1][0:DB * H, 0:P], nO.rearrange("p b h -> p (b h)"), ident).then_inc(n_tp, 1)

        def out_phase(tag, w_out, first):
            take = area()
            N = 2 * P
            XR = take(2 * NB, N)
            reg = lambda w, r: w[:, r * KT * N:(r + 1) * KT * N].rearrange("p (k c) -> p k c", k=KT)
            flat = lambda w, r: w[:, r * KT * N:(r + 1) * KT * N]
            w_ld, x_ld, hi, lo, used, done, mm, ev = (two(f"{tag}_{s}") for s in
                                                      ("w", "x", "hi", "lo", "used", "done", "mm", "ev"))
            y_hi, y_lo = sem(f"{tag}_yhi"), sem(f"{tag}_ylo")

            with nc.Block() as block:
                @block.sync
                def _(sp):
                    with sp.Fori(0, 2) as i:
                        for r in range(2):
                            cols = bass.ds((i * 2 + r) * N, N)
                            sp.wait_ge(lo[r], i)
                            sp.dma_start(reg(RAW, r), w_out[0, :, cols].rearrange("(k p) c -> p k c", p=P))\
                              .then_inc(w_ld[r], 16)
                            sp.wait_ge(done[r], NB * i)
                            if first:
                                sp.dma_start(XR[:, r * NB:r * NB + NT, :],
                                             x_prompt[0, :, cols].rearrange("(t p) c -> p t c", p=P)).then_inc(x_ld[r], 16)
                                sp.dma_start(XR[0:TS, r * NB + NT, :],
                                             x_sample[:, :, cols].rearrange("b s c -> (b s) c")).then_inc(x_ld[r], 16)
                            else:
                                sp.dma_start(XR[:, r * NB:r * NB + NT, :],
                                             d_x1[0:SEQ, cols].rearrange("(t p) c -> p t c", p=P)).then_inc(x_ld[r], 16)
                                sp.dma_start(XR[0:TS, r * NB + NT, :], d_x1[SEQ:TOK, cols]).then_inc(x_ld[r], 16)

                @block.scalar
                def _(act):
                    for k in range(KT):
                        act.activation(XH[:, k, :], YT[:, k, :], ACT.Copy).then_inc(y_hi, 1)
                    with act.Fori(0, 2) as i:
                        for r in range(2):
                            act.wait_ge(w_ld[r], 16 * (i + 1))
                            act.wait_ge(used[r], i)
                            act.activation(flat(WH, r), flat(RAW, r), ACT.Copy).then_inc(hi[r], 1)

                @block.vector
                def _(dve):
                    v = nc.vector
                    for k in range(KT):
                        dve.wait_ge(y_hi, k + 1)
                        v.tensor_tensor(XL[:, k, :], YT[:, k, :], XH[:, k, :].bitcast(F32), ALU.subtract).then_inc(y_lo, 1)
                    dve.wait_ge(y_lo, KT)

                    def cut(i, r):
                        dve.wait_ge(hi[r], i + 1)
                        v.tensor_tensor(flat(WL, r), flat(RAW, r), flat(WH, r).bitcast(F32), ALU.subtract)\
                         .then_inc(lo[r], 1)

                    def chunk(i, r):
                        dve.wait_ge(x_ld[r], 32 * (i + 1))
                        for t in range(NB):
                            u = NB * r + t
                            n = P if t < NT else TS
                            dve.wait_ge(mm[u % 2], NB * i + u // 2 + 1)
                            v.tensor_tensor(X1[0:n, t, bass.ds((i * 2 + r) * N, N)], BK[u % 2][0:n, 0:N],
                                            XR[0:n, r * NB + t, :], ALU.add).then_inc(done[r], 1)
                            dve.wait_ge(done[r], NB * i + t + 1)
                            dve.sem_inc(ev[u % 2], 1)
                    cut(0, 0)
                    cut(0, 1)
                    chunk(0, 0)
                    cut(1, 0)
                    chunk(0, 1)
                    cut(1, 1)
                    chunk(1, 0)
                    chunk(1, 1)

                @block.tensor
                def _(pe):
                    pe.wait_ge(y_lo, KT)
                    with pe.Fori(0, 2) as i:
                        for r in range(2):
                            pe.wait_ge(hi[r], i + 1)
                            pe.wait_ge(lo[r], i + 1)
                            for t in range(NB):
                                u = NB * r + t
                                rows = P if t < NT else TS
                                tt = slice(t * P, t * P + rows)
                                pe.wait_ge(ev[u % 2], NB * i + u // 2)
                                n = 0
                                for k in range(KT):
                                    for x, w in ((XH, WH), (XH, WL), (XL, WH)):
                                        last = nc.tensor.matmul(BK[u % 2][0:rows, 0:N], x[:, k, tt], reg(w, r)[:, k, :],
                                                                start=(n == 0), stop=(n == 3 * KT - 1))
                                        n += 1
                                last.then_inc(mm[u % 2], 1)
                            pe.wait_ge(mm[(NB * r + NB - 1) % 2], NB * i + (NB * r + NB - 1) // 2 + 1)
                            pe.sem_inc(used[r], 1)

                @block.gpsimd
                def _(pool):
                    pass

        def attention_phase():
            take = area(AREA - 2 * SEQ)
            QKR = take(2, 2, P)
            RA, RB = take(8, HALF), take(8, HALF)
            V = take(NT, P)
            PR = take(2, SEQ)
            WT = take(NT, P)
            EZ, ZC, GZ = take(2, P), take(2, P), take(2, P)
            Y, JK = take(2, P), take(2, P)
            SM = take(4, P)
            SL = take(P)
            LQ = take(4, DK)
            le, nl = take(2), LAM[:, :]
            mx, nm, sm, rc, ssq, var, rs, rr2 = (take(2) for _ in range(8))
            cf = take(1)
            KR = RAW[:, 4 * KT * P:5 * KT * P].rearrange("p (t c) -> p t c", t=NT)
            QTR = phase_tensor("QTR", [P, 2, SEQ], F32R)
            QTH, QTL = QTR[:, 0, :], QTR[:, 1, :]
            KTH = WH[:, 4 * KT * P:5 * KT * P]
            KTL = WL[:, 4 * KT * P:5 * KT * P]
            N = 2 * P
            reg = lambda w, r: w[:, r * KT * N:(r + 1) * KT * N].rearrange("p (k c) -> p k c", k=KT)
            c_k, c_w, c_sst, c_kst, c_vst = sem("c_k"), two("c_w"), sem("c_sst"), sem("c_kst"), sem("c_vst")
            hi, lo = two("c_hi"), two("c_lo")
            lamS, lamE, lamD = sem("c_lam"), sem("c_lame"), sem("c_lamd")
            pj, rope, kr, kth, vz, sc, mxs, ex, ww, av, ot, otf, sq, rr, sg, gz, yy, smd = (
                sem(f"c_{s}") for s in ("pj", "rope", "kr", "kth", "vz", "sc", "mx", "ex", "w", "av",
                                        "ot", "otf", "sq", "rr", "sg", "gz", "y", "sm"))
            tr, trf, wt, wte = two("c_tr"), two("c_trf"), two("c_wt"), two("c_wte")
            dch, pch = sem("c_dve"), sem("c_pool")
            B_V, B_O = BK[0], BK[1]
            S = [PD[c][:, :, :].rearrange("p a n -> p (a n)") for c in range(2)]
            PARTS = [[(w_in_b[0, :, :], 0, gB), (w_kv, 0, gKV)], [(w_kv, D, gKV), (w_in_b[0, :, :], D, gB)]]

            def heads(eng, sweep1, sweep2, tail, links=None, per=0):
                sweep1(0, None)
                with eng.Fori(0, H - 1) as h:
                    if links:
                        links.enter(h, per)
                    sweep2(h, False)
                    sweep1(h + 1, h)
                if links:
                    links.leave(H - 1)
                sweep2(H - 1, True)
                tail(H - 1)

            with nc.Block() as block:
                @block.sync
                def _(sp):
                    def load(r, h):
                        for j, (w, base, _) in enumerate(PARTS[r]):
                            sp.dma_start(reg(RAW, r)[:, :, j * P:(j + 1) * P],
                                         w[:, bass.ds(base + h * P, P)].rearrange("(k p) c -> p k c", p=P))\
                              .then_inc(c_w[r], 16)

                    load(0, 0)
                    load(1, 0)
                    for j, w in enumerate((lam_q1, lam_k1, lam_q2, lam_k2)):
                        sp.dma_start(LQ[:, j, :], w[0, :].partition_broadcast(P)).then_inc(c_k, 16)
                    sp.dma_start(SL, subln_b[0, :].partition_broadcast(P)).then_inc(c_k, 16)

                    def body(h, last):
                        if not last:
                            sp.wait_ge(lo[0], 2 * KT * (h + 1))
                            load(0, h + 1)
                        sp.wait_ge(kr, NT * (h + 1))
                        sp.dma_start(k_p[0, :, bass.ds(h, 1), :, :].rearrange("(t p) a c d -> p t (a c d)", p=P), KR)\
                          .then_inc(c_kst, 16)
                        if not last:
                            sp.wait_ge(lo[1], 2 * KT * (h + 1))
                            load(1, h + 1)
                        sp.wait_ge(vz, NT * (h + 1))
                        sp.dma_start(v_p[0, :, bass.ds(h, 1), :].rearrange("(t p) a e -> p t (a e)", p=P), V)\
                          .then_inc(c_vst, 16)
                        sp.wait_ge(smd, h + 1)
                        sp.dma_start(d_smB[:, :, bass.ds(h * P, P)], SM[0:TS, :, :]).then_inc(c_sst, 16)
                        sp.dma_start(k_s[:, :, bass.ds(h, 1), :, :].rearrange("b s a c d -> (b s) (a c d)"), SM[0:TS, 1, :])\
                          .then_inc(c_sst, 16)
                        sp.dma_start(v_s[:, :, bass.ds(h, 1), :].rearrange("b s a e -> (b s) (a e)"), SM[0:TS, 2, :])\
                          .then_inc(c_sst, 16)
                    with sp.Fori(0, H - 1) as h:
                        body(h, False)
                    body(H - 1, True)
                    sp.wait_ge(c_kst, 16 * H)
                    sp.wait_ge(c_vst, 16 * H)
                    sp.wait_ge(c_sst, 48 * H)

                @block.scalar
                def _(act):
                    def cut(r, k):
                        for j, (_, _, g) in enumerate(PARTS[r]):
                            cols = slice(j * P, (j + 1) * P)
                            act.activation(reg(WH, r)[:, k, cols], reg(RAW, r)[:, k, cols], ACT.Copy,
                                           scale=g[:, k:k + 1]).then_inc(hi[r], 1)

                    act.wait_ge(c_w[0], 32)
                    for k in range(KT):
                        cut(0, k)
                    act.wait_ge(lamS, 1)
                    act.activation(le, mx, ACT.Exp).then_inc(lamE, 1)

                    def values(h, t):
                        act.wait_ge(pj, 2 * NB * h + NB + t + 1)
                        if t < NT:
                            if t == 0:
                                act.wait_ge(c_vst, 16 * h)
                            act.wait_ge(gz, NT * h + max(t - 1, 0))
                            act.activation(V[:, t, :], B_V[:, 0:P], ACT.Copy)
                            act.activation(EZ[:, t % 2, :], B_V[:, P:2 * P], ACT.Tanh, scale=0.5)
                            act.activation(ZC[:, t % 2, :], B_V[:, P:2 * P], ACT.Copy).then_inc(vz, 1)
                        else:
                            act.activation(SM[0:TS, 2:4, :], B_V[0:TS, 0:2 * P].rearrange("p (a c) -> p a c", a=2),
                                           ACT.Copy).then_inc(smd, 1)

                    def squares(h, c):
                        act.wait_ge(av, NT * h + c + 1)
                        act.activation(JK[:, c % 2, :], B_O[:, 0:P], ACT.Square, scale=rc[:, c % 2:c % 2 + 1],
                                       accum_out=ssq[:, c % 2:c % 2 + 1]).then_inc(sq, 1)

                    def weights(h, c):
                        n = min(c + 1, 4)
                        act.wait_ge(wt[0], NT * h + c + 1)
                        act.activation(WT[:, 0:n, :], BK[2][:, 0:n * P].rearrange("p (a c) -> p a c", a=n),
                                       ACT.Copy).then_inc(wte[0], 1)

                    def sweep1(h, before):
                        act.wait_ge(c_w[1], 32 * (h + 1))
                        act.wait_ge(pj, 2 * NB * h)
                        for t in range(NB):
                            if t < KT:
                                cut(1, t)
                            if t == 0 and before is not None:
                                squares(before, NT - 1)
                            if t >= 1:
                                c = t - 1
                                act.wait_ge(tr[c % 2], 4 * h + c // 2 + 1)
                                act.activation(QTH[:, c * P:(c + 1) * P], BK[2 + c % 2][:, 0:P], ACT.Copy)
                                act.activation(KTH[:, c * P:(c + 1) * P], BK[2 + c % 2][:, P:2 * P], ACT.Copy)\
                                   .then_inc(kth, 1)

                    def sweep2(h, last):
                        if not last:
                            act.wait_ge(c_w[0], 32 * (h + 2))
                        values(h, 0)
                        for t in range(NB):
                            if t >= 1:
                                weights(h, t - 1)
                            if t < NT:
                                if t > 4:
                                    act.wait_ge(wt[1], 4 * h + (t - 4))
                                for c in range(2):
                                    act.wait_ge(mxs, 2 * (NT * h + t) + c + 1)
                                    act.wait_ge(ww, NT * h + t)
                                    act.activation(PR[:, c, 0:(t + 1) * P], S[c][:, 0:(t + 1) * P], ACT.Exp,
                                                   scale=ATTN_SCALE, bias=nm[:, c:c + 1],
                                                   accum_out=sm[:, c:c + 1]).then_inc(ex, 1)
                                if not last:
                                    cut(0, t)
                            if t >= 1:
                                values(h, t)
                            if 1 <= t < NT:
                                squares(h, t - 1)
                    heads(act, sweep1, sweep2, lambda h: squares(h, NT - 1))

                @block.gpsimd
                def _(pool):
                    g = nc.gpsimd
                    links = Chain(pool, pch)
                    pool.wait_ge(lamD, 1)

                    def root(h, c):
                        b = c % 2
                        pool.wait_ge(sq, NT * h + c + 1)
                        apart(pool)
                        links.link(g.tensor_scalar(var[:, b:b + 1], ssq[:, b:b + 1], 1.0 / P, EPS, ALU.mult, ALU.add))
                        links.link(g.tensor_tensor(rs[:, b:b + 1], var[:, b:b + 1], neg_half, ALU.pow))
                        g.tensor_tensor(rr2[:, b:b + 1], rs[:, b:b + 1], rc[:, b:b + 1], ALU.mult).then_inc(rr, 1)

                    def sweep1(h, before):
                        if before is not None:
                            root(before, NT - 1)
                        pool.wait_ge(c_kst, 16 * h)
                        for t in range(NT):
                            pool.wait_ge(rope, NB * h + t + 1)
                            apart(pool)
                            g.tensor_copy(KR[:, t, :], QKR[:, t % 2, 1, :]).then_inc(kr, 1)

                    def sweep2(h, last):
                        for t in range(NB):
                            if 1 <= t < NT:
                                b = (t - 1) % 2
                                pool.wait_ge(sg, NT * h + t)
                                links.link(g.tensor_tensor(GZ[:, b, :], ZC[:, b, :], EZ[:, b, :], ALU.mult))
                                g.tensor_tensor(GZ[:, b, :], GZ[:, b, :], SL, ALU.mult).then_inc(gz, 1)
                                root(h, t - 1)
                        pool.wait_ge(sg, NT * h + NT)
                        b = (NT - 1) % 2
                        links.link(g.tensor_tensor(GZ[:, b, :], ZC[:, b, :], EZ[:, b, :], ALU.mult))
                        g.tensor_tensor(GZ[:, b, :], GZ[:, b, :], SL, ALU.mult).then_inc(gz, 1)
                    heads(pool, sweep1, sweep2, lambda h: root(h, NT - 1), links, 24)

                @block.vector
                def _(dve):
                    v = nc.vector
                    links = Chain(dve, dch)

                    def cut(r, k, h):
                        for j, (_, _, g) in enumerate(PARTS[r]):
                            cols = slice(j * P, (j + 1) * P)
                            dve.wait_ge(hi[r], 2 * (KT * h + k) + j + 1)
                            v.scalar_tensor_tensor(reg(WL, r)[:, k, cols], reg(RAW, r)[:, k, cols], g[:, k:k + 1],
                                                   reg(WH, r)[:, k, cols].bitcast(F32), ALU.mult, ALU.subtract)\
                             .then_inc(lo[r], 1)

                    for k in range(KT):
                        cut(0, k, 0)
                    dve.wait_ge(c_k, 80)
                    v.tensor_scalar(SL, SL, 0.5 * (1.0 - LAM_INIT), None, ALU.mult)
                    v.tensor_tensor(LQ[:, 0, :], LQ[:, 0, :], LQ[:, 1, :], ALU.mult)
                    links.link(v.tensor_tensor(LQ[:, 2, :], LQ[:, 2, :], LQ[:, 3, :], ALU.mult))
                    v.tensor_reduce(mx[:, 0:1], LQ[:, 0, :], AX, ALU.add)
                    v.tensor_reduce(mx[:, 1:2], LQ[:, 2, :], AX, ALU.add).then_inc(lamS, 1)
                    dve.wait_ge(lamE, 1)
                    links.link(v.tensor_tensor(nl, le[:, 1:2], le[:, 0:1], ALU.subtract))
                    v.tensor_scalar(nl, nl, LAM_INIT, None, ALU.subtract).then_inc(lamD, 1)
                    dve.wait_ge(lamD, 1)

                    def rotate(h, t):
                        n = P if t < NT else TS
                        dve.wait_ge(pj, 2 * NB * h + t + 1)
                        src = BK[4 + t % 2][0:n, 0:N].rearrange("p (g c) -> p g c", c=HALF)
                        cos = cst[0:n, C_COS + t * HALF:C_COS + (t + 1) * HALF]
                        sin = cst[0:n, C_SIN + t * HALF:C_SIN + (t + 1) * HALF].unsqueeze(1).to_broadcast([n, 4, HALF])
                        v.tensor_tensor(RA[0:n, :, :], src, cos.unsqueeze(1).to_broadcast([n, 8, HALF]), ALU.mult)
                        v.tensor_tensor(RB[0:n, 0:8:2, :], src[:, 1:8:2, :], sin, ALU.mult)
                        links.link(v.tensor_tensor(RB[0:n, 1:8:2, :], src[:, 0:8:2, :], sin, ALU.mult))
                        if t < NT:
                            dve.wait_ge(tr[t % 2], 4 * h + t // 2)
                            dve.wait_ge(kr, NT * h + max(t - 1, 0))
                            dst = QKR[:, t % 2, :, :]
                        else:
                            dve.wait_ge(c_sst, 48 * h)
                            dst = SM[0:n, 0:2, :]
                        dst = dst.rearrange("p a (g c) -> p (a g) c", c=HALF)
                        v.tensor_tensor(dst[:, 0:8:2, :], RA[0:n, 0:8:2, :], RB[0:n, 0:8:2, :], ALU.subtract)
                        v.tensor_tensor(dst[:, 1:8:2, :], RA[0:n, 1:8:2, :], RB[0:n, 1:8:2, :], ALU.add)\
                         .then_inc(rope, 1)
                        dve.wait_ge(rope, NB * h + t + 1)

                    def o_transposed(h, c):
                        dve.wait_ge(ot, NT * h + c + 1)
                        v.tensor_copy(YT[:, bass.ds(h, 1), c * P:(c + 1) * P].rearrange("p a c -> p (a c)"),
                                      B_O[:, P:2 * P]).then_inc(otf, 1)

                    def output(h, c):
                        b = c % 2
                        dve.wait_ge(rr, NT * h + c + 1)
                        dve.wait_ge(gz, NT * h + c + 1)
                        v.scalar_tensor_tensor(Y[:, b, :], B_O[:, 0:P], rr2[:, b:b + 1], GZ[:, b, :],
                                               ALU.mult, ALU.mult).then_inc(yy, 1)

                    def sweep1(h, before):
                        for t in range(NB):
                            rotate(h, t)
                            if t < KT:
                                cut(1, t, h)
                            if before is not None:
                                if t == 0:
                                    output(before, NT - 1)
                                    o_transposed(before, NT - 2)
                                if t == 1:
                                    o_transposed(before, NT - 1)
                            if t >= 1:
                                c = t - 1
                                dve.wait_ge(kth, NT * h + c + 1)
                                tt = slice(c * P, (c + 1) * P)
                                v.tensor_tensor(QTL[:, tt], BK[2 + c % 2][:, 0:P], QTH[:, tt].bitcast(F32), ALU.subtract)
                                v.tensor_tensor(KTL[:, tt], BK[2 + c % 2][:, P:2 * P], KTH[:, tt].bitcast(F32),
                                                ALU.subtract).then_inc(trf[c % 2], 1)

                    def sigmoid(h, t):
                        b = t % 2
                        dve.wait_ge(vz, NT * h + t + 1)
                        v.tensor_scalar(EZ[:, b, :], EZ[:, b, :], 1.0, None, ALU.add).then_inc(sg, 1)

                    def sweep2(h, last):
                        for t in range(NB):
                            n = (t + 1) * P
                            if t > 4:
                                m = t - 4
                                dve.wait_ge(wt[1], 4 * h + m)
                                v.tensor_copy(WT[:, 4:4 + m, :], BK[3][:, 0:m * P].rearrange("p (a c) -> p a c", a=m))\
                                 .then_inc(wte[1], 1)
                            if t < NT:
                                for c in range(2):
                                    if c == 1 and t >= 2:
                                        output(h, t - 2)
                                    dve.wait_ge(sc, 2 * (NT * h + t) + c + 1)
                                    links.link(v.tensor_tensor(S[c][:, n - P:n], S[c][:, n - P:n],
                                                               cst[:, C_MB:C_MB + P], ALU.add))
                                    links.link(v.tensor_reduce(mx[:, c:c + 1], S[c][:, 0:n], AX, ALU.max, negate=True))
                                    v.tensor_scalar(nm[:, c:c + 1], mx[:, c:c + 1], ATTN_SCALE, None, ALU.mult)\
                                     .then_inc(mxs, 1)
                            if t == NT:
                                output(h, t - 2)
                            if t >= 3:
                                o_transposed(h, t - 3)
                            if t >= 1:
                                sigmoid(h, t - 1)
                            if t < NT:
                                if not last:
                                    cut(0, t, h + 1)
                                b = t % 2
                                dve.wait_ge(ex, 2 * (NT * h + t) + 2)
                                links.link(v.reciprocal(cf, sm[:, 1:2]))
                                links.link(v.scalar_tensor_tensor(cf, sm[:, 0:1], nl, cf, ALU.mult, ALU.mult))
                                v.reciprocal(rc[:, b:b + 1], sm[:, 0:1])
                                v.scalar_tensor_tensor(PR[:, 0, 0:n], PR[:, 1, 0:n], cf, PR[:, 0, 0:n],
                                                       ALU.mult, ALU.add).then_inc(ww, 1)
                                dve.wait_ge(ww, NT * h + t + 1)

                    def tail(h):
                        output(h, NT - 1)
                        o_transposed(h, NT - 2)
                        o_transposed(h, NT - 1)
                    heads(dve, sweep1, sweep2, tail, links, 9 + 8 * 2 * 2 + 16)

                @block.tensor
                def _(pe):
                    def project(r, t, bank):
                        rows = P if t < NT else TS
                        tt = slice(t * P, t * P + rows)
                        i = 0
                        for k in range(KT):
                            for x, w in ((XH, WH), (XH, WL), (XL, WH)):
                                last = nc.tensor.matmul(bank[0:rows, 0:N], x[:, k, tt], reg(w, r)[:, k, :],
                                                        start=(i == 0), stop=(i == 3 * KT - 1))
                                i += 1
                        last.then_inc(pj, 1)

                    def scores(h, t):
                        width = (t // 2 + 1) * 2 * P
                        for c in range(2):
                            pe.wait_ge(ex, 2 * NT * h + max(2 * t - 1 + c, 0))
                            rows = slice(DK * c, DK * c + DK)
                            for at in range(0, width, 512):
                                kk = slice(at, min(at + 512, width))
                                i = 0
                                for q, k in ((QTH, KTH), (QTH, KTL), (QTL, KTH)):
                                    x = nc.tensor.matmul(S[c][:, kk], q[rows, t * P:(t + 1) * P], k[rows, kk],
                                                         start=(i == 0), stop=(i == 2))
                                    i += 1
                            x.then_inc(sc, 1)

                    def turn_weights(h, c):
                        pe.wait_ge(ww, NT * h + c + 1)
                        for g in range(c // 4 + 1):
                            pe.wait_ge(wte[g], NT * h + c) if g == 0 else pe.wait_ge(wte[1], 4 * h + (c - 4))
                            for kb in range(4 * g, min(c + 1, 4 * g + 4)):
                                x = nc.tensor.transpose(BK[2 + g][:, (kb % 4) * P:(kb % 4 + 1) * P],
                                                        PR[:, 0, kb * P:(kb + 1) * P], ident)
                            x.then_inc(wt[g], 1)

                    def weigh(h, c):
                        pe.wait_ge(yy, NT * h + c)
                        pe.wait_ge(wte[0], NT * h + c + 1)
                        if c >= 4:
                            pe.wait_ge(wte[1], 4 * h + (c - 3))
                        pe.wait_ge(vz, NT * h + c + 1)
                        for kb in range(c + 1):
                            x = nc.tensor.matmul(B_O[:, 0:P], WT[:, kb, :], V[:, kb, :],
                                                 start=(kb == 0), stop=(kb == c))
                        x.then_inc(av, 1)

                    def turn_output(h, c):
                        pe.wait_ge(yy, NT * h + c + 1)
                        pe.wait_ge(otf, NT * h + c)
                        nc.tensor.transpose(B_O[:, P:2 * P], Y[:, c % 2, :], ident).then_inc(ot, 1)

                    def sweep1(h, before):
                        pe.wait_ge(hi[0], 2 * KT * (h + 1))
                        pe.wait_ge(lo[0], 2 * KT * (h + 1))
                        pe.wait_ge(ex, 2 * NT * h)
                        for t in range(NB):
                            pe.wait_ge(rope, NB * h + max(t - 1, 0))
                            project(0, t, BK[4 + t % 2])
                            if before is not None:
                                if t == 0:
                                    turn_output(before, NT - 2)
                                    weigh(before, NT - 1)
                                if t == 1:
                                    turn_output(before, NT - 1)
                            if t >= 1:
                                b = (t - 1) % 2
                                pe.wait_ge(rope, NB * h + t)
                                pe.wait_ge(trf[b], 4 * h + (t - 1) // 2)
                                for j in range(2):
                                    x = nc.tensor.transpose(BK[2 + b][:, j * P:(j + 1) * P], QKR[:, b, j, :], ident)
                                x.then_inc(tr[b], 1)

                    def sweep2(h, last):
                        def project_values(t):
                            pe.wait_ge(vz, NT * h + t)
                            pe.wait_ge(smd, h)
                            project(1, t, B_V)

                        pe.wait_ge(hi[1], 2 * KT * (h + 1))
                        pe.wait_ge(lo[1], 2 * KT * (h + 1))
                        project_values(0)
                        for b in range(2):
                            pe.wait_ge(trf[b], 4 * (h + 1))
                        pe.wait_ge(rope, NB * (h + 1))
                        scores(h, 0)
                        for t in range(1, NT):
                            scores(h, t)
                            turn_weights(h, t - 1)
                            project_values(t)
                            if t >= 2:
                                turn_output(h, t - 2)
                            weigh(h, t - 1)
                        project_values(NT)
                        turn_weights(h, NT - 1)

                    def tail(h):
                        turn_output(h, NT - 2)
                        weigh(h, NT - 1)
                        turn_output(h, NT - 1)
                    heads(pe, sweep1, sweep2, tail)

        def decode_phase():
            take = area(AREA - 3 * P * NT // 2 - 2 * TS)
            G = 2 * P
            NEW = PAGES * P
            ROWS = H * 2 * DS
            KB = RAW[:, 0:4 * D].rearrange("p (s n) -> p s n", s=4)
            VB = take(4, D)
            SR, SX = take(TOK), take(TOK)
            AVS = take(D)
            QS = take(H, TS)
            WS = take(NB * TS)
            sgn, mx, nm, sm, rc, cf = (take(1) for _ in range(6))
            QZ = WH[:, 0:H * 136]
            WTS = WH[:, 1088:1088 + NB * 64].rearrange("p (a c) -> p a c", a=NB)
            VH2 = phase_tensor("VH2", [P, 2, D], F32R)
            VH = [WH[:, 1664 + s * D:1664 + (s + 1) * D] for s in range(2)] + [VH2[:, s, :] for s in range(2)]
            VL = [WL[:, s * D:(s + 1) * D] for s in (0, 1, 3, 4)]
            VHN, VLN = WH[:, 1664 + 2 * D:1664 + 3 * D], WL[:, 2 * D:3 * D]
            d_pt, d_in, d_avs = sem("d_pt"), sem("d_in"), sem("d_avs")
            k_ld = [sem(f"d_k{s}") for s in range(4)]
            v_ld = [sem(f"d_v{s}") for s in range(4)]
            ini, pre, pre2, tp, kh, kl, sc, slo, add, mxs, exd, wd, wtp, wr, whi, wlo, vh, vl, av, avd, avc, qh, ql, vn = (
                sem(f"d_{s}") for s in ("ini", "pre", "pre2", "tp", "kh", "kl", "sc", "slo", "add", "mx", "ex", "w", "wtp",
                                        "wr", "whi", "wlo", "vh", "vl", "av", "avd", "avc", "qh", "ql", "vn"))
            dch = sem("d_dve")
            S_AT = [(BK[2], 0, G), (BK[2], G, G), (BK[3], 0, G), (BK[6], 0, G + TS)]
            S_RD = [(BK[2], 2 * G, 0), (BK[3], G, 2 * G), (BK[6], G + TS, 3 * G)]
            OUT = PD[0]

            ORDER = ("L", "Q", "K0", "E", "K1", "K2", "K3", "V0", "W", "K4", "V1", "R0", "V2", "K5", "V3", "K6", "V4",
                     "R1", "V5", "K7", "V6", "V7")
            PE_ORDER = ("T0", "T1", "T2", "S0", "W", "T3", "T4", "S1", "V0", "T5", "V1", "V2", "T6", "S2", "V3", "V4",
                        "T7", "V5", "V6", "V7", "N", "S3")

            def sequences(eng, body, links=None, per=0):
                body(0, True, False)
                with eng.Fori(1, DB) as b:
                    if links:
                        links.enter(b - 1, per)
                    body(b, True, True)
                if links:
                    links.leave(DB - 1)
                body(DB, False, True)

            def wait(eng, s, count):
                if not isinstance(count, int) or count > 0:
                    eng.wait_ge(s, count)

            def page(eng, index):
                return bass.ds(eng.value_load(PT[0:1, bass.ds(index, 1)], min_val=0, max_val=cache_k.shape[0] - 1), 1)

            with nc.Block() as block:
                @block.sync
                def _(sp):
                    sp.dma_start(PT[:, :], page_table.rearrange("b n -> (b n)").unsqueeze(0)).then_inc(d_pt, 16)
                    for j, dst in enumerate((RAW[0:TS, 4 * D - D:4 * D], RAW[0:TS, 4 * D:5 * D], AVS[0:TS, :])):
                        sp.dma_start(dst, d_smB[:, j, :]).then_inc(d_in, 16)
                    sp.wait_ge(d_pt, 16)
                    sp.wait_ge(pre, 1)

                    def body(b, keys, values):
                        if keys:
                            for p in range(PAGES):
                                wait(sp, tp, 2 * PAGES * b + 2 * (p - 3))
                                src = cache_k[page(sp, b * PAGES + p), :, :, :, :]
                                sp.dma_start(KB[:, p % 4, :], src.rearrange("a p h c d -> (a p) (h c d)"))\
                                  .then_inc(k_ld[p % 4], 16)
                    sequences(sp, body)

                @block.gpsimd
                def _(pool):
                    pool.wait_ge(d_pt, 16)

                    def load(i):
                        def at(p):
                            wait(pool, vl, PAGES * i + (p - 3))
                            src = cache_v[page(pool, i * PAGES + p), :, :, :]
                            pool.dma_start(VB[:, p % 4, :], src.rearrange("a p h e -> (a p) (h e)"))\
                                .then_inc(v_ld[p % 4], 16)
                        for p in range(PAGES):
                            at(p)
                    load(0)
                    with pool.Fori(1, DB) as i:
                        load(i)

                @block.scalar
                def _(act):
                    act.wait_ge(d_in, 48)
                    act.wait_ge(pre, 1)
                    act.activation(QS, BK[2][:, 0:H * TS].rearrange("p (h t) -> p h t", h=H), ACT.Copy)
                    act.activation(XH[:, :, NEW:TOK], BK[2][:, H * TS:2 * H * TS].rearrange("p (h t) -> p h t", h=H),
                                   ACT.Copy).then_inc(pre2, 1)
                    act.activation(VHN[0:TS, :], AVS[0:TS, :], ACT.Copy).then_inc(vn, 1)
                    act.wait_ge(pre2, 1)
                    act.wait_ge(ini, 2)

                    def body(b, keys, values):
                        i = b - 1

                        def k_high(p):
                            for j in range(2):
                                act.wait_ge(tp, 2 * PAGES * b + 2 * p + j + 1)
                                act.activation(XH[:, 4 * j:4 * j + 4, p * P:(p + 1) * P],
                                               BK[j].rearrange("p (h t) -> p h t", h=4), ACT.Copy).then_inc(kh, 1)

                        def v_high(p):
                            act.wait_ge(v_ld[p % 4], 16 * (2 * i + p // 4 + 1))
                            wait(act, av, PAGES * i + max(p - 3, 0))
                            act.activation(VH[p % 4], VB[:, p % 4, :], ACT.Copy).then_inc(vh, 1)

                        def low_rows(s, r):
                            bank, n, at = S_RD[r]
                            act.wait_ge(sc, 4 * s + (2, 3, 4)[r])
                            act.activation(SX[0:64, at:at + n], bank[64:128, 0:n], ACT.Copy).then_inc(slo, 1)

                        def queries():
                            wait(act, sc, 4 * b)
                            for c in range(2):
                                rows = slice(DK * c, DK * c + DK)
                                dst = QZ.rearrange("p (h r) -> p h r", r=136)[rows, :, DS * c:DS * c + DS]
                                act.activation(dst, QS[rows, :, bass.ds(b * DS, DS)], ACT.Copy).then_inc(qh, 1)

                        def exponentials():
                            act.wait_ge(mxs, i + 1)
                            act.activation(SR[0:64, :], SR[0:64, :], ACT.Exp, scale=ATTN_SCALE, bias=nm[0:64, :],
                                           accum_out=sm[0:64, :]).then_inc(exd, 1)

                        def weights_high():
                            act.wait_ge(wr, i + 1)
                            ws = WS.rearrange("p (a c) -> p a c", a=NB)
                            act.activation(WTS[:, 0:PAGES, 0:TS], ws[:, 0:PAGES, :], ACT.Copy)
                            act.activation(WTS[0:TS, PAGES, 0:TS], ws[0:TS, PAGES, :], ACT.Copy).then_inc(whi, 1)

                        for step in ORDER:
                            if step[0] == "K" and keys:
                                k_high(int(step[1]))
                            elif step[0] == "R" and keys:
                                low_rows(b, int(step[1]))
                            elif step == "L" and values:
                                low_rows(i, 2)
                            elif step == "Q" and keys:
                                queries()
                            elif step == "E" and values:
                                exponentials()
                            elif step == "W" and values:
                                weights_high()
                            elif step[0] == "V" and values:
                                v_high(int(step[1]))
                        if values:
                            act.wait_ge(avd, i + 1)
                            wait(act, d_avs, 16 * i)
                            for j in range(2):
                                last = act.activation(AVS[0:64, 512 * j:512 * j + 512], OUT[0:64, j, :], ACT.Copy)
                            last.then_inc(avc, 1)
                            act.wait_ge(avc, i + 1)
                            act.dma_start(d_av[bass.ds(i, 1), :, :].rearrange("a r n -> (a r) n"), AVS[0:64, :])\
                               .then_inc(d_avs, 16)
                    sequences(act, body)
                    act.wait_ge(d_avs, 16 * DB)

                @block.vector
                def _(dve):
                    v = nc.vector
                    links = Chain(dve, dch)
                    v.memset(QZ.bitcast(F32), 0.0).then_inc(ini, 1)
                    links.link(v.tensor_scalar(sgn[0:64, :], LAM[0:64, :], 1.0, None, ALU.subtract))
                    v.tensor_scalar(sgn[0:64, :], sgn[0:64, :], cst[0:64, C_C1:C_C1 + 1], 1.0, ALU.mult, ALU.add)\
                     .then_inc(ini, 1)
                    dve.wait_ge(ini, 2)
                    dve.wait_ge(pre2, 1)
                    v.tensor_tensor(XL[:, :, NEW:TOK], BK[2][:, H * TS:2 * H * TS].rearrange("p (h t) -> p h t", h=H),
                                    XH[:, :, NEW:TOK].bitcast(F32), ALU.subtract).then_inc(vn, 1)
                    dve.wait_ge(vn, 2)
                    v.tensor_tensor(VLN[0:TS, :], AVS[0:TS, :], VHN[0:TS, :].bitcast(F32), ALU.subtract).then_inc(vn, 1)

                    def body(b, keys, values):
                        i = b - 1

                        def k_low(p):
                            for j in range(2):
                                dve.wait_ge(kh, 2 * PAGES * b + 2 * p + j + 1)
                                cols = (slice(None), slice(4 * j, 4 * j + 4), slice(p * P, (p + 1) * P))
                                v.tensor_tensor(XL[cols], BK[j].rearrange("p (h t) -> p h t", h=4),
                                                XH[cols].bitcast(F32), ALU.subtract).then_inc(kl, 1)

                        def v_low(p):
                            dve.wait_ge(vh, PAGES * i + p + 1)
                            v.tensor_tensor(VL[p % 4], VB[:, p % 4, :], VH[p % 4].bitcast(F32),
                                            ALU.subtract).then_inc(vl, 1)

                        def add_rows(s, r):
                            bank, n, at = S_RD[r]
                            dve.wait_ge(slo, 3 * s + r + 1)
                            v.tensor_tensor(SR[0:64, at:at + n], bank[0:64, 0:n], SX[0:64, at:at + n], ALU.add)\
                             .then_inc(add, 1)

                        def maximum():
                            add_rows(i, 2)
                            dve.wait_ge(add, 3 * b)
                            mask = cst[0:64, bass.ds(C_NEW + i * TS, TS)]
                            links.link(v.tensor_tensor(SR[0:64, NEW:TOK], SR[0:64, NEW:TOK], mask, ALU.add))
                            links.link(v.tensor_reduce(mx[0:64, :], SR[0:64, :], AX, ALU.max, negate=True))
                            v.tensor_scalar(nm[0:64, :], mx[0:64, :], ATTN_SCALE, None, ALU.mult).then_inc(mxs, 1)

                        def queries():
                            for c in range(2):
                                rows = slice(DK * c, DK * c + DK)
                                z = QZ.rearrange("p (h r) -> p h r", r=136)[rows, :, :]
                                dve.wait_ge(qh, 2 * b + c + 1)
                                v.tensor_tensor(z[:, :, 64 + DS * c:64 + DS * c + DS], QS[rows, :, bass.ds(b * DS, DS)],
                                                z[:, :, DS * c:DS * c + DS].bitcast(F32), ALU.subtract).then_inc(ql, 1)

                        def shares():
                            dve.wait_ge(exd, i + 1)
                            links.link(v.reciprocal(rc[0:64, :], sm[0:64, :]))
                            links.link(v.tensor_tensor(cf[0:64, :], rc[0:64, :], sgn[0:64, :], ALU.mult))
                            v.tensor_scalar(SR[0:64, :], SR[0:64, :], cf[0:64, :], None, ALU.mult).then_inc(wd, 1)

                        def weights_low():
                            dve.wait_ge(wtp, i + 1)
                            v.tensor_reduce(WS[:, 0:PAGES * TS].rearrange("p (a q) -> p a q", q=DS),
                                            BK[7].rearrange("p (a c q) -> p a q c", c=2, q=DS), AX, ALU.add)
                            v.tensor_reduce(WS[0:TS, PAGES * TS:NB * TS].rearrange("p (a q) -> p a q", q=DS),
                                            BK[3][0:TS, G:G + 64].rearrange("p (a c q) -> p a q c", c=2, q=DS),
                                            AX, ALU.add).then_inc(wr, 1)
                            dve.wait_ge(whi, i + 1)
                            dve.wait_ge(wr, i + 1)
                            ws = WS.rearrange("p (a c) -> p a c", a=NB)
                            v.tensor_tensor(WTS[:, 0:PAGES, TS:2 * TS], ws[:, 0:PAGES, :],
                                            WTS[:, 0:PAGES, 0:TS].bitcast(F32), ALU.subtract)
                            v.tensor_tensor(WTS[0:TS, PAGES, TS:2 * TS], ws[0:TS, PAGES, :],
                                            WTS[0:TS, PAGES, 0:TS].bitcast(F32), ALU.subtract).then_inc(wlo, 1)

                        for step in ORDER:
                            if step[0] == "K" and keys:
                                k_low(int(step[1]))
                            elif step[0] == "R" and keys:
                                if step == "R0" and values:
                                    dve.wait_ge(wtp, i + 1)
                                add_rows(b, int(step[1]))
                            elif step == "L" and values:
                                maximum()
                            elif step == "Q" and keys:
                                queries()
                            elif step == "E" and values:
                                shares()
                            elif step == "W" and values:
                                weights_low()
                            elif step[0] == "V" and values:
                                v_low(int(step[1]))
                    sequences(dve, body, links, 4)

                @block.tensor
                def _(pe):
                    pe.wait_ge(d_in, 48)
                    for h in range(H):
                        nc.tensor.transpose(BK[2][:, h * TS:(h + 1) * TS],
                                            RAW[0:TS, 3 * D + h * P:3 * D + (h + 1) * P], ident[0:TS, 0:TS])
                    for h in range(H):
                        x = nc.tensor.transpose(BK[2][:, (H + h) * TS:(H + h + 1) * TS],
                                                RAW[0:TS, 4 * D + h * P:4 * D + (h + 1) * P], ident[0:TS, 0:TS])
                    x.then_inc(pre, 1)
                    pe.wait_ge(vn, 3)

                    def body(b, keys, values):
                        i = b - 1

                        def turn(p):
                            pe.wait_ge(k_ld[p % 4], 16 * (2 * b + p // 4 + 1))
                            for j in range(2):
                                wait(pe, kl, 2 * PAGES * b + (2 * p + j - 1))
                                for h in range(4):
                                    x = nc.tensor.transpose(BK[j][:, h * P:(h + 1) * P],
                                                            KB[:, p % 4, (4 * j + h) * P:(4 * j + h + 1) * P], ident)
                                x.then_inc(tp, 1)

                        def score(g):
                            bank, at, n = S_AT[g]
                            pe.wait_ge(kl, 2 * PAGES * b + 4 * (g + 1))
                            if g == 0:
                                pe.wait_ge(ql, 2 * b + 2)
                            wait(pe, add, 3 * i + (1, 1, 2, 3)[g])
                            m = 0
                            for h in range(H):
                                for k in (XH, XL):
                                    x = nc.tensor.matmul(bank[:, at:at + n], QZ[:, h * P:(h + 1) * P],
                                                         k[:, h, g * G:g * G + n], start=(m == 0), stop=(m == 2 * H - 1))
                                    m += 1
                            x.then_inc(sc, 1)

                        def weights():
                            pe.wait_ge(wd, i + 1)
                            apart(pe)
                            for p in range(PAGES):
                                nc.tensor.transpose(BK[7][:, p * 64:(p + 1) * 64], SR[0:64, p * P:(p + 1) * P],
                                                    ident[0:64, 0:64])
                            nc.tensor.transpose(BK[3][0:TS, G:G + 64], SR[0:64, NEW:TOK], ident[0:64, 0:64])\
                              .then_inc(wtp, 1)

                        def value(p):
                            pe.wait_ge(vl, PAGES * i + p + 1)
                            if p == 0:
                                pe.wait_ge(wlo, i + 1)
                                wait(pe, avc, i)
                            for j in range(2):
                                for w in (VH, VL):
                                    x = nc.tensor.matmul(OUT[0:64, j, :], WTS[:, p, :], w[p % 4][:, 512 * j:512 * j + 512],
                                                         start=(p == 0 and w is VH), stop=False)
                            x.then_inc(av, 1)

                        def new_value():
                            for j in range(2):
                                for w in (VHN, VLN):
                                    x = nc.tensor.matmul(OUT[0:64, j, :], WTS[0:TS, PAGES, :],
                                                         w[0:TS, 512 * j:512 * j + 512], start=False, stop=(w is VLN))
                            x.then_inc(avd, 1)

                        for step in PE_ORDER:
                            if step[0] == "T" and keys:
                                turn(int(step[1]))
                            elif step[0] == "S" and keys:
                                score(int(step[1]))
                            elif step[0] == "V" and values:
                                value(int(step[1]))
                            elif step == "W" and values:
                                weights()
                            elif step == "N" and values:
                                new_value()
                    sequences(pe, body)

        def decode_output_phase():
            take = area()
            O = take(2, D)
            Z, E, SQ, Y = take(D), take(D), take(D), take(D)
            SL = take(P)
            ss, var, rs = take(H), take(H), take(H)
            o_ld, o_ez, o_ss, o_rs, o_y, o_t, ach, pch, dch = (
                sem(f"o_{s}") for s in ("ld", "ez", "ss", "rs", "y", "t", "act", "pool", "dve"))
            by_head = lambda t: t[0:TS, :].rearrange("p (h e) -> p h e", h=H)
            col = lambda t: t[0:TS, :].unsqueeze(2).to_broadcast([TS, H, P])
            with nc.Block() as block:
                @block.sync
                def _(sp):
                    for b in range(DB):
                        for part in range(2):
                            src = bass.AP(d_av.tensor, (b * 64 + part * TS) * D, [[D, DS], [DS * D + P, H], [1, P]])
                            sp.dma_start(O[b * DS:(b + 1) * DS, part, :].rearrange("p (h e) -> p h e", h=H), src)\
                              .then_inc(o_ld, 16)
                    sp.dma_start(Z[0:TS, :], d_smB[:, 3, :]).then_inc(o_ld, 16)
                    sp.dma_start(SL[0:TS, :], subln_b[0, :].partition_broadcast(TS)).then_inc(o_ld, 16)

                @block.scalar
                def _(act):
                    act.wait_ge(o_ld, 16 * (2 * DB + 2))
                    act.activation(E[0:TS, :], Z[0:TS, :], ACT.Tanh, scale=0.5).then_inc(o_ez, 1)

                @block.gpsimd
                def _(pool):
                    links = Chain(pool, pch)
                    pool.wait_ge(o_ss, 1)
                    links.link(nc.gpsimd.tensor_scalar(var[0:TS, :], ss[0:TS, :], 1.0 / P, EPS, ALU.mult, ALU.add))
                    nc.gpsimd.tensor_tensor(rs[0:TS, :], var[0:TS, :], neg_half[0:TS, :].to_broadcast([TS, H]), ALU.pow)\
                      .then_inc(o_rs, 1)

                @block.vector
                def _(dve):
                    v = nc.vector
                    links = Chain(dve, dch)
                    dve.wait_ge(o_ld, 16 * (2 * DB + 2))
                    links.link(v.tensor_tensor(O[0:TS, 0, :], O[0:TS, 0, :], O[0:TS, 1, :], ALU.add))
                    links.link(v.tensor_tensor(SQ[0:TS, :], O[0:TS, 0, :], O[0:TS, 0, :], ALU.mult))
                    v.tensor_reduce(ss[0:TS, :], by_head(SQ), AX, ALU.add).then_inc(o_ss, 1)
                    dve.wait_ge(o_ez, 1)
                    links.link(v.tensor_scalar(E[0:TS, :], E[0:TS, :], 1.0, None, ALU.add))
                    links.link(v.tensor_tensor(Z[0:TS, :], Z[0:TS, :], E[0:TS, :], ALU.mult))
                    links.link(v.tensor_tensor(by_head(Z), by_head(Z), SL[0:TS, :].unsqueeze(1).to_broadcast([TS, H, P]),
                                               ALU.mult))
                    dve.wait_ge(o_rs, 1)
                    links.link(v.tensor_tensor(by_head(Y), O[0:TS, 0, :].rearrange("p (h e) -> p h e", h=H), col(rs),
                                               ALU.mult))
                    v.scalar_tensor_tensor(Y[0:TS, :], Y[0:TS, :], 0.5 * (1.0 - LAM_INIT), Z[0:TS, :], ALU.mult, ALU.mult)\
                     .then_inc(o_y, 1)
                    dve.wait_ge(o_t, 1)
                    v.tensor_copy(YT[:, :, SEQ:TOK], BK[0][:, 0:H * TS].rearrange("p (h t) -> p h t", h=H))

                @block.tensor
                def _(pe):
                    pe.wait_ge(o_y, 1)
                    for h in range(H):
                        x = nc.tensor.transpose(BK[0][:, h * TS:(h + 1) * TS], Y[0:TS, h * P:(h + 1) * P],
                                                ident[0:TS, 0:TS])
                    x.then_inc(o_t, 1)

        def final_phase():
            take = area()
            GF = take(D)
            JK = take(2, D)
            out = take(2, D)
            ss, var, rs = take(2), take(2), take(2)
            f_ld, pch = sem("f_ld"), sem("f_pool")
            sq, rr, nn, st = two("f_sq"), two("f_rs"), two("f_n"), two("f_st")

            def each_pair(eng, body, links=None):
                with eng.Fori(0, NT // 2) as i:
                    if links:
                        links.enter(i, 2)
                    for b in range(2):
                        body(i, b, P)
                if links:
                    links.leave(NT // 2)
                body(NT // 2, 0, TS)

            def rows(i, b, n):
                return X1[0:n, bass.ds(2 * i + b, 1), :].rearrange("p a n -> p (a n)")

            with nc.Block() as block:
                @block.sync
                def _(sp):
                    sp.dma_start(GF, final_norm_g.partition_broadcast(P)).then_inc(f_ld, 16)

                    def body(i, b, n):
                        sp.wait_ge(nn[b], i + 1)
                        dst = y_p[0, bass.ds((2 * i + b) * P, P), :] if n == P else y_s.rearrange("b s n -> (b s) n")
                        sp.dma_start(dst, out[0:n, b, :]).then_inc(st[b], 16)
                    each_pair(sp, body)
                    sp.wait_ge(st[0], 16 * (NT // 2 + 1))
                    sp.wait_ge(st[1], 16 * (NT // 2))

                @block.scalar
                def _(act):
                    def body(i, b, n):
                        act.wait_ge(nn[b], i)
                        act.activation(JK[0:n, b, :], rows(i, b, n), ACT.Square, accum_out=ss[0:n, b:b + 1])\
                           .then_inc(sq[b], 1)
                    each_pair(act, body)

                @block.gpsimd
                def _(pool):
                    links = Chain(pool, pch)

                    def body(i, b, n):
                        pool.wait_ge(sq[b], i + 1)
                        apart(pool)
                        links.link(nc.gpsimd.tensor_scalar(var[0:n, b:b + 1], ss[0:n, b:b + 1], 1.0 / D, EPS,
                                                           ALU.mult, ALU.add))
                        nc.gpsimd.tensor_tensor(rs[0:n, b:b + 1], var[0:n, b:b + 1], neg_half[0:n, :], ALU.pow)\
                          .then_inc(rr[b], 1)
                    each_pair(pool, body, links)

                @block.vector
                def _(dve):
                    dve.wait_ge(f_ld, 16)

                    def body(i, b, n):
                        dve.wait_ge(rr[b], i + 1)
                        dve.wait_ge(st[b], 16 * i)
                        nc.vector.scalar_tensor_tensor(out[0:n, b, :], rows(i, b, n), rs[0:n, b:b + 1], GF[0:n, :],
                                                       ALU.mult, ALU.mult).then_inc(nn[b], 1)
                    each_pair(dve, body)

                @block.tensor
                def _(pe):
                    pass

        run(norm_phase, "na", True)
        run(gates_phase)
        run(mlstm_phase)
        run(mlstm_sample_phase)
        run(out_phase, "oa", w_out_a, True)
        run(norm_phase, "nb", False)
        run(attention_phase)
        run(decode_phase)
        run(decode_output_phase)
        run(out_phase, "ob", w_out_b, False)
        run(final_phase)



_INS = ['x_prompt', 'x_sample', 'cache_k', 'cache_v', 'state_C', 'state_n', 'state_m', 'page_table',
        'norm_g', 'w_in_a', 'b_i_a', 'b_f_a', 'hnorm_a', 'w_out_a', 'kv_norm_g', 'w_kv', 'w_in_b',
        'lam_q1', 'lam_k1', 'lam_q2', 'lam_k2', 'subln_b', 'w_out_b', 'final_norm_g']
_OUTS = [(1, SEQ, D), (DB, DS, D), (1, SEQ, H, 2, DK), (1, SEQ, H, P), (1, 1, H, P, P), (1, 1, H, P), (1, 1, H),
         (DB, DS, H, 2, DK), (DB, DS, H, P), (1, DB, H, P, P), (1, DB, H, P), (1, DB, H)]


def kernel(**inputs):
    import numpy as _np
    import concourse.bacc as _bacc
    from concourse import mybir as _mybir
    from concourse.bass_utils import run_bass_kernel_spmd as _run

    nc = _bacc.Bacc("TRN2", target_bir_lowering=False, num_devices=1)
    arrays, args = {}, []
    for name in _INS:
        a = _np.ascontiguousarray(inputs[name])
        arrays[f"in_{name}"] = a
        args.append(nc.dram_tensor(f"in_{name}", a.shape, _mybir.dt.from_np(a.dtype), kind="ExternalInput").ap())
    c = constants()
    arrays["in_consts"] = c
    args.append(nc.dram_tensor("in_consts", c.shape, _mybir.dt.float32, kind="ExternalInput").ap())
    for i, shape in enumerate(_OUTS):
        args.append(nc.dram_tensor(f"out_{i}", shape, _mybir.dt.float32, kind="ExternalOutput").ap())
    trunk_step(nc, *args)
    r = _run(nc, [arrays], core_ids=[0])
    return tuple(r.results[0][f"out_{i}"] for i in range(len(_OUTS)))
```

```python
from contextlib import ExitStack

import numpy as np

import concourse.bass as bass
from concourse import mybir

ALU = mybir.AluOpType
ACT = mybir.ActivationFunctionType
F32 = mybir.dt.float32
F32R = mybir.dt.float32r
I32 = mybir.dt.int32
AX = mybir.AxisListType.X

P = 128
D = 1024
KT = D // P
H = 8
NT = 8
SEQ = NT * P
DB, DS = 8, 4
TS = DB * DS
TOK = SEQ + TS
NB = NT + 1
PAGES = 8
DK = 64
HALF = DK // 2
EPS = 1e-6
BIG = 1e30
LAM_INIT = 0.8 - 0.6 * float(np.exp(-0.3))
ATTN_SCALE = DK ** -0.5
K_SCALE = P ** -0.5

C_ID = 0
C_MA = C_ID + P
C_MB = C_MA + P
C_COS = C_MB + P
C_SIN = C_COS + NB * HALF
C_MS = C_SIN + NB * HALF
C_ONE = C_MS + TS
C_COMP = C_ONE + DB
C_NEW = C_COMP + 2
C_EXP = C_NEW + DB * TS
C_C1 = C_EXP + 2
C_N = C_C1 + 1


def constants():
    c = np.zeros((P, C_N), np.float32)
    r = np.arange(P)
    c[:, C_ID:C_ID + P] = np.eye(P)
    c[:, C_MA:C_MA + P] = np.where(r[:, None] <= r[None, :], 0.0, BIG)
    c[:, C_MB:C_MB + P] = np.where(r[None, :] <= r[:, None], 0.0, -BIG)
    inv = (np.float32(10000.0) ** (-(np.arange(HALF, dtype=np.float32) / np.float32(HALF)))).astype(np.float32)
    for t in range(NB):
        pos = (t * P + r if t < NT else PAGES * P + r % DS).astype(np.float32)
        ang = pos[:, None] * inv[None, :]
        c[:, C_COS + t * HALF:C_COS + (t + 1) * HALF] = np.cos(ang)
        c[:, C_SIN + t * HALF:C_SIN + (t + 1) * HALF] = np.sin(ang)
    s = np.arange(TS)
    own = (s[:, None] // DS == s[None, :] // DS)
    c[:TS, C_MS:C_MS + TS] = np.where(own & (s[:, None] <= s[None, :]), 0.0, BIG)
    c[:TS, C_ONE:C_ONE + DB] = s[:, None] // DS == np.arange(DB)[None, :]
    c[:, C_COMP:C_COMP + 2] = r[:, None] // DK == np.arange(2)[None, :]
    q = np.arange(64) % DS
    for b in range(DB):
        ok = (s[None, :] // DS == b) & (s[None, :] % DS <= q[:, None])
        c[:64, C_NEW + b * TS:C_NEW + (b + 1) * TS] = np.where(ok, 0.0, -BIG)
    c[:, C_EXP] = -0.5
    c[:, C_EXP + 1] = 1.0
    c[:, C_C1] = r // DS % 2
    return c


class Chain:

    def __init__(self, eng, sem):
        self.eng, self.sem, self.base, self.n = eng, sem, 0, 0

    def link(self, ins):
        ins.then_inc(self.sem, 1)
        self.n += 1
        self.eng.wait_ge(self.sem, self.base + self.n)

    def enter(self, i, per):
        self.start, self.base, self.n, self.per = self.base + self.n, self.base + self.n + i * per, 0, per

    def leave(self, times):
        assert self.n == self.per, f"links in a turn: {self.n}"
        self.base, self.n = self.start + times * self.per, 0


def trunk_step(
    nc: bass.Bass,
    x_prompt, x_sample, cache_k, cache_v, state_C, state_n, state_m, page_table,
    norm_g, w_in_a, b_i_a, b_f_a, hnorm_a, w_out_a, kv_norm_g, w_kv, w_in_b,
    lam_q1, lam_k1, lam_q2, lam_k2, subln_b, w_out_b, final_norm_g, consts,
    y_p, y_s, k_p, v_p, c_p, n_p, m_p, k_s, v_s, c_s, n_s, m_s,
):
    ctx = ExitStack()

    def sb(name, shape, dt=F32):
        return ctx.enter_context(nc.sbuf_tensor(name, shape, dt))

    held = []

    def sem(name):
        held.append(nc.alloc_semaphore(name=name))
        return held[-1]

    scratch = []

    def phase_tensor(name, shape, dt=F32):
        return scratch[-1].enter_context(nc.sbuf_tensor(name, shape, dt))

    def run(program, *args):
        scratch.append(ExitStack())
        program(*args)
        scratch.pop().close()

    def fresh_semaphores():
        nc.clear_and_free_semaphores(list(held))
        held.clear()
        nc.all_engine_barrier()

    def two(name):
        return [sem(f"{name}{k}") for k in range(2)]

    consts_in = nc.alloc_semaphore(name="consts_in")

    passed = nc.alloc_semaphore(name="passed")

    def apart(eng):
        eng.sem_inc(passed, 1)

    def dram(name, shape):
        return nc.dram_tensor(name, shape, F32, kind="Internal").ap()

    with ctx:
        cst = sb("cst", [P, C_N])
        ident = cst[:, C_ID:C_ID + P]
        XH = sb("XH", [P, KT, TOK], F32R)
        XL = sb("XL", [P, KT, TOK], F32R)
        YX = sb("YX", [P, NB * D])
        YT = YX[:, 0:KT * TOK].rearrange("p (k t) -> p k t", k=KT)
        X1 = YX[:, :].rearrange("p (b n) -> p b n", b=NB)
        WH = sb("WH", [P, KT * 640], F32R)
        WL = sb("WL", [P, KT * 640], F32R)
        RAW = sb("RAW", [P, KT * 640])
        gA = sb("gA", [P, KT])
        gB = sb("gB", [P, KT])
        gKV = sb("gKV", [P, KT])
        one_row = cst[:, C_EXP + 1:C_EXP + 2]
        neg_half = cst[:, C_EXP:C_EXP + 1]
        PS = [ctx.enter_context(nc.psum_tensor(f"PS{k}", [P, 512], F32)) for k in range(4)]
        PD = [ctx.enter_context(nc.psum_tensor(f"PD{k}", [P, 2, 512], F32)) for k in range(2)]
        BK = [PS[0][:, :], PS[1][:, :], PS[2][:, :], PS[3][:, :],
              PD[0][:, 0, :], PD[0][:, 1, :], PD[1][:, 0, :], PD[1][:, 1, :]]

        AREA = 9430
        areas = []

        def area(size=AREA):
            areas.append(size)
            work = phase_tensor(f"WORK{len(areas)}", [P, size])
            at = [0]

            def take(*shape):
                n = int(np.prod(shape))
                v = work[:, at[0]:at[0] + n]
                at[0] += n
                assert at[0] <= size, at[0]
                if len(shape) == 1:
                    return v
                if len(shape) == 2:
                    return v.rearrange("p (a b) -> p a b", a=shape[0])
                return v.rearrange("p (a b c) -> p a b c", a=shape[0], b=shape[1])
            return take

        d_G = dram("d_G", [H, TOK])
        d_dec = dram("d_dec", [H, 2 * NT])
        d_smA = dram("d_smA", [TS, 5, D])
        d_smB = dram("d_smB", [TS, 4, D])
        d_x1 = dram("d_x1", [TOK, D])
        d_av = dram("d_av", [DB, 64, D])

        COL = sb("COL", [P, NB, 4, H])
        LAM = sb("LAM", [P, 1])
        PT = sb("PT", [1, DB * PAGES], I32)
        DEC = sb("DEC", [P, H * 2 * NT])

        GW = RAW[:, KT * 5 * P - KT * 2 * H:].rearrange("p (k c) -> p k c", k=KT)
        GH = WH[:, KT * 4 * P:KT * 4 * P + KT * 64].rearrange("p (k c) -> p k c", k=KT)
        GL = WL[:, KT * 4 * P:KT * 4 * P + KT * 64].rearrange("p (k c) -> p k c", k=KT)
        qk_weights = lambda w: w[:, 0:KT * 2 * P].rearrange("p (k c) -> p k c", k=KT)

        def load_qk_weights(sp, h, loaded):
            for j in range(2):
                sp.dma_start(qk_weights(RAW)[:, :, j * P:(j + 1) * P],
                             w_in_a[0, :, bass.ds(j * D + h * P, P)].rearrange("(k p) c -> p k c", p=P)).then_inc(loaded, 16)

        QK_B = ((w_in_b[0, :, :], gB), (w_kv, gKV))

        def load_qk_b(sp, h, loaded):
            for j, (w, _) in enumerate(QK_B):
                sp.dma_start(qk_weights(RAW)[:, :, j * P:(j + 1) * P],
                             w[:, bass.ds(h * P, P)].rearrange("(k p) c -> p k c", p=P)).then_inc(loaded, 16)

        def tok(j, n):
            return bass.ds(j * P, n)

        def norm_phase():
            take = area()
            SLOTS = 4
            xin = take(SLOTS, D)
            xn = take(2, D)
            junk = take(2, D)
            ss, var, rs = take(2), take(2), take(2)
            ld = [sem(f"na_ld{s}") for s in range(SLOTS)]
            sq, rr, xs, tp, hi, lo, pch, g_ld, g_zero, g_hi = (
                sem(f"na_{s}") for s in ("sq", "rs", "xn", "tp", "hi", "lo", "pool", "gw", "zero", "ghi"))
            size = lambda t: P if t < NT else TS
            bank = lambda t, half: BK[2 * (t % 2) + half].rearrange("p (k t) -> p k t", k=4)[:, :, 0:size(t)]

            with nc.Block() as block:
                @block.sync
                def _(sp):
                    for t in range(NB):
                        if t == 1:
                            sp.dma_start(cst[:, :], consts).then_inc(consts_in, 16)
                        if t >= SLOTS:
                            sp.wait_ge(xs, t - SLOTS + 1)
                        src = x_prompt[0, tok(t, P), :] if t < NT else x_sample.rearrange("b s n -> (b s) n")
                        sp.dma_start(xin[0:size(t), t % SLOTS, :], src).then_inc(ld[t % SLOTS], 16)
                        if t == 2:
                            with nc.allow_non_contiguous_dma("gate columns"):
                                sp.dma_start(GW, w_in_a[0, :, 5 * D:].rearrange("(k p) c -> p k c", p=P)).then_inc(g_ld, 16)

                @block.scalar
                def _(act):
                    with nc.allow_non_contiguous_dma("gains by contraction row"):
                        for g, v in ((gA, norm_g[0, :]), (gB, norm_g[1, :]), (gKV, kv_norm_g)):
                            act.dma_start(g[:, :], v.rearrange("(k p) -> p k", p=P)).then_inc(consts_in, 16)

                    def high(t):
                        for half in range(2):
                            act.wait_ge(tp, 2 * t + half + 1)
                            act.activation(XH[:, 4 * half:4 * half + 4, tok(t, size(t))], bank(t, half), ACT.Copy)\
                               .then_inc(hi, 1)

                    for t in range(NB):
                        n, b = size(t), t % 2
                        act.wait_ge(ld[t % SLOTS], 16 * (t // SLOTS + 1))
                        if t >= 2:
                            act.wait_ge(rr, t - 1)
                        act.activation(junk[0:n, b, :], xin[0:n, t % SLOTS, :], ACT.Square,
                                       accum_out=ss[0:n, b:b + 1]).then_inc(sq, 1)
                        if t >= 2:
                            high(t - 2)
                        if t == 6:
                            act.wait_ge(g_ld, 16)
                            act.wait_ge(consts_in, 64)
                            act.wait_ge(g_zero, 2)
                            for k in range(KT):
                                for f in range(2):
                                    last = act.activation(GH[:, k, 32 * f:32 * f + H], GW[:, k, H * f:H * f + H], ACT.Copy,
                                                          scale=gA[:, k:k + 1])
                            last.then_inc(g_hi, 1)
                    high(NB - 2)
                    high(NB - 1)

                @block.gpsimd
                def _(pool):
                    links = Chain(pool, pch)
                    nc.gpsimd.memset(GH.bitcast(F32), 0.0).then_inc(g_zero, 1)
                    nc.gpsimd.memset(GL.bitcast(F32), 0.0).then_inc(g_zero, 1)
                    pool.wait_ge(consts_in, 64)
                    for t in range(NB):
                        n, b = size(t), t % 2
                        pool.wait_ge(sq, t + 1)
                        if t >= 2:
                            pool.wait_ge(xs, t - 1)
                        links.link(nc.gpsimd.tensor_scalar(var[0:n, b:b + 1], ss[0:n, b:b + 1], 1.0 / D, EPS,
                                                           ALU.mult, ALU.add))
                        nc.gpsimd.tensor_tensor(rs[0:n, b:b + 1], var[0:n, b:b + 1], neg_half[0:n, :],
                                                ALU.pow).then_inc(rr, 1)

                @block.vector
                def _(dve):
                    def low(t):
                        for half in range(2):
                            dve.wait_ge(hi, 2 * t + half + 1)
                            cols = (slice(None), slice(4 * half, 4 * half + 4), tok(t, size(t)))
                            nc.vector.tensor_tensor(XL[cols], bank(t, half), XH[cols].bitcast(F32), ALU.subtract)\
                              .then_inc(lo, 1)

                    for t in range(NB):
                        n, b = size(t), t % 2
                        dve.wait_ge(rr, t + 1)
                        if t >= 2:
                            dve.wait_ge(tp, 2 * t - 2)
                        nc.vector.tensor_scalar(xn[0:n, b, :], xin[0:n, t % SLOTS, :], rs[0:n, b:b + 1], None,
                                                ALU.mult).then_inc(xs, 1)
                        if t >= 2:
                            low(t - 2)
                        if t == 7:
                            dve.wait_ge(g_hi, 1)
                            for k in range(KT):
                                for f in range(2):
                                    cols = slice(32 * f, 32 * f + H)
                                    nc.vector.scalar_tensor_tensor(GL[:, k, cols], GW[:, k, H * f:H * f + H], gA[:, k:k + 1],
                                                                   GH[:, k, cols].bitcast(F32), ALU.mult, ALU.subtract)
                    low(NB - 2)
                    low(NB - 1)

                @block.tensor
                def _(pe):
                    pe.wait_ge(consts_in, 64)
                    for t in range(NB):
                        n, b = size(t), t % 2
                        pe.wait_ge(xs, t + 1)
                        if t >= 2:
                            pe.wait_ge(lo, 2 * t - 2)
                        for k in range(KT):
                            out = BK[2 * b + k // 4].rearrange("p (k t) -> p k t", k=4)[:, k % 4, 0:n]
                            last = nc.tensor.transpose(out, xn[0:n, b, k * P:(k + 1) * P], ident[0:n, 0:n])
                            if k % 4 == 3:
                                last.then_inc(tp, 1)

        def gates_phase():
            take = area()
            gi, gf, t1, t2, bc, G = (take(TOK) for _ in range(6))
            QTT = take(TOK)
            bi, bf = take(1), take(1)
            m = take(NT + 1)
            M0 = take(DB)
            mS = take(DB)
            decE = take(2 * NT)
            onesr = take(P)
            g_ld, g_zero, g_hi, g_mm, g_ev, g_ab, g_ln, g_arg, g_exp, g_row, g_tp, g_col, g_st, dch, g_dec, g_w = (
                sem(s) for s in ("g_ld", "g_zero", "g_hi", "g_mm", "g_ev", "g_ab", "g_ln", "g_arg", "g_exp",
                                 "g_row", "g_tp", "g_col", "g_st", "g_dve", "g_dec", "g_w"))
            ach = sem("g_act")
            TH = TOK // 3

            def smp(t, d):
                return t[0:H, SEQ:TOK].rearrange("h (b s) -> h b s", s=DS)[:, :, d]

            with nc.Block() as block:
                @block.sync
                def _(sp):
                    with nc.allow_non_contiguous_dma("gate columns"):
                        load_qk_weights(sp, 0, g_w)
                        sp.dma_start(bi[0:H, :], b_i_a.rearrange("a h -> h a")).then_inc(g_ld, 16)
                        sp.dma_start(bf[0:H, :], b_f_a.rearrange("a h -> h a")).then_inc(g_ld, 16)
                        sp.dma_start(M0[0:H, :], state_m[0, :, :].rearrange("b h -> h b")).then_inc(g_ld, 16)
                        sp.wait_ge(g_row, 1)
                        sp.dma_start(d_G, G[0:H, :]).then_inc(g_st, 16)
                        sp.dma_start(m_p.rearrange("a b h -> h (a b)"), m[0:H, NT:NT + 1]).then_inc(g_st, 16)
                        sp.dma_start(m_s[0, :, :].rearrange("b h -> h b"), mS[0:H, :]).then_inc(g_st, 16)
                        sp.wait_ge(g_exp, 1)
                        sp.dma_start(d_dec, decE[0:H, :]).then_inc(g_dec, 16)
                        sp.wait_ge(g_dec, 16)
                        sp.dma_start(DEC[:, :], d_dec.rearrange("h c -> (h c)").partition_broadcast(P)).then_inc(g_st, 16)
                        sp.wait_ge(g_st, 64)

                @block.scalar
                def _(act):
                    act.wait_ge(g_w, 32)
                    for k in range(KT):
                        act.activation(qk_weights(WH)[:, k, :], qk_weights(RAW)[:, k, :], ACT.Copy, scale=gA[:, k:k + 1])\
                           .then_inc(g_hi, 1)
                    act.wait_ge(g_mm, 1)
                    for c in range(3):
                        for f, t in ((0, gi), (1, gf)):
                            last = act.activation(t[0:H, c * TH:(c + 1) * TH], BK[c][32 * f:32 * f + H, 0:TH], ACT.Copy)
                    last.then_inc(g_ev, 1)
                    act.wait_ge(g_ab, 1)
                    links = Chain(act, ach)
                    links.link(act.activation(t2[0:H, :], t1[0:H, :], ACT.Exp, scale=-1.0))
                    act.activation(bc[0:H, :], t2[0:H, :], ACT.Ln, bias=one_row[0:H, :]).then_inc(g_ln, 1)
                    act.wait_ge(g_arg, 1)
                    act.wait_ge(g_zero, 1)
                    act.activation(decE[0:H, 0:NT], t1[0:H, P - 1:SEQ:P], ACT.Exp)
                    links.link(act.activation(decE[0:H, NT:2 * NT], smp(t1, DS - 1), ACT.Exp))
                    act.activation(QTT[32:32 + H, :], t1[0:H, :], ACT.Exp).then_inc(g_exp, 1)
                    act.activation(QTT[64:64 + H, :], t2[0:H, :], ACT.Exp, scale=-1.0).then_inc(g_exp, 1)
                    act.wait_ge(g_arg, 2)
                    act.activation(QTT[96:96 + H, :], gf[0:H, :], ACT.Exp).then_inc(g_exp, 1)

                @block.vector
                def _(dve):
                    links = Chain(dve, dch)
                    v = nc.vector
                    v.memset(onesr[0:H, :], 1.0)
                    v.memset(m[0:H, 0:1], 0.0)
                    v.memset(QTT, 0.0).then_inc(g_zero, 1)
                    dve.wait_ge(g_zero, 1)
                    for k in range(KT):
                        dve.wait_ge(g_hi, k + 1)
                        v.scalar_tensor_tensor(qk_weights(WL)[:, k, :], qk_weights(RAW)[:, k, :], gA[:, k:k + 1],
                                               qk_weights(WH)[:, k, :].bitcast(F32), ALU.mult, ALU.subtract)
                    dve.wait_ge(g_ld, 48)
                    dve.wait_ge(g_ev, 1)
                    v.tensor_scalar(gi[0:H, :], gi[0:H, :], bi[0:H, :], None, ALU.add)
                    links.link(v.tensor_scalar(gf[0:H, :], gf[0:H, :], bf[0:H, :], None, ALU.add))
                    v.scalar_tensor_tensor(t1[0:H, :], gf[0:H, :], -1.0, gf[0:H, :], ALU.mult, ALU.max).then_inc(g_ab, 1)
                    dve.wait_ge(g_ln, 1)
                    links.link(v.scalar_tensor_tensor(t1[0:H, :], gf[0:H, :], 0.0, bc[0:H, :], ALU.min, ALU.subtract))
                    for c in range(NT):
                        cc = slice(c * P, (c + 1) * P)
                        v.tensor_tensor_scan(bc[0:H, cc], onesr[0:H, :], t1[0:H, cc], 0.0, ALU.mult, ALU.add)
                    links.link(v.tensor_copy(smp(bc, 0), smp(t1, 0)))
                    for d in range(1, DS):
                        links.link(v.tensor_tensor(smp(bc, d), smp(bc, d - 1), smp(t1, d), ALU.add))
                    links.link(v.tensor_tensor(gi[0:H, :], gi[0:H, :], bc[0:H, :], ALU.subtract))
                    v.tensor_copy(QTT[0:H, :], gi[0:H, :])
                    for c in range(NT):
                        cc = slice(c * P, (c + 1) * P)
                        last = slice((c + 1) * P - 1, (c + 1) * P)
                        links.link(v.tensor_tensor_scan(G[0:H, cc], gi[0:H, cc], gi[0:H, cc], m[0:H, c:c + 1],
                                                        ALU.max, ALU.max))
                        links.link(v.tensor_tensor(m[0:H, c + 1:c + 2], bc[0:H, last], G[0:H, last], ALU.add))
                    links.link(v.tensor_tensor(smp(G, 0), M0[0:H, :], smp(gi, 0), ALU.max))
                    for d in range(1, DS):
                        links.link(v.tensor_tensor(smp(G, d), smp(G, d - 1), smp(gi, d), ALU.max))
                    v.tensor_tensor(mS[0:H, :], smp(bc, DS - 1), smp(G, DS - 1), ALU.add).then_inc(g_row, 1)
                    for c in range(NT):
                        cc = slice(c * P, (c + 1) * P)
                        v.tensor_scalar(t1[0:H, cc], G[0:H, cc], -1.0, m[0:H, c:c + 1], ALU.mult, ALU.add)
                    for d in range(DS):
                        v.tensor_tensor(smp(t1, d), M0[0:H, :], smp(G, d), ALU.subtract)
                    v.tensor_tensor(t2[0:H, :], bc[0:H, :], G[0:H, :], ALU.add).then_inc(g_arg, 1)
                    for c in range(NT):
                        cc = slice(c * P, (c + 1) * P)
                        last = slice((c + 1) * P - 1, (c + 1) * P)
                        v.tensor_scalar(gf[0:H, cc], gi[0:H, cc], G[0:H, last], None, ALU.subtract)
                    for d in range(DS):
                        last = v.tensor_tensor(smp(gf, d), smp(gi, d), smp(G, DS - 1), ALU.subtract)
                    last.then_inc(g_arg, 1)
                    for c in range(NB):
                        n = P if c < NT else TS
                        if c % 4 == 0:
                            dve.wait_ge(g_tp, c // 4 + 1)
                        src = BK[3 + c // 4].rearrange("p (c q r) -> p c q r", c=4, q=4)[0:n, c % 4, :, 0:H]
                        last = v.tensor_copy(COL[0:n, c, :, :], src)
                    links.link(last)
                    v.tensor_scalar(COL[:, 0:NT, 3, :], COL[:, 0:NT, 3, :], K_SCALE, None, ALU.mult)
                    links.link(v.tensor_scalar(COL[0:TS, NT, 3, :], COL[0:TS, NT, 3, :], K_SCALE, None, ALU.mult))

                @block.tensor
                def _(pe):
                    for c in range(3):
                        cc = slice(c * TH, (c + 1) * TH)
                        n = 0
                        for k in range(KT):
                            for w, x in ((GH, XH), (GH, XL), (GL, XH)):
                                last = nc.tensor.matmul(BK[c][0:64, 0:TH], w[:, k, :], x[:, k, cc],
                                                        start=(n == 0), stop=(n == 3 * KT - 1))
                                n += 1
                    last.then_inc(g_mm, 1)
                    pe.wait_ge(g_exp, 3)
                    pe.wait_ge(g_arg, 2)
                    for c in range(NB):
                        n = P if c < NT else TS
                        out = BK[3 + c // 4].rearrange("p (c r) -> p c r", c=4)[0:n, c % 4, :]
                        last = nc.tensor.transpose(out, QTT[:, c * P:c * P + n], ident)
                        if c % 4 == 3 or c == NB - 1:
                            last.then_inc(g_tp, 1)

                @block.gpsimd
                def _(pool):
                    pass

        def mlstm_phase():
            take = area()
            QK = take(2, 2, P)
            QKT = take(NT, 2, P)
            KW = take(NT, P)
            GB = take(SEQ)
            DM, EX, AT = take(2, P), take(2, P), take(2, P)
            VA = take(2, P + 2)
            SG = take(2, 2, P)
            ZC, GZ = take(2, P), take(2, P)
            IS, NU = take(2, P + 2), take(2, P + 2)
            U, Y = take(2, P), take(2, P)
            dn, rd, ssq, var, rs = (take(2) for _ in range(5))
            JK = take(2, P)
            CA = take(P + 2)
            CS = take(P + 2)
            SS = take(5, P)
            HN = take(P)
            N1, N2 = 2 * P, 3 * P
            r0 = qk_weights
            r1 = lambda w: w[:, KT * N1:KT * (N1 + N2)].rearrange("p (k c) -> p k c", k=KT)
            a_w0, a_w1, a_g, a_hn, a_sst, a_cst = (sem(f"a_{s}") for s in ("w0", "w1", "g", "hn", "sst", "cst"))
            hi0, lo0, hi1, lo1 = (sem(f"a_{s}") for s in ("hi0", "lo0", "hi1", "lo1"))
            pj_mm, qk, voz, kw, dd, ee, s_mm, at, cell, ca, num, isc, uu, sq, rr, sg, gz, yy, ss, ct, cev = (
                sem(f"a_{s}") for s in ("pj", "qk", "voz", "kw", "dm", "ex", "s", "at", "cell", "ca", "num", "is",
                                        "u", "sq", "rs", "sg", "gz", "y", "ss", "ct", "cev"))
            pj_free, tr_mm, tr_free = two("a_pjf"), two("a_tr"), two("a_trf")
            dch, pch, ones_set = sem("a_dve"), sem("a_pool"), sem("a_ones")
            B_S, B_IN, B_X, B_C = BK[4], BK[5], BK[6], BK[7]

            def heads(eng, sweep1, sweep2, tail, links=None, per=0):
                sweep1(0, None)
                with eng.Fori(0, H - 1) as h:
                    if links:
                        links.enter(h, per)
                    sweep2(h, False)
                    sweep1(h + 1, h)
                if links:
                    links.leave(H - 1)
                sweep2(H - 1, True)
                tail(H - 1)

            def w_cols(group, h):
                return w_in_a[0, :, bass.ds(group * D + h * P, P)].rearrange("(k p) c -> p k c", p=P)

            with nc.Block() as block:
                @block.sync
                def _(sp):
                    def load1(h):
                        for j in range(3):
                            sp.dma_start(r1(RAW)[:, :, j * P:(j + 1) * P], w_cols(2 + j, h)).then_inc(a_w1, 16)

                    load1(0)

                    def body(h, last):
                        if not last:
                            sp.wait_ge(lo0, KT * h)
                            load_qk_weights(sp, h + 1, a_w0)
                        sp.wait_ge(dd, NT * h)
                        sp.dma_start(GB, d_G[bass.ds(h, 1), 0:SEQ].rearrange("a n -> (a n)").partition_broadcast(P))\
                          .then_inc(a_g, 16)
                        sp.wait_ge(gz, NT * h)
                        sp.dma_start(HN, hnorm_a[0, bass.ds(h * P, P)].partition_broadcast(P)).then_inc(a_hn, 16)
                        if not last:
                            sp.wait_ge(lo1, KT * (h + 1))
                            load1(h + 1)
                        sp.wait_ge(ss, h + 1)
                        sp.dma_start(d_smA[:, :, bass.ds(h * P, P)], SS[0:TS, :, :]).then_inc(a_sst, 16)
                        sp.wait_ge(cev, h + 1)
                        sp.dma_start(c_p[0, 0, bass.ds(h, 1), :, :].rearrange("a v k -> (a v) k"), CS[:, 0:P])\
                          .then_inc(a_cst, 16)
                        sp.dma_start(n_p[0, 0, bass.ds(h, 1), :].rearrange("a k -> k a"), CS[:, P:P + 1])\
                          .then_inc(a_cst, 16)
                    with sp.Fori(0, H - 1) as h:
                        body(h, False)
                    body(H - 1, True)
                    sp.wait_ge(a_sst, 16 * H)
                    sp.wait_ge(a_cst, 32 * H)

                @block.scalar
                def _(act):
                    def cut0(k):
                        act.activation(r0(WH)[:, k, :], r0(RAW)[:, k, :], ACT.Copy, scale=gA[:, k:k + 1])\
                           .then_inc(hi0, 1)

                    def tail(h):
                        act.wait_ge(ct, h + 1)
                        act.wait_ge(a_cst, 32 * h)
                        act.activation(CS[:, 0:P], B_X[:, 0:P], ACT.Copy)
                        act.activation(CS[:, P:P + 1], CA[:, P:P + 1], ACT.Copy).then_inc(cev, 1)

                    def sweep1(h, before):
                        act.wait_ge(a_w1, 48 * (h + 1))
                        act.wait_ge(pj_mm, 2 * NB * h)
                        for t in range(NB):
                            if t < KT:
                                act.activation(r1(WH)[:, t, :], r1(RAW)[:, t, :], ACT.Copy, scale=gA[:, t:t + 1])\
                                   .then_inc(hi1, 1)
                            act.wait_ge(pj_mm, 2 * NB * h + t + 1)
                            src = BK[t % 2][:, 0:N1].rearrange("p (j c) -> p j c", j=2)
                            if t < NT:
                                act.wait_ge(tr_mm[t % 2], 8 * h + t // 2)
                                act.wait_ge(kw, NT * h + max(t - 1, 0))
                                act.activation(QK[:, t % 2, :, :], src, ACT.Copy).then_inc(qk, 1)
                            else:
                                act.wait_ge(a_sst, 16 * h)
                                act.activation(SS[0:TS, 0:2, :], src[0:TS, :, :], ACT.Copy).then_inc(qk, 1)
                            act.wait_ge(qk, NB * h + t + 1)
                            act.sem_inc(pj_free[t % 2], 1)
                            if t == 0 and before is not None:
                                tail(before)

                    def sweep2(h, last):
                        if not last:
                            act.wait_ge(a_w0, 32 * (h + 1))
                            act.wait_ge(pj_mm, 2 * NB * h + NB)
                        for t in range(NB):
                            if t < NT:
                                act.wait_ge(dd, NT * h + t + 1)
                                act.activation(EX[:, t % 2, :], DM[:, t % 2, :], ACT.Exp, scale=-1.0,
                                               bias=COL[:, t, 0, bass.ds(h, 1)]).then_inc(ee, 1)
                                if not last:
                                    cut0(t)

                            def chunk(c):
                                act.wait_ge(cell, NT * h + c + 1)
                                act.activation(IS[:, c % 2, 0:P + 1], B_X[:, 0:P + 1], ACT.Copy,
                                               scale=COL[:, c, 1, bass.ds(h, 1)]).then_inc(isc, 1)
                                act.wait_ge(uu, NT * h + c + 1)
                                act.activation(JK[:, c % 2, :], U[:, c % 2, :], ACT.Square,
                                               accum_out=ssq[:, c % 2:c % 2 + 1]).then_inc(sq, 1)
                            u = NB + t
                            act.wait_ge(pj_mm, 2 * NB * h + u + 1)
                            src = BK[u % 2][:, 0:N2].rearrange("p (j c) -> p j c", j=3)
                            if t < NT:
                                act.wait_ge(cell, NT * h + max(t - 1, 0))
                                act.wait_ge(yy, NT * h + max(t - 1, 0))
                                act.activation(VA[:, t % 2, 0:P], src[:, 0, :], ACT.Copy)
                                act.activation(SG[:, t % 2, :, :], src[:, 1:3, :], ACT.Tanh, scale=0.5)
                                act.activation(ZC[:, t % 2, :], src[:, 2, :], ACT.Copy).then_inc(voz, 1)
                                act.wait_ge(voz, NT * h + t + 1)
                            else:
                                act.activation(SS[0:TS, 2:5, :], src[0:TS, :, :], ACT.Copy).then_inc(ss, 1)
                                act.wait_ge(ss, h + 1)
                            act.sem_inc(pj_free[u % 2], 1)
                            if t >= 1:
                                chunk(t - 1)
                    heads(act, sweep1, sweep2, tail)

                @block.gpsimd
                def _(pool):
                    links = Chain(pool, pch)
                    g = nc.gpsimd
                    def sweep1(h, before):
                        pool.wait_ge(cell, NT * h)
                        for t in range(NT):
                            pool.wait_ge(qk, NB * h + t + 1)
                            g.tensor_tensor(KW[:, t, :], QK[:, t % 2, 1, :],
                                            COL[:, t, 3, bass.ds(h, 1)].to_broadcast([P, P]), ALU.mult)\
                             .then_inc(kw, 1)

                    def sweep2(h, last):
                        pool.wait_ge(a_hn, 16 * (h + 1))
                        for t in range(NB):
                            if t >= 1:
                                b = (t - 1) % 2
                                pool.wait_ge(sq, NT * h + t)
                                apart(pool)
                                links.link(g.tensor_scalar(var[:, b:b + 1], ssq[:, b:b + 1], 4.0 / P, 16 * EPS,
                                                           ALU.mult, ALU.add))
                                g.tensor_tensor(rs[:, b:b + 1], var[:, b:b + 1], neg_half, ALU.pow).then_inc(rr, 1)
                            if t < NT:
                                b = t % 2
                                pool.wait_ge(sg, NT * h + t + 1)
                                links.link(g.tensor_tensor(GZ[:, b, :], ZC[:, b, :], SG[:, b, 1, :], ALU.mult))
                                g.tensor_tensor(GZ[:, b, :], GZ[:, b, :], HN, ALU.mult)\
                                 .then_inc(gz, 1)
                    heads(pool, sweep1, sweep2, lambda h: None, links, 16)

                @block.vector
                def _(dve):
                    v = nc.vector
                    links = Chain(dve, dch)

                    def cut0(h, k):
                        dve.wait_ge(hi0, KT * h + k + 1)
                        v.scalar_tensor_tensor(r0(WL)[:, k, :], r0(RAW)[:, k, :], gA[:, k:k + 1],
                                               r0(WH)[:, k, :].bitcast(F32), ALU.mult, ALU.subtract).then_inc(lo0, 1)

                    v.memset(VA[:, :, P:P + 1], 1.0).then_inc(ones_set, 1)
                    def y_transposed(h, c):
                        dve.wait_ge(tr_mm[c % 2], 8 * h + 4 + c // 2 + 1)
                        v.tensor_copy(YT[:, bass.ds(h, 1), c * P:(c + 1) * P].rearrange("p a c -> p (a c)"),
                                      BK[2 + c % 2][:, 0:P]).then_inc(tr_free[c % 2], 1)

                    def sweep1(h, before):
                        for t in range(NB):
                            if t == 1 and before is not None:
                                y_transposed(before, NT - 1)
                            if t < KT:
                                dve.wait_ge(hi1, KT * h + t + 1)
                                v.scalar_tensor_tensor(r1(WL)[:, t, :], r1(RAW)[:, t, :], gA[:, t:t + 1],
                                                       r1(WH)[:, t, :].bitcast(F32), ALU.mult, ALU.subtract)\
                                 .then_inc(lo1, 1)
                            if t >= 1:
                                b = (t - 1) % 2
                                dve.wait_ge(tr_mm[b], 8 * h + (t - 1) // 2 + 1)
                                v.tensor_copy(QKT[:, t - 1, :, :],
                                              BK[2 + b][:, 0:N1].rearrange("p (j c) -> p j c", j=2))\
                                 .then_inc(tr_free[b], 1)

                    def sweep2(h, last):
                        dve.wait_ge(cev, h)
                        v.memset(CA, 0.0).then_inc(ca, 1)
                        dve.wait_ge(a_g, 16 * (h + 1))
                        for t in range(NB):
                            if t < NT:
                                v.tensor_tensor(DM[:, t % 2, :], GB[:, t * P:(t + 1) * P], cst[:, C_MA:C_MA + P],
                                                ALU.add).then_inc(dd, 1)
                                dve.wait_ge(ee, NT * h + t + 1)
                                dve.wait_ge(s_mm, NT * h + t + 1)
                                v.scalar_tensor_tensor(AT[:, t % 2, :], B_S[:, 0:P], K_SCALE, EX[:, t % 2, :],
                                                       ALU.mult, ALU.mult).then_inc(at, 1)
                                if not last:
                                    cut0(h, t)
                            if t >= 1:
                                c = t - 1
                                b = c % 2
                                dve.wait_ge(cell, NT * h + c + 1)
                                v.scalar_tensor_tensor(CA[:, 0:P + 1], CA[:, 0:P + 1],
                                                       DEC[:, bass.ds(h * 2 * NT + c, 1)], B_C[:, 0:P + 1],
                                                       ALU.mult, ALU.add).then_inc(ca, 1)
                                dve.wait_ge(isc, NT * h + c + 1)
                                v.tensor_tensor(NU[:, b, 0:P + 1], B_IN[:, 0:P + 1], IS[:, b, 0:P + 1], ALU.add)\
                                 .then_inc(num, 1)
                                dve.wait_ge(num, NT * h + c + 1)
                                den = NU[:, b, P:P + 1]
                                links.link(v.scalar_tensor_tensor(dn[:, b:b + 1], den, -1.0, den, ALU.mult, ALU.max))
                                links.link(v.tensor_tensor(dn[:, b:b + 1], dn[:, b:b + 1],
                                                           COL[:, c, 2, bass.ds(h, 1)], ALU.max))
                                links.link(v.reciprocal(rd[:, b:b + 1], dn[:, b:b + 1]))
                                v.scalar_tensor_tensor(U[:, b, :], NU[:, b, 0:P], rd[:, b:b + 1], SG[:, b, 0, :],
                                                       ALU.mult, ALU.mult).then_inc(uu, 1)
                            if t >= 2:
                                y_transposed(h, t - 2)
                            if t < NT:
                                b = t % 2
                                dve.wait_ge(voz, NT * h + t + 1)
                                v.tensor_scalar(SG[:, b, :, :], SG[:, b, :, :], 1.0, None, ALU.add).then_inc(sg, 1)
                                dve.wait_ge(sg, NT * h + t + 1)
                            if t >= 1:
                                b = (t - 1) % 2
                                dve.wait_ge(rr, NT * h + t)
                                dve.wait_ge(gz, NT * h + t)
                                v.scalar_tensor_tensor(Y[:, b, :], U[:, b, :], rs[:, b:b + 1], GZ[:, b, :],
                                                       ALU.mult, ALU.mult).then_inc(yy, 1)
                    heads(dve, sweep1, sweep2, lambda h: y_transposed(h, NT - 1), links, 24)

                @block.tensor
                def _(pe):
                    def project(reg, n, t, bank):
                        rows = P if t < NT else TS
                        tt = slice(t * P, t * P + rows)
                        i = 0
                        for k in range(KT):
                            for x, w in ((XH, WH), (XH, WL), (XL, WH)):
                                last = nc.tensor.matmul(bank[0:rows, 0:n], x[:, k, tt], reg(w)[:, k, :],
                                                        start=(i == 0), stop=(i == 3 * KT - 1))
                                i += 1
                        last.then_inc(pj_mm, 1)

                    pe.wait_ge(ones_set, 1)

                    def y_transpose(h, c):
                        pe.wait_ge(yy, NT * h + c + 1)
                        pe.wait_ge(tr_free[c % 2], 8 * h + 4 + c // 2)
                        nc.tensor.transpose(BK[2 + c % 2][:, 0:P], Y[:, c % 2, :], ident).then_inc(tr_mm[c % 2], 1)

                    def tail(h):
                        y_transpose(h, NT - 1)
                        pe.wait_ge(ca, NB * h + NB)
                        pe.wait_ge(isc, NT * h + NT)
                        nc.tensor.transpose(B_X[:, 0:P], CA[:, 0:P], ident).then_inc(ct, 1)

                    def sweep1(h, before):
                        pe.wait_ge(hi0, KT * h)
                        pe.wait_ge(lo0, KT * h)
                        for t in range(NB):
                            pe.wait_ge(pj_free[t % 2], NB * h + t // 2)
                            project(r0, N1, t, BK[t % 2])
                            if t == 0 and before is not None:
                                tail(before)
                            if t >= 1:
                                b = (t - 1) % 2
                                pe.wait_ge(qk, NB * h + t)
                                pe.wait_ge(tr_free[b], 8 * h + (t - 1) // 2)
                                for j in range(2):
                                    x = nc.tensor.transpose(BK[2 + b][:, j * P:(j + 1) * P], QK[:, b, j, :], ident)
                                x.then_inc(tr_mm[b], 1)

                    def sweep2(h, last):
                        pe.wait_ge(hi1, KT * (h + 1))
                        pe.wait_ge(lo1, KT * (h + 1))

                        def run_cell(c):
                            b = c % 2
                            pe.wait_ge(at, NT * h + c + 1)
                            pe.wait_ge(voz, NT * h + c + 1)
                            pe.wait_ge(num, NT * h + c)
                            nc.tensor.matmul(B_IN[:, 0:P + 1], AT[:, b, :], VA[:, b, 0:P + 1], start=True, stop=True)
                            pe.wait_ge(ca, NB * h + c + 1)
                            pe.wait_ge(isc, NT * h + c)
                            nc.tensor.matmul(B_X[:, 0:P + 1], QKT[:, c, 0, :], CA[:, 0:P + 1], start=True, stop=True)
                            pe.wait_ge(kw, NT * h + c + 1)
                            nc.tensor.matmul(B_C[:, 0:P + 1], KW[:, c, :], VA[:, b, 0:P + 1], start=True, stop=True)\
                              .then_inc(cell, 1)

                        for t in range(NB):
                            u = NB + t
                            if t < NT:
                                pe.wait_ge(tr_free[t % 2], 8 * h + t // 2 + 1)
                                pe.wait_ge(at, NT * h + t)
                                nc.tensor.matmul(B_S[:, 0:P], QKT[:, t, 1, :], QKT[:, t, 0, :], start=True, stop=True)\
                                  .then_inc(s_mm, 1)
                            pe.wait_ge(pj_free[u % 2], NB * h + u // 2)
                            project(r1, N2, t, BK[u % 2])
                            if t >= 1:
                                run_cell(t - 1)
                            if t >= 2:
                                y_transpose(h, t - 2)
                    heads(pe, sweep1, sweep2, tail)

        def mlstm_sample_phase():
            take = area()
            XS = RAW[:, 2 * DB * P:2 * DB * P + 10 * P].rearrange("p (s j c) -> p s j c", s=2, j=5)
            CI = RAW[:, 0:2 * DB * P].rearrange("p (s b k) -> p s b k", s=2, b=DB)
            CN = take(2, DB, P)
            GS = take(H, TS)
            CT = take(DB, P + 2)
            nN = take(P)
            nT = take(DB, H)
            nO = take(DB, H)
            nM = take(DB)
            QT2 = take(2, TS)
            QZ = take(DB * (TS + DS))
            VW = take(DB, P)
            WG = take(DB)
            VA = take(2, P + 2)
            DM, EX, AT = take(TS), take(TS), take(TS)
            SG = take(2, 2, P)
            GZ, U, Y, JK = take(2, P), take(2, P), take(2, P), take(P)
            IS, NU = take(2, P + 2), take(2, P + 2)
            dn, rd, ssq, var, rs = (take(2) for _ in range(5))
            HN = take(D)
            b_x, b_c, b_st, cn, yy = two("b_x"), two("b_c"), two("b_st"), two("b_cn"), two("b_y")
            b_k, b_n = sem("b_k"), sem("b_n")
            ini, qt, ctp, s_mm, qe, cte, ee, dd, at, wg, qz, vw, cell, upd, isc, num, uu, sq, rr, ez, sg, gz, yt, yte, nev = (
                sem(f"b_{s}") for s in ("ini", "qt", "ctp", "s", "qe", "cte", "ex", "dm", "at", "wg", "qz", "vw", "cell",
                                        "upd", "is", "num", "u", "sq", "rs", "ez", "sg", "gz", "yt", "yte", "nev"))
            dch, pch, n_tp = sem("b_dve"), sem("b_pool"), sem("b_ntp")

            def heads(eng, body, links=None, per=0):
                with eng.Fori(0, H // 2) as i:
                    if links:
                        links.enter(i, per)
                    for b in range(2):
                        body(i, b, i * 2 + b)
                if links:
                    links.leave(H // 2)

            with nc.Block() as block:
                @block.sync
                def _(sp):
                    sp.dma_start(GS[0:TS, :, :], d_G[:, SEQ:TOK].partition_broadcast(TS)).then_inc(b_k, 16)
                    sp.dma_start(HN, hnorm_a[0, :].partition_broadcast(P)).then_inc(b_k, 16)
                    sp.dma_start(nN[0:DB * H, :], state_n[0, :, :, :].rearrange("b h k -> (b h) k")).then_inc(b_k, 16)

                    with sp.Fori(0, H // 2) as i:
                        for b in range(2):
                            h = i * 2 + b
                            sp.wait_ge(cn[b], i)
                            apart(sp)
                            sp.wait_ge(yy[b], i)
                            sp.dma_start(XS[0:TS, b, :, :], d_smA[:, :, bass.ds(h * P, P)]).then_inc(b_x[b], 16)
                            sp.dma_start(CI[:, b, :, :],
                                         state_C[0, :, bass.ds(h, 1), :, :].rearrange("b a v k -> v (b a) k"))\
                              .then_inc(b_c[b], 16)

                @block.scalar
                def _(act):
                    def body(i, b, h):
                        act.wait_ge(qt, h + 1)
                        act.activation(QT2, BK[0][:, 0:2 * TS].rearrange("p (a t) -> p a t", a=2), ACT.Copy)\
                           .then_inc(qe, 1)
                        act.wait_ge(b_x[b], 16 * (i + 1))
                        act.wait_ge(yy[b], i)
                        act.activation(SG[0:TS, b, :, :], XS[0:TS, b, 3:5, :], ACT.Tanh, scale=0.5).then_inc(ez, 1)
                        act.activation(VA[0:TS, b, 0:P], XS[0:TS, b, 2, :], ACT.Copy)
                        act.wait_ge(dd, h + 1)
                        act.activation(EX[0:TS, :], DM[0:TS, :], ACT.Exp, scale=-1.0,
                                       bias=COL[0:TS, NT, 0, bass.ds(h, 1)]).then_inc(ee, 1)
                        act.wait_ge(ctp, h + 1)
                        for g in range(2):
                            last = act.activation(CT[:, 4 * g:4 * g + 4, 0:P],
                                                  BK[1 + g].rearrange("p (b v) -> p b v", b=4), ACT.Copy)
                        last.then_inc(cte, 1)
                        act.wait_ge(cell, h + 1)
                        act.activation(IS[0:TS, b, 0:P + 1], BK[5][0:TS, 0:P + 1], ACT.Copy,
                                       scale=COL[0:TS, NT, 1, bass.ds(h, 1)]).then_inc(isc, 1)
                        act.wait_ge(uu, h + 1)
                        act.activation(JK[0:TS, :], U[0:TS, b, :], ACT.Square, accum_out=ssq[0:TS, b:b + 1]).then_inc(sq, 1)
                    heads(act, body)

                @block.gpsimd
                def _(pool):
                    g = nc.gpsimd
                    links = Chain(pool, pch)
                    pool.wait_ge(b_k, 48)

                    def body(i, b, h):
                        pool.wait_ge(sg, h + 1)
                        links.link(g.tensor_tensor(GZ[0:TS, b, :], XS[0:TS, b, 4, :], SG[0:TS, b, 1, :], ALU.mult))
                        g.tensor_tensor(GZ[0:TS, b, :], GZ[0:TS, b, :], HN[0:TS, bass.ds(h * P, P)], ALU.mult).then_inc(gz, 1)
                        pool.wait_ge(sq, h + 1)
                        apart(pool)
                        links.link(g.tensor_scalar(var[0:TS, b:b + 1], ssq[0:TS, b:b + 1], 4.0 / P, 16 * EPS, ALU.mult, ALU.add))
                        g.tensor_tensor(rs[0:TS, b:b + 1], var[0:TS, b:b + 1], neg_half[0:TS, :], ALU.pow).then_inc(rr, 1)
                        pool.wait_ge(cn[b], i + 1)
                        pool.dma_start(c_s[0, :, bass.ds(h, 1), :, :].rearrange("b a v k -> v (b a) k"), CN[:, b, :, :])\
                            .then_inc(b_st[b], 16)
                    heads(pool, body, links, 4)
                    pool.wait_ge(nev, 1)
                    pool.dma_start(n_s[0, :, :, :].rearrange("b h k -> (b h) k"), nN[0:DB * H, :]).then_inc(b_n, 16)
                    for b in range(2):
                        pool.wait_ge(b_st[b], 16 * (H // 2))
                    pool.wait_ge(b_n, 16)

                @block.vector
                def _(dve):
                    v = nc.vector
                    links = Chain(dve, dch)
                    v.memset(QZ, 0.0).then_inc(ini, 1)
                    v.memset(VA[:, :, P:P + 1], 1.0).then_inc(ini, 1)
                    dve.wait_ge(ini, 2)
                    dve.wait_ge(n_tp, 1)
                    links.link(v.tensor_copy(nT, BK[0][:, 0:DB * H].rearrange("p (b h) -> p b h", b=DB)))
                    dve.wait_ge(b_k, 48)

                    def weight(i, b, h):
                        hh = bass.ds(h, 1)
                        v.tensor_tensor(DM[0:TS, :], GS[0:TS, hh, :].rearrange("p a t -> p (a t)"),
                                        cst[0:TS, C_MS:C_MS + TS], ALU.add).then_inc(dd, 1)
                        dve.wait_ge(upd, h)
                        v.tensor_tensor(WG[0:TS, :], cst[0:TS, C_ONE:C_ONE + DB],
                                        COL[0:TS, NT, 3, hh].to_broadcast([TS, DB]), ALU.mult).then_inc(wg, 1)
                        dve.wait_ge(wg, h + 1)
                        dve.wait_ge(b_x[b], 16 * (i + 1))
                        v.tensor_tensor(VW[0:TS, :, :],
                                        XS[0:TS, b, 2, :].unsqueeze(1).to_broadcast([TS, DB, P]),
                                        WG[0:TS, :].unsqueeze(2).to_broadcast([TS, DB, P]), ALU.mult).then_inc(vw, 1)

                    def y_transposed(h):
                        dve.wait_ge(yt, h + 1)
                        v.tensor_copy(YT[:, bass.ds(h, 1), SEQ:TOK].rearrange("p a t -> p (a t)"),
                                      BK[4][:, 2 * P:2 * P + TS]).then_inc(yte, 1)

                    def body(i, b, h, first, last):
                        hh = bass.ds(h, 1)
                        dve.wait_ge(qe, h + 1)
                        v.tensor_copy(QZ.rearrange("p (b s) -> p b s", s=TS + DS)[:, :, 0:DS],
                                      QT2[:, 0, :].rearrange("p (b s) -> p b s", s=DS))
                        v.tensor_copy(CT[:, :, P:P + 1].rearrange("p b a -> p (b a)"),
                                      nT[:, :, hh].rearrange("p b a -> p (b a)")).then_inc(qz, 1)
                        dve.wait_ge(ee, h + 1)
                        dve.wait_ge(s_mm, h + 1)
                        dec = DEC[:, bass.ds(h * 2 * NT + NT, DB)]
                        links.link(v.tensor_tensor(nM, nT[:, :, hh].rearrange("p b a -> p (b a)"), dec, ALU.mult))
                        v.tensor_tensor(nO[:, :, hh].rearrange("p b a -> p (b a)"), nM, BK[3][:, 64:64 + DB], ALU.add)
                        v.scalar_tensor_tensor(AT[0:TS, :], BK[3][0:TS, 0:TS], K_SCALE, EX[0:TS, :],
                                               ALU.mult, ALU.mult).then_inc(at, 1)
                        if not first:
                            y_transposed(h - 1)
                        dve.wait_ge(ez, h + 1)
                        v.tensor_scalar(SG[0:TS, b, :, :], SG[0:TS, b, :, :], 1.0, None, ALU.add).then_inc(sg, 1)
                        dve.wait_ge(sg, h + 1)
                        if not last:
                            weight(i + b, 1 - b, h + 1)
                        dve.wait_ge(cell, h + 1)
                        dve.wait_ge(isc, h + 1)
                        c = slice(b, b + 1)
                        links.link(v.tensor_tensor(NU[0:TS, b, 0:P + 1], BK[4][0:TS, 0:P + 1], IS[0:TS, b, 0:P + 1],
                                                   ALU.add))
                        den = NU[0:TS, b, P:P + 1]
                        links.link(v.scalar_tensor_tensor(dn[0:TS, c], den, -1.0, den, ALU.mult, ALU.max))
                        links.link(v.tensor_tensor(dn[0:TS, c], dn[0:TS, c], COL[0:TS, NT, 2, hh], ALU.max))
                        links.link(v.reciprocal(rd[0:TS, c], dn[0:TS, c]))
                        v.scalar_tensor_tensor(U[0:TS, b, :], NU[0:TS, b, 0:P], rd[0:TS, c], SG[0:TS, b, 0, :],
                                               ALU.mult, ALU.mult).then_inc(uu, 1)
                        dve.wait_ge(upd, h + 1)
                        dve.wait_ge(b_st[b], 16 * i)
                        for s in range(DB):
                            last_one = v.scalar_tensor_tensor(CN[:, b, s, :], CI[:, b, s, :],
                                                              DEC[:, bass.ds(h * 2 * NT + NT + s, 1)],
                                                              BK[6 + s // 4].rearrange("p (b k) -> p b k", b=4)[:, s % 4, :],
                                                              ALU.mult, ALU.add)
                        last_one.then_inc(cn[b], 1)
                        dve.wait_ge(rr, h + 1)
                        dve.wait_ge(gz, h + 1)
                        v.scalar_tensor_tensor(Y[0:TS, b, :], U[0:TS, b, :], rs[0:TS, c], GZ[0:TS, b, :],
                                               ALU.mult, ALU.mult).then_inc(yy[b], 1)

                    weight(0, 0, 0)
                    body(0, 0, 0, True, False)
                    body(0, 1, 1, False, False)
                    with dve.Fori(1, H // 2 - 1) as i:
                        links.enter(i - 1, 10)
                        for b in range(2):
                            body(i, b, i * 2 + b, False, False)
                    links.leave(H // 2 - 2)
                    body(H // 2 - 1, 0, H - 2, False, False)
                    body(H // 2 - 1, 1, H - 1, False, True)
                    y_transposed(H - 1)
                    dve.wait_ge(n_tp, 2)
                    v.tensor_copy(nN[0:DB * H, :], BK[1][0:DB * H, 0:P]).then_inc(nev, 1)

                @block.tensor
                def _(pe):
                    pe.wait_ge(b_k, 48)
                    nc.tensor.transpose(BK[0][:, 0:DB * H], nN[0:DB * H, :], ident[0:DB * H, 0:DB * H]).then_inc(n_tp, 1)
                    pe.wait_ge(dch, 1)

                    def y_transpose(i, b):
                        pe.wait_ge(yy[b], i + 1)
                        apart(pe)
                        nc.tensor.transpose(BK[4][:, 2 * P:2 * P + TS], Y[0:TS, b, :], ident[0:TS, 0:TS]).then_inc(yt, 1)

                    def body(i, b, h, first):
                        pe.wait_ge(b_x[b], 16 * (i + 1))
                        apart(pe)
                        for j in range(2):
                            last = nc.tensor.transpose(BK[0][:, j * TS:(j + 1) * TS], XS[0:TS, b, j, :],
                                                       ident[0:TS, 0:TS])
                        last.then_inc(qt, 1)
                        pe.wait_ge(b_c[b], 16 * (i + 1))
                        for s in range(DB):
                            out = BK[1 + s // 4].rearrange("p (b v) -> p b v", b=4)[:, s % 4, :]
                            last = nc.tensor.transpose(out, CI[:, b, s, :], ident)
                        last.then_inc(ctp, 1)
                        pe.wait_ge(qe, h + 1)
                        pe.wait_ge(wg, h + 1)
                        nc.tensor.matmul(BK[3][0:TS, 0:TS], QT2[:, 1, :], QT2[:, 0, :], start=True, stop=True)
                        nc.tensor.matmul(BK[3][:, 64:64 + DB], XS[0:TS, b, 1, :], WG[0:TS, :], start=True, stop=True)\
                          .then_inc(s_mm, 1)
                        if not first:
                            y_transpose(i - 1 + b, 1 - b)
                        pe.wait_ge(vw, h + 1)
                        pe.wait_ge(cn[1 - b], i + b)
                        for s in range(DB):
                            out = BK[6 + s // 4].rearrange("p (b k) -> p b k", b=4)[:, s % 4, :]
                            last = nc.tensor.matmul(out, VW[0:TS, s, :], XS[0:TS, b, 1, :], start=True, stop=True)
                        last.then_inc(upd, 1)
                        pe.wait_ge(yte, h)
                        pe.wait_ge(at, h + 1)
                        apart(pe)
                        nc.tensor.matmul(BK[4][0:TS, 0:P + 1], AT[0:TS, :], VA[0:TS, b, 0:P + 1], start=True, stop=True)
                        pe.wait_ge(cte, h + 1)
                        pe.wait_ge(qz, h + 1)
                        for s in range(DB):
                            last = nc.tensor.matmul(BK[5][0:TS, 0:P + 1], QZ[:, s * TS:(s + 1) * TS], CT[:, s, 0:P + 1],
                                                    start=(s == 0), stop=(s == DB - 1))
                        last.then_inc(cell, 1)

                    body(0, 0, 0, True)
                    body(0, 1, 1, False)
                    with pe.Fori(1, H // 2) as i:
                        for b in range(2):
                            body(i, b, i * 2 + b, False)
                    y_transpose(H // 2 - 1, 1)
                    pe.wait_ge(yte, H)
                    nc.tensor.transpose(BK[1][0:DB * H, 0:P], nO.rearrange("p b h -> p (b h)"), ident).then_inc(n_tp, 1)

        def out_phase(tag, w_out, first):
            N = 2 * P
            take = area(AREA + 460)
            XR = take(2 * NB, N)
            XN = take(2, D)
            JK = take(2, D)
            GF = None if first else take(D)
            ss, var, rs = take(2), take(2), take(2)
            if not first:
                O, Z, E, Y = XN, JK[:, 0, :], JK[:, 1, :], GF
                SQ = O[:, 1, :]
                SL = take(P)
                oss, ovar, ors = take(H), take(H), take(H)
            by_head = lambda t: t[0:TS, :].rearrange("p (h e) -> p h e", h=H)
            o_ld, o_ez, o_ss, o_rs, o_y, o_t, o_hi, o_lo, och, dch = (
                sem(f"{tag}_o{s}") for s in ("ld", "ez", "ss", "rs", "y", "t", "hi", "lo", "pool", "dve"))
            reg = lambda w, r: w[:, r * KT * N:(r + 1) * KT * N].rearrange("p (k c) -> p k c", k=KT)
            flat = lambda w, r: w[:, r * KT * N:(r + 1) * KT * N]
            w_ld, x_ld, hi, lo, used, done, mm, ev, st = (two(f"{tag}_{s}") for s in
                                                          ("w", "x", "hi", "lo", "used", "done", "mm", "ev", "st"))
            y_hi, y_lo, sq, rr, xs, tp, nh, nl, pch, f_ld = (
                sem(f"{tag}_{s}") for s in ("yhi", "ylo", "sq", "rs", "xn", "tp", "nh", "nl", "pool", "gf"))
            bw, bh = sem(f"{tag}_bw"), sem(f"{tag}_bh")
            ready = slice(0, TOK if first else SEQ)
            size = lambda t: P if t < NT else TS
            whole = lambda t: NB + t + 1

            with nc.Block() as block:
                @block.sync
                def _(sp):
                    def sample_values():
                        for b in range(DB):
                            for part in range(2):
                                src = bass.AP(d_av.tensor, (b * 64 + part * TS) * D, [[D, DS], [DS * D + P, H], [1, P]])
                                sp.dma_start(O[b * DS:(b + 1) * DS, part, :].rearrange("p (h e) -> p h e", h=H), src)\
                                  .then_inc(o_ld, 16)
                        sp.dma_start(Z[0:TS, :], d_smB[:, 3, :]).then_inc(o_ld, 16)
                        sp.dma_start(SL[0:TS, :], subln_b[0, :].partition_broadcast(TS)).then_inc(o_ld, 16)

                    for i in range(2):
                        for r in range(2):
                            cols = bass.ds((i * 2 + r) * N, N)
                            if i:
                                sp.wait_ge(lo[r], i)
                            sp.dma_start(reg(RAW, r), w_out[0, :, cols].rearrange("(k p) c -> p k c", p=P))\
                              .then_inc(w_ld[r], 16)
                            if i:
                                sp.wait_ge(done[r], NB * i)
                            elif r == 0 and not first:
                                sample_values()
                            if first:
                                sp.dma_start(XR[:, r * NB:r * NB + NT, :],
                                             x_prompt[0, :, cols].rearrange("(t p) c -> p t c", p=P)).then_inc(x_ld[r], 16)
                                sp.dma_start(XR[0:TS, r * NB + NT, :],
                                             x_sample[:, :, cols].rearrange("b s c -> (b s) c")).then_inc(x_ld[r], 16)
                            else:
                                sp.dma_start(XR[:, r * NB:r * NB + NT, :],
                                             d_x1[0:SEQ, cols].rearrange("(t p) c -> p t c", p=P)).then_inc(x_ld[r], 16)
                                sp.dma_start(XR[0:TS, r * NB + NT, :], d_x1[SEQ:TOK, cols]).then_inc(x_ld[r], 16)
                    if first:
                        sp.wait_ge(lo[0], 2)
                        load_qk_b(sp, 0, bw)
                    else:
                        sp.wait_ge(o_t, 1)
                        sp.dma_start(GF, final_norm_g.partition_broadcast(P)).then_inc(f_ld, 16)
                    for t in range(NB):
                        n, b = size(t), t % 2
                        if first:
                            sp.wait_ge(done[1], whole(t))
                            sp.dma_start(d_x1[tok(t, n), :], X1[0:n, t, :]).then_inc(st[0], 16)
                        else:
                            sp.wait_ge(xs, t + 1)
                            dst = y_p[0, tok(t, n), :] if t < NT else y_s.rearrange("b s n -> (b s) n")
                            sp.dma_start(dst, XN[0:n, b, :]).then_inc(st[b], 16)
                    if first:
                        sp.wait_ge(st[0], 16 * NB)
                    else:
                        sp.wait_ge(st[0], 16 * (NT // 2 + 1))
                        sp.wait_ge(st[1], 16 * (NT // 2))

                @block.scalar
                def _(act):
                    def cut(i, r):
                        act.wait_ge(w_ld[r], 16 * (i + 1))
                        if i:
                            act.wait_ge(used[r], i)
                        act.activation(flat(WH, r), flat(RAW, r), ACT.Copy).then_inc(hi[r], 1)

                    for k in range(KT):
                        if k == KT // 2:
                            cut(0, 0)
                        act.activation(XH[:, k, ready], YT[:, k, ready], ACT.Copy).then_inc(y_hi, 1)
                    if not first:
                        act.wait_ge(o_ld, 16 * (2 * DB + 2))
                        act.activation(E[0:TS, :], Z[0:TS, :], ACT.Tanh, scale=0.5).then_inc(o_ez, 1)
                    cut(0, 1)
                    if not first:
                        act.wait_ge(o_t, 1)
                        act.activation(XH[:, :, SEQ:TOK], BK[2][:, 0:H * TS].rearrange("p (h t) -> p h t", h=H), ACT.Copy)\
                           .then_inc(o_hi, 1)
                    cut(1, 0)
                    cut(1, 1)

                    def high(t):
                        for half in range(2):
                            act.wait_ge(tp, 2 * t + half + 1)
                            act.activation(XH[:, 4 * half:4 * half + 4, tok(t, size(t))],
                                           BK[2 + 2 * (t % 2) + half].rearrange("p (k t) -> p k t", k=4)[:, :, 0:size(t)],
                                           ACT.Copy).then_inc(nh, 1)

                    for t in range(NB):
                        n, b = size(t), t % 2
                        act.wait_ge(done[1], whole(t))
                        act.activation(JK[0:n, b, :], X1[0:n, t, :], ACT.Square, accum_out=ss[0:n, b:b + 1]).then_inc(sq, 1)
                        if first and t >= 2:
                            high(t - 2)
                        if first and t < KT:
                            if t == 0:
                                act.wait_ge(bw, 32)
                                act.wait_ge(used[0], 2)
                            for j, (_, g) in enumerate(QK_B):
                                cols = slice(j * P, (j + 1) * P)
                                act.activation(qk_weights(WH)[:, t, cols], qk_weights(RAW)[:, t, cols], ACT.Copy,
                                               scale=g[:, t:t + 1]).then_inc(bh, 1)
                    if first:
                        high(NB - 2)
                        high(NB - 1)

                @block.gpsimd
                def _(pool):
                    links = Chain(pool, pch)
                    if not first:
                        pool.wait_ge(o_ss, 1)
                        links.link(nc.gpsimd.tensor_scalar(ovar[0:TS, :], oss[0:TS, :], 1.0 / P, EPS, ALU.mult, ALU.add))
                        nc.gpsimd.tensor_tensor(ors[0:TS, :], ovar[0:TS, :], neg_half[0:TS, :].to_broadcast([TS, H]),
                                                ALU.pow).then_inc(o_rs, 1)
                    for t in range(NB):
                        n, b = size(t), t % 2
                        pool.wait_ge(sq, t + 1)
                        links.link(nc.gpsimd.tensor_scalar(var[0:n, b:b + 1], ss[0:n, b:b + 1], 1.0 / D, EPS,
                                                           ALU.mult, ALU.add))
                        nc.gpsimd.tensor_tensor(rs[0:n, b:b + 1], var[0:n, b:b + 1], neg_half[0:n, :],
                                                ALU.pow).then_inc(rr, 1)

                @block.vector
                def _(dve):
                    v = nc.vector

                    def cut(i, r):
                        dve.wait_ge(hi[r], i + 1)
                        v.tensor_tensor(flat(WL, r), flat(RAW, r), flat(WH, r).bitcast(F32), ALU.subtract)\
                         .then_inc(lo[r], 1)

                    for k in range(KT):
                        if k == KT // 2:
                            cut(0, 0)
                        dve.wait_ge(y_hi, k + 1)
                        v.tensor_tensor(XL[:, k, ready], YT[:, k, ready], XH[:, k, ready].bitcast(F32), ALU.subtract)\
                         .then_inc(y_lo, 1)
                    dve.wait_ge(y_lo, KT)

                    def add(i, r, t):
                        u = NB * r + t
                        n = size(t)
                        dve.wait_ge(mm[u % 2], NB * i + u // 2 + 1)
                        v.tensor_tensor(X1[0:n, t, bass.ds((i * 2 + r) * N, N)], BK[u % 2][0:n, 0:N],
                                        XR[0:n, r * NB + t, :], ALU.add).then_inc(done[r], 1)
                        dve.wait_ge(done[r], NB * i + t + 1)
                        dve.sem_inc(ev[u % 2], 1)

                    links = Chain(dve, dch)

                    def sample_sums():
                        dve.wait_ge(o_ld, 16 * (2 * DB + 2))
                        links.link(v.tensor_tensor(O[0:TS, 0, :], O[0:TS, 0, :], O[0:TS, 1, :], ALU.add))
                        links.link(v.tensor_tensor(SQ[0:TS, :], O[0:TS, 0, :], O[0:TS, 0, :], ALU.mult))
                        v.tensor_reduce(oss[0:TS, :], by_head(SQ), AX, ALU.add).then_inc(o_ss, 1)

                    def sample_gates():
                        dve.wait_ge(o_ez, 1)
                        links.link(v.tensor_scalar(E[0:TS, :], E[0:TS, :], 1.0, None, ALU.add))
                        links.link(v.tensor_tensor(Z[0:TS, :], Z[0:TS, :], E[0:TS, :], ALU.mult))
                        links.link(v.tensor_tensor(by_head(Z), by_head(Z),
                                                   SL[0:TS, :].unsqueeze(1).to_broadcast([TS, H, P]), ALU.mult))

                    def sample_outputs():
                        dve.wait_ge(o_rs, 1)
                        links.link(v.tensor_tensor(by_head(Y), O[0:TS, 0, :].rearrange("p (h e) -> p h e", h=H),
                                                   ors[0:TS, :].unsqueeze(2).to_broadcast([TS, H, P]), ALU.mult))
                        v.scalar_tensor_tensor(Y[0:TS, :], Y[0:TS, :], 0.5 * (1.0 - LAM_INIT), Z[0:TS, :],
                                               ALU.mult, ALU.mult).then_inc(o_y, 1)

                    def sample_low():
                        dve.wait_ge(o_hi, 1)
                        v.tensor_tensor(XL[:, :, SEQ:TOK], BK[2][:, 0:H * TS].rearrange("p (h t) -> p h t", h=H),
                                        XH[:, :, SEQ:TOK].bitcast(F32), ALU.subtract).then_inc(o_lo, 1)

                    def chunk(i, r):
                        dve.wait_ge(x_ld[r], 32 * (i + 1))
                        for t in range(NB):
                            add(i, r, t)
                            if not first and i == r == 0:
                                if t == 0:
                                    sample_sums()
                                if t == 1:
                                    sample_gates()
                                if t == 2:
                                    sample_outputs()
                                if t == 5:
                                    sample_low()
                    cut(0, 1)
                    chunk(0, 0)
                    cut(1, 0)
                    chunk(0, 1)
                    cut(1, 1)
                    chunk(1, 0)

                    def normed(t):
                        n, b = size(t), t % 2
                        dve.wait_ge(rr, t + 1)
                        if first:
                            if t >= 2:
                                dve.wait_ge(tp, 2 * t - 2)
                            v.tensor_scalar(XN[0:n, b, :], X1[0:n, t, :], rs[0:n, b:b + 1], None, ALU.mult).then_inc(xs, 1)
                        else:
                            if t >= 2:
                                dve.wait_ge(st[b], 16 * (t // 2))
                            v.scalar_tensor_tensor(XN[0:n, b, :], X1[0:n, t, :], rs[0:n, b:b + 1], GF[0:n, :],
                                                   ALU.mult, ALU.mult).then_inc(xs, 1)

                    def low(t):
                        for half in range(2):
                            dve.wait_ge(nh, 2 * t + half + 1)
                            cols = (slice(None), slice(4 * half, 4 * half + 4), tok(t, size(t)))
                            src = BK[2 + 2 * (t % 2) + half].rearrange("p (k t) -> p k t", k=4)[:, :, 0:size(t)]
                            v.tensor_tensor(XL[cols], src, XH[cols].bitcast(F32), ALU.subtract).then_inc(nl, 1)

                    dve.wait_ge(x_ld[1], 64)
                    if not first:
                        dve.wait_ge(f_ld, 16)
                    for t in range(NB):
                        add(1, 1, t)
                        if first and t >= 3:
                            low(t - 3)
                        if t >= 1:
                            normed(t - 1)
                        if first and t < KT:
                            for j, (_, g) in enumerate(QK_B):
                                cols = slice(j * P, (j + 1) * P)
                                dve.wait_ge(bh, 2 * t + j + 1)
                                v.scalar_tensor_tensor(qk_weights(WL)[:, t, cols], qk_weights(RAW)[:, t, cols], g[:, t:t + 1],
                                                       qk_weights(WH)[:, t, cols].bitcast(F32), ALU.mult, ALU.subtract)
                    if first:
                        low(NB - 3)
                    normed(NB - 1)
                    if first:
                        low(NB - 2)
                        low(NB - 1)

                @block.tensor
                def _(pe):
                    def project(i, r, t):
                        u = NB * r + t
                        rows = size(t)
                        tt = slice(t * P, t * P + rows)
                        if i or u // 2:
                            pe.wait_ge(ev[u % 2], NB * i + u // 2)
                        n = 0
                        for k in range(KT):
                            if (i, r, t) == (0, 0, 0):
                                pe.wait_ge(y_lo, k + 1)
                            for x, w in ((XH, WH), (XH, WL), (XL, WH)):
                                last = nc.tensor.matmul(BK[u % 2][0:rows, 0:N], x[:, k, tt], reg(w, r)[:, k, :],
                                                        start=(n == 0), stop=(n == 3 * KT - 1))
                                n += 1
                        last.then_inc(mm[u % 2], 1)

                    def turn(t):
                        n, b = size(t), t % 2
                        pe.wait_ge(xs, t + 1)
                        if t >= 2:
                            pe.wait_ge(nl, 2 * t - 2)
                        for k in range(KT):
                            out = BK[2 + 2 * b + k // 4].rearrange("p (k t) -> p k t", k=4)[:, k % 4, 0:n]
                            last = nc.tensor.transpose(out, XN[0:n, b, k * P:(k + 1) * P], ident[0:n, 0:n])
                            if k % 4 == 3:
                                last.then_inc(tp, 1)

                    for i in range(2):
                        for r in range(2):
                            pe.wait_ge(hi[r], i + 1)
                            pe.wait_ge(lo[r], i + 1)
                            for t in range(NB):
                                if not first and (i, r, t) == (0, 0, NT):
                                    pe.wait_ge(o_lo, 1)
                                project(i, r, t)
                                if not first and (i, r, t) == (0, 0, 4):
                                    pe.wait_ge(o_y, 1)
                                    for h in range(H):
                                        x = nc.tensor.transpose(BK[2][:, h * TS:(h + 1) * TS], Y[0:TS, h * P:(h + 1) * P],
                                                                ident[0:TS, 0:TS])
                                    x.then_inc(o_t, 1)
                                if first and i and r and t >= 2:
                                    turn(t - 2)
                            pe.wait_ge(mm[(NB * r + NB - 1) % 2], NB * i + (NB * r + NB - 1) // 2 + 1)
                            pe.sem_inc(used[r], 1)
                    if first:
                        turn(NB - 2)
                        turn(NB - 1)

        def attention_phase():
            take = area(AREA - 2 * SEQ)
            QKR = take(2, 2, P)
            RA, RB = take(8, HALF), take(8, HALF)
            V = take(NT, P)
            PR = take(2, SEQ)
            WT = take(NT, P)
            EZ, ZC, GZ = take(2, P), take(2, P), take(2, P)
            Y, JK = take(2, P), take(2, P)
            SM = take(4, P)
            SL = take(P)
            LQ = take(4, DK)
            le, nl = take(2), LAM[:, :]
            mx, nm, sm, rc, ssq, var, rs, rr2 = (take(2) for _ in range(8))
            cf = take(1)
            KR = RAW[:, 4 * KT * P:5 * KT * P].rearrange("p (t c) -> p t c", t=NT)
            QTR = phase_tensor("QTR", [P, 2, SEQ], F32R)
            QTH, QTL = QTR[:, 0, :], QTR[:, 1, :]
            KTH = WH[:, 4 * KT * P:5 * KT * P]
            KTL = WL[:, 4 * KT * P:5 * KT * P]
            N = 2 * P
            reg = lambda w, r: w[:, r * KT * N:(r + 1) * KT * N].rearrange("p (k c) -> p k c", k=KT)
            c_k, c_w, c_sst, c_kst, c_vst = sem("c_k"), two("c_w"), sem("c_sst"), sem("c_kst"), sem("c_vst")
            hi, lo = two("c_hi"), two("c_lo")
            lamS, lamE, lamD = sem("c_lam"), sem("c_lame"), sem("c_lamd")
            pj, rope, kr, kth, vz, sc, mxs, ex, ww, av, ot, otf, sq, rr, sg, gz, yy, smd = (
                sem(f"c_{s}") for s in ("pj", "rope", "kr", "kth", "vz", "sc", "mx", "ex", "w", "av",
                                        "ot", "otf", "sq", "rr", "sg", "gz", "y", "sm"))
            tr, trf, wt, wte = two("c_tr"), two("c_trf"), two("c_wt"), two("c_wte")
            dch, pch = sem("c_dve"), sem("c_pool")
            B_V, B_O = BK[0], BK[1]
            S = [PD[c][:, :, :].rearrange("p a n -> p (a n)") for c in range(2)]
            PARTS = [[(w_in_b[0, :, :], 0, gB), (w_kv, 0, gKV)], [(w_kv, D, gKV), (w_in_b[0, :, :], D, gB)]]

            def heads(eng, sweep1, sweep2, tail, links=None, per=0):
                sweep1(0, None)
                with eng.Fori(0, H - 1) as h:
                    if links:
                        links.enter(h, per)
                    sweep2(h, False)
                    sweep1(h + 1, h)
                if links:
                    links.leave(H - 1)
                sweep2(H - 1, True)
                tail(H - 1)

            with nc.Block() as block:
                @block.sync
                def _(sp):
                    def load(r, h):
                        for j, (w, base, _) in enumerate(PARTS[r]):
                            sp.dma_start(reg(RAW, r)[:, :, j * P:(j + 1) * P],
                                         w[:, bass.ds(base + h * P, P)].rearrange("(k p) c -> p k c", p=P))\
                              .then_inc(c_w[r], 16)

                    load(1, 0)
                    for j, w in enumerate((lam_q1, lam_k1, lam_q2, lam_k2)):
                        sp.dma_start(LQ[:, j, :], w[0, :].partition_broadcast(P)).then_inc(c_k, 16)
                    sp.dma_start(SL, subln_b[0, :].partition_broadcast(P)).then_inc(c_k, 16)

                    def body(h, last):
                        if not last:
                            sp.wait_ge(lo[0], 2 * KT * h)
                            load_qk_b(sp, h + 1, c_w[0])
                        sp.wait_ge(kr, NT * (h + 1))
                        sp.dma_start(k_p[0, :, bass.ds(h, 1), :, :].rearrange("(t p) a c d -> p t (a c d)", p=P), KR)\
                          .then_inc(c_kst, 16)
                        if not last:
                            sp.wait_ge(lo[1], 2 * KT * (h + 1))
                            load(1, h + 1)
                        sp.wait_ge(vz, NT * (h + 1))
                        sp.dma_start(v_p[0, :, bass.ds(h, 1), :].rearrange("(t p) a e -> p t (a e)", p=P), V)\
                          .then_inc(c_vst, 16)
                        sp.wait_ge(smd, h + 1)
                        sp.dma_start(d_smB[:, :, bass.ds(h * P, P)], SM[0:TS, :, :]).then_inc(c_sst, 16)
                        sp.dma_start(k_s[:, :, bass.ds(h, 1), :, :].rearrange("b s a c d -> (b s) (a c d)"), SM[0:TS, 1, :])\
                          .then_inc(c_sst, 16)
                        sp.dma_start(v_s[:, :, bass.ds(h, 1), :].rearrange("b s a e -> (b s) (a e)"), SM[0:TS, 2, :])\
                          .then_inc(c_sst, 16)
                    with sp.Fori(0, H - 1) as h:
                        body(h, False)
                    body(H - 1, True)
                    sp.wait_ge(c_kst, 16 * H)
                    sp.wait_ge(c_vst, 16 * H)
                    sp.wait_ge(c_sst, 48 * H)

                @block.scalar
                def _(act):
                    def cut(r, k):
                        for j, (_, _, g) in enumerate(PARTS[r]):
                            cols = slice(j * P, (j + 1) * P)
                            act.activation(reg(WH, r)[:, k, cols], reg(RAW, r)[:, k, cols], ACT.Copy,
                                           scale=g[:, k:k + 1]).then_inc(hi[r], 1)

                    act.wait_ge(lamS, 1)
                    act.activation(le, mx, ACT.Exp).then_inc(lamE, 1)

                    def values(h, t):
                        act.wait_ge(pj, 2 * NB * h + NB + t + 1)
                        if t < NT:
                            if t == 0:
                                act.wait_ge(c_vst, 16 * h)
                            act.wait_ge(gz, NT * h + max(t - 1, 0))
                            act.activation(V[:, t, :], B_V[:, 0:P], ACT.Copy)
                            act.activation(EZ[:, t % 2, :], B_V[:, P:2 * P], ACT.Tanh, scale=0.5)
                            act.activation(ZC[:, t % 2, :], B_V[:, P:2 * P], ACT.Copy).then_inc(vz, 1)
                        else:
                            act.activation(SM[0:TS, 2:4, :], B_V[0:TS, 0:2 * P].rearrange("p (a c) -> p a c", a=2),
                                           ACT.Copy).then_inc(smd, 1)

                    def squares(h, c):
                        act.wait_ge(av, NT * h + c + 1)
                        act.activation(JK[:, c % 2, :], B_O[:, 0:P], ACT.Square, scale=rc[:, c % 2:c % 2 + 1],
                                       accum_out=ssq[:, c % 2:c % 2 + 1]).then_inc(sq, 1)

                    def weights(h, c):
                        n = min(c + 1, 4)
                        act.wait_ge(wt[0], NT * h + c + 1)
                        act.activation(WT[:, 0:n, :], BK[2][:, 0:n * P].rearrange("p (a c) -> p a c", a=n),
                                       ACT.Copy).then_inc(wte[0], 1)

                    def sweep1(h, before):
                        act.wait_ge(c_w[1], 32 * (h + 1))
                        act.wait_ge(pj, 2 * NB * h)
                        for t in range(NB):
                            if t < KT:
                                cut(1, t)
                            if t == 0 and before is not None:
                                weights(before, NT - 1)
                            if t == 1 and before is not None:
                                squares(before, NT - 1)
                            if t >= 1:
                                c = t - 1
                                act.wait_ge(tr[c % 2], 4 * h + c // 2 + 1)
                                act.activation(QTH[:, c * P:(c + 1) * P], BK[2 + c % 2][:, 0:P], ACT.Copy)
                                act.activation(KTH[:, c * P:(c + 1) * P], BK[2 + c % 2][:, P:2 * P], ACT.Copy)\
                                   .then_inc(kth, 1)

                    def sweep2(h, last):
                        if not last:
                            act.wait_ge(c_w[0], 32 * (h + 1))
                        for t in range(NB):
                            values(h, t)
                            if 1 <= t < NT:
                                weights(h, t - 1)
                            if t < NT:
                                if t > 4:
                                    act.wait_ge(wt[1], 4 * h + (t - 4))
                                for c in range(2):
                                    act.wait_ge(mxs, 2 * (NT * h + t) + c + 1)
                                    act.wait_ge(ww, NT * h + t)
                                    act.activation(PR[:, c, 0:(t + 1) * P], S[c][:, 0:(t + 1) * P], ACT.Exp,
                                                   scale=ATTN_SCALE, bias=nm[:, c:c + 1],
                                                   accum_out=sm[:, c:c + 1]).then_inc(ex, 1)
                                if not last:
                                    cut(0, t)
                            if 1 <= t < NT:
                                squares(h, t - 1)

                    def tail(h):
                        weights(h, NT - 1)
                        squares(h, NT - 1)
                    heads(act, sweep1, sweep2, tail)

                @block.gpsimd
                def _(pool):
                    g = nc.gpsimd
                    links = Chain(pool, pch)
                    pool.wait_ge(lamD, 1)

                    def root(h, c):
                        b = c % 2
                        pool.wait_ge(sq, NT * h + c + 1)
                        apart(pool)
                        links.link(g.tensor_scalar(var[:, b:b + 1], ssq[:, b:b + 1], 1.0 / P, EPS, ALU.mult, ALU.add))
                        links.link(g.tensor_tensor(rs[:, b:b + 1], var[:, b:b + 1], neg_half, ALU.pow))
                        g.tensor_tensor(rr2[:, b:b + 1], rs[:, b:b + 1], rc[:, b:b + 1], ALU.mult).then_inc(rr, 1)

                    def sweep1(h, before):
                        pool.wait_ge(c_kst, 16 * h)
                        for t in range(NT):
                            pool.wait_ge(rope, NB * h + t + 1)
                            apart(pool)
                            g.tensor_copy(KR[:, t, :], QKR[:, t % 2, 1, :]).then_inc(kr, 1)
                            if t == 0 and before is not None:
                                root(before, NT - 1)

                    def sweep2(h, last):
                        for t in range(NB):
                            if 1 <= t < NT:
                                b = (t - 1) % 2
                                pool.wait_ge(sg, NT * h + t)
                                links.link(g.tensor_tensor(GZ[:, b, :], ZC[:, b, :], EZ[:, b, :], ALU.mult))
                                g.tensor_tensor(GZ[:, b, :], GZ[:, b, :], SL, ALU.mult).then_inc(gz, 1)
                                root(h, t - 1)
                        pool.wait_ge(sg, NT * h + NT)
                        b = (NT - 1) % 2
                        links.link(g.tensor_tensor(GZ[:, b, :], ZC[:, b, :], EZ[:, b, :], ALU.mult))
                        g.tensor_tensor(GZ[:, b, :], GZ[:, b, :], SL, ALU.mult).then_inc(gz, 1)
                    heads(pool, sweep1, sweep2, lambda h: root(h, NT - 1), links, 24)

                @block.vector
                def _(dve):
                    v = nc.vector
                    links = Chain(dve, dch)

                    def cut(r, k, h):
                        for j, (_, _, g) in enumerate(PARTS[r]):
                            cols = slice(j * P, (j + 1) * P)
                            dve.wait_ge(hi[r], 2 * (KT * h + k) + j + 1)
                            v.scalar_tensor_tensor(reg(WL, r)[:, k, cols], reg(RAW, r)[:, k, cols], g[:, k:k + 1],
                                                   reg(WH, r)[:, k, cols].bitcast(F32), ALU.mult, ALU.subtract)\
                             .then_inc(lo[r], 1)

                    dve.wait_ge(c_k, 80)
                    v.tensor_scalar(SL, SL, 0.5 * (1.0 - LAM_INIT), None, ALU.mult)
                    v.tensor_tensor(LQ[:, 0, :], LQ[:, 0, :], LQ[:, 1, :], ALU.mult)
                    links.link(v.tensor_tensor(LQ[:, 2, :], LQ[:, 2, :], LQ[:, 3, :], ALU.mult))
                    v.tensor_reduce(mx[:, 0:1], LQ[:, 0, :], AX, ALU.add)
                    v.tensor_reduce(mx[:, 1:2], LQ[:, 2, :], AX, ALU.add).then_inc(lamS, 1)
                    dve.wait_ge(lamE, 1)
                    links.link(v.tensor_tensor(nl, le[:, 1:2], le[:, 0:1], ALU.subtract))
                    v.tensor_scalar(nl, nl, LAM_INIT, None, ALU.subtract).then_inc(lamD, 1)
                    dve.wait_ge(lamD, 1)

                    def rotate(h, t):
                        n = P if t < NT else TS
                        dve.wait_ge(pj, 2 * NB * h + t + 1)
                        src = BK[4 + t % 2][0:n, 0:N].rearrange("p (g c) -> p g c", c=HALF)
                        cos = cst[0:n, C_COS + t * HALF:C_COS + (t + 1) * HALF]
                        sin = cst[0:n, C_SIN + t * HALF:C_SIN + (t + 1) * HALF].unsqueeze(1).to_broadcast([n, 4, HALF])
                        v.tensor_tensor(RA[0:n, :, :], src, cos.unsqueeze(1).to_broadcast([n, 8, HALF]), ALU.mult)
                        v.tensor_tensor(RB[0:n, 0:8:2, :], src[:, 1:8:2, :], sin, ALU.mult)
                        links.link(v.tensor_tensor(RB[0:n, 1:8:2, :], src[:, 0:8:2, :], sin, ALU.mult))
                        if t < NT:
                            dve.wait_ge(tr[t % 2], 4 * h + t // 2)
                            dve.wait_ge(kr, NT * h + max(t - 1, 0))
                            dst = QKR[:, t % 2, :, :]
                        else:
                            dve.wait_ge(c_sst, 48 * h)
                            dst = SM[0:n, 0:2, :]
                        dst = dst.rearrange("p a (g c) -> p (a g) c", c=HALF)
                        v.tensor_tensor(dst[:, 0:8:2, :], RA[0:n, 0:8:2, :], RB[0:n, 0:8:2, :], ALU.subtract)
                        v.tensor_tensor(dst[:, 1:8:2, :], RA[0:n, 1:8:2, :], RB[0:n, 1:8:2, :], ALU.add)\
                         .then_inc(rope, 1)
                        dve.wait_ge(rope, NB * h + t + 1)

                    def o_transposed(h, c):
                        dve.wait_ge(ot, NT * h + c + 1)
                        v.tensor_copy(YT[:, bass.ds(h, 1), c * P:(c + 1) * P].rearrange("p a c -> p (a c)"),
                                      B_O[:, P:2 * P]).then_inc(otf, 1)

                    def output(h, c):
                        b = c % 2
                        dve.wait_ge(rr, NT * h + c + 1)
                        dve.wait_ge(gz, NT * h + c + 1)
                        v.scalar_tensor_tensor(Y[:, b, :], B_O[:, 0:P], rr2[:, b:b + 1], GZ[:, b, :],
                                               ALU.mult, ALU.mult).then_inc(yy, 1)

                    def weights(h, c):
                        m = c - 3
                        dve.wait_ge(wt[1], 4 * h + m)
                        v.tensor_copy(WT[:, 4:4 + m, :], BK[3][:, 0:m * P].rearrange("p (a c) -> p a c", a=m))\
                         .then_inc(wte[1], 1)

                    def sweep1(h, before):
                        for t in range(NB):
                            rotate(h, t)
                            if t < KT:
                                cut(1, t, h)
                            if before is not None:
                                if t == 0:
                                    weights(before, NT - 1)
                                if t == 1:
                                    output(before, NT - 1)
                                    o_transposed(before, NT - 2)
                                if t == 2:
                                    o_transposed(before, NT - 1)
                            if t >= 1:
                                c = t - 1
                                dve.wait_ge(kth, NT * h + c + 1)
                                tt = slice(c * P, (c + 1) * P)
                                v.tensor_tensor(QTL[:, tt], BK[2 + c % 2][:, 0:P], QTH[:, tt].bitcast(F32), ALU.subtract)
                                v.tensor_tensor(KTL[:, tt], BK[2 + c % 2][:, P:2 * P], KTH[:, tt].bitcast(F32),
                                                ALU.subtract).then_inc(trf[c % 2], 1)

                    def sigmoid(h, t):
                        b = t % 2
                        dve.wait_ge(vz, NT * h + t + 1)
                        v.tensor_scalar(EZ[:, b, :], EZ[:, b, :], 1.0, None, ALU.add).then_inc(sg, 1)

                    def sweep2(h, last):
                        for t in range(NB):
                            n = (t + 1) * P
                            if t < NT:
                                for c in range(2):
                                    if c == 1 and t > 4:
                                        weights(h, t - 1)
                                    if c == 1 and t >= 2:
                                        output(h, t - 2)
                                    dve.wait_ge(sc, 2 * (NT * h + t) + c + 1)
                                    links.link(v.tensor_tensor(S[c][:, n - P:n], S[c][:, n - P:n],
                                                               cst[:, C_MB:C_MB + P], ALU.add))
                                    links.link(v.tensor_reduce(mx[:, c:c + 1], S[c][:, 0:n], AX, ALU.max, negate=True))
                                    v.tensor_scalar(nm[:, c:c + 1], mx[:, c:c + 1], ATTN_SCALE, None, ALU.mult)\
                                     .then_inc(mxs, 1)
                            if t == NT:
                                output(h, t - 2)
                            if t >= 3:
                                o_transposed(h, t - 3)
                            if t >= 1:
                                sigmoid(h, t - 1)
                            if t < NT:
                                if not last:
                                    cut(0, t, h)
                                b = t % 2
                                dve.wait_ge(ex, 2 * (NT * h + t) + 2)
                                links.link(v.reciprocal(cf, sm[:, 1:2]))
                                links.link(v.scalar_tensor_tensor(cf, sm[:, 0:1], nl, cf, ALU.mult, ALU.mult))
                                v.reciprocal(rc[:, b:b + 1], sm[:, 0:1])
                                v.scalar_tensor_tensor(PR[:, 0, 0:n], PR[:, 1, 0:n], cf, PR[:, 0, 0:n],
                                                       ALU.mult, ALU.add).then_inc(ww, 1)
                                dve.wait_ge(ww, NT * h + t + 1)

                    def tail(h):
                        weights(h, NT - 1)
                        output(h, NT - 1)
                        o_transposed(h, NT - 2)
                        o_transposed(h, NT - 1)
                    heads(dve, sweep1, sweep2, tail, links, 9 + 8 * 2 * 2 + 16)

                @block.tensor
                def _(pe):
                    def project(r, t, bank):
                        rows = P if t < NT else TS
                        tt = slice(t * P, t * P + rows)
                        i = 0
                        for k in range(KT):
                            for x, w in ((XH, WH), (XH, WL), (XL, WH)):
                                last = nc.tensor.matmul(bank[0:rows, 0:N], x[:, k, tt], reg(w, r)[:, k, :],
                                                        start=(i == 0), stop=(i == 3 * KT - 1))
                                i += 1
                        last.then_inc(pj, 1)

                    def scores(h, t):
                        width = (t // 2 + 1) * 2 * P
                        for c in range(2):
                            pe.wait_ge(ex, 2 * NT * h + max(2 * t - 1 + c, 0))
                            rows = slice(DK * c, DK * c + DK)
                            for at in range(0, width, 512):
                                kk = slice(at, min(at + 512, width))
                                i = 0
                                for q, k in ((QTH, KTH), (QTH, KTL), (QTL, KTH)):
                                    x = nc.tensor.matmul(S[c][:, kk], q[rows, t * P:(t + 1) * P], k[rows, kk],
                                                         start=(i == 0), stop=(i == 2))
                                    i += 1
                            x.then_inc(sc, 1)

                    def turn_weights(h, c):
                        pe.wait_ge(ww, NT * h + c + 1)
                        for g in range(c // 4 + 1):
                            pe.wait_ge(wte[g], NT * h + c) if g == 0 else pe.wait_ge(wte[1], 4 * h + (c - 4))
                            for kb in range(4 * g, min(c + 1, 4 * g + 4)):
                                x = nc.tensor.transpose(BK[2 + g][:, (kb % 4) * P:(kb % 4 + 1) * P],
                                                        PR[:, 0, kb * P:(kb + 1) * P], ident)
                            x.then_inc(wt[g], 1)

                    def weigh(h, c):
                        pe.wait_ge(yy, NT * h + c)
                        pe.wait_ge(wte[0], NT * h + c + 1)
                        if c >= 4:
                            pe.wait_ge(wte[1], 4 * h + (c - 3))
                        pe.wait_ge(vz, NT * h + c + 1)
                        for kb in range(c + 1):
                            x = nc.tensor.matmul(B_O[:, 0:P], WT[:, kb, :], V[:, kb, :],
                                                 start=(kb == 0), stop=(kb == c))
                        x.then_inc(av, 1)

                    def turn_output(h, c):
                        pe.wait_ge(yy, NT * h + c + 1)
                        pe.wait_ge(otf, NT * h + c)
                        nc.tensor.transpose(B_O[:, P:2 * P], Y[:, c % 2, :], ident).then_inc(ot, 1)

                    def sweep1(h, before):
                        pe.wait_ge(hi[0], 2 * KT * h)
                        pe.wait_ge(lo[0], 2 * KT * h)
                        pe.wait_ge(ex, 2 * NT * h)
                        for t in range(NB):
                            pe.wait_ge(rope, NB * h + max(t - 1, 0))
                            project(0, t, BK[4 + t % 2])
                            if before is not None:
                                if t == 0:
                                    turn_weights(before, NT - 1)
                                if t == 1:
                                    turn_output(before, NT - 2)
                                    weigh(before, NT - 1)
                                if t == 2:
                                    turn_output(before, NT - 1)
                            if t >= 1:
                                b = (t - 1) % 2
                                pe.wait_ge(rope, NB * h + t)
                                pe.wait_ge(trf[b], 4 * h + (t - 1) // 2)
                                for j in range(2):
                                    x = nc.tensor.transpose(BK[2 + b][:, j * P:(j + 1) * P], QKR[:, b, j, :], ident)
                                x.then_inc(tr[b], 1)

                    def sweep2(h, last):
                        def project_values(t):
                            pe.wait_ge(vz, NT * h + t)
                            pe.wait_ge(smd, h)
                            project(1, t, B_V)

                        pe.wait_ge(hi[1], 2 * KT * (h + 1))
                        pe.wait_ge(lo[1], 2 * KT * (h + 1))
                        project_values(0)
                        for b in range(2):
                            pe.wait_ge(trf[b], 4 * (h + 1))
                        pe.wait_ge(rope, NB * (h + 1))
                        scores(h, 0)
                        project_values(1)
                        for t in range(1, NT):
                            scores(h, t)
                            turn_weights(h, t - 1)
                            project_values(t + 1)
                            if t >= 2:
                                turn_output(h, t - 2)
                            weigh(h, t - 1)

                    def tail(h):
                        turn_weights(h, NT - 1)
                        turn_output(h, NT - 2)
                        weigh(h, NT - 1)
                        turn_output(h, NT - 1)
                    heads(pe, sweep1, sweep2, tail)

        def decode_phase():
            take = area(AREA - 3 * P * NT // 2 - 2 * TS)
            G = 2 * P
            NEW = PAGES * P
            ROWS = H * 2 * DS
            KB = RAW[:, 0:4 * D].rearrange("p (s n) -> p s n", s=4)
            VB = take(4, D)
            SR, SX = take(TOK), take(TOK)
            AVS = take(D)
            QS = take(H, TS)
            WS = take(NB * TS)
            sgn, mx, nm, sm, rc, cf = (take(1) for _ in range(6))
            QZ = WH[:, 0:H * 136]
            WTS = WH[:, 1088:1088 + NB * 64].rearrange("p (a c) -> p a c", a=NB)
            VH2 = phase_tensor("VH2", [P, 2, D], F32R)
            VH = [WH[:, 1664 + s * D:1664 + (s + 1) * D] for s in range(2)] + [VH2[:, s, :] for s in range(2)]
            VL = [WL[:, s * D:(s + 1) * D] for s in (0, 1, 3, 4)]
            VHN, VLN = WH[:, 1664 + 2 * D:1664 + 3 * D], WL[:, 2 * D:3 * D]
            d_pt, d_in, d_avs = sem("d_pt"), sem("d_in"), sem("d_avs")
            k_ld = [sem(f"d_k{s}") for s in range(4)]
            v_ld = [sem(f"d_v{s}") for s in range(4)]
            ini, pre, pre2, tp, kh, kl, sc, slo, add, mxs, exd, wd, wtp, wr, whi, wlo, vh, vl, vlp, av, avd, avc, qh, ql, vn = (
                sem(f"d_{s}") for s in ("ini", "pre", "pre2", "tp", "kh", "kl", "sc", "slo", "add", "mx", "ex", "w", "wtp",
                                        "wr", "whi", "wlo", "vh", "vl", "vlp", "av", "avd", "avc", "qh", "ql", "vn"))
            dch = sem("d_dve")
            S_AT = [(BK[2], 0, G), (BK[2], G, G), (BK[3], 0, G), (BK[6], 0, G + TS)]
            S_RD = [(BK[2], 2 * G, 0), (BK[3], G, 2 * G), (BK[6], G + TS, 3 * G)]
            OUT = PD[0]

            ORDER = ("Q", "K0", "E", "K1", "K2", "K3", "V0", "W", "K4", "V1", "R0", "V2", "K5", "V3", "K6", "V4",
                     "R1", "V5", "V6", "K7", "V7", "L")
            PE_ORDER = ("T0", "T1", "T2", "T3", "S0", "T4", "W", "S1", "T5", "V0", "V1", "V2", "T6", "S2", "V3", "T7",
                        "V4", "V5", "V6", "S3", "V7", "N")

            def sequences(eng, body, links=None, per=0):
                body(0, True, False)
                with eng.Fori(1, DB) as b:
                    if links:
                        links.enter(b - 1, per)
                    body(b, True, True)
                if links:
                    links.leave(DB - 1)
                body(DB, False, True)

            def wait(eng, s, count):
                if not isinstance(count, int) or count > 0:
                    eng.wait_ge(s, count)

            def page(eng, index):
                return bass.ds(eng.value_load(PT[0:1, bass.ds(index, 1)], min_val=0, max_val=cache_k.shape[0] - 1), 1)

            with nc.Block() as block:
                @block.sync
                def _(sp):
                    sp.dma_start(PT[:, :], page_table.rearrange("b n -> (b n)").unsqueeze(0)).then_inc(d_pt, 16)
                    for j, dst in enumerate((RAW[0:TS, 4 * D - D:4 * D], RAW[0:TS, 4 * D:5 * D], AVS[0:TS, :])):
                        sp.dma_start(dst, d_smB[:, j, :]).then_inc(d_in, 16)
                    sp.wait_ge(d_pt, 16)
                    sp.wait_ge(pre, 1)

                    def keys(b, p):
                        wait(sp, tp, 2 * PAGES * b + 2 * (p - 3))
                        src = cache_k[page(sp, b * PAGES + p), :, :, :, :]
                        sp.dma_start(KB[:, p % 4, :], src.rearrange("a p h c d -> (a p) (h c d)"))\
                          .then_inc(k_ld[p % 4], 16)

                    def values(i, p, following=True):
                        if p % 4 == 3:
                            wait(sp, vlp, 2 * i + p // 4)
                        elif p >= 4:
                            sp.wait_ge(vl, 6 * i + (p - 3))
                        elif following:
                            sp.wait_ge(vl, 6 * i - (2 - p))
                        src = cache_v[page(sp, i * PAGES + p), :, :, :]
                        sp.dma_start(VB[:, p % 4, :], src.rearrange("a p h e -> (a p) (h e)"))\
                          .then_inc(v_ld[p % 4], 16)

                    def store(i):
                        sp.wait_ge(avc, i + 1)
                        sp.dma_start(d_av[bass.ds(i, 1), :, :].rearrange("a r n -> (a r) n"), AVS[0:64, :])\
                          .then_inc(d_avs, 16)

                    for p in range(PAGES):
                        keys(0, p)
                    for p in range(4):
                        keys(1, p)
                        values(0, p, False)
                    with sp.Fori(1, DB - 1) as b:
                        for p in range(4, PAGES):
                            keys(b, p)
                        for p in range(4, PAGES):
                            values(b - 1, p)
                        for p in range(4):
                            keys(b + 1, p)
                        for p in range(4):
                            values(b, p)
                        store(b - 1)
                    for p in range(4, PAGES):
                        keys(DB - 1, p)
                    for p in range(4, PAGES):
                        values(DB - 2, p)
                    for p in range(4):
                        values(DB - 1, p)
                    store(DB - 2)
                    for p in range(4, PAGES):
                        values(DB - 1, p)
                    store(DB - 1)
                    sp.wait_ge(d_avs, 16 * DB)

                @block.gpsimd
                def _(pool):
                    with pool.Fori(0, DB) as i:
                        for p in (3, 7):
                            pool.wait_ge(vh, PAGES * i + p + 1)
                            nc.gpsimd.tensor_tensor(VL[p % 4], VB[:, p % 4, :], VH[p % 4].bitcast(F32), ALU.subtract)\
                              .then_inc(vlp, 1)

                @block.scalar
                def _(act):
                    act.wait_ge(d_in, 48)
                    act.wait_ge(pre, 1)
                    act.activation(QS, BK[2][:, 0:H * TS].rearrange("p (h t) -> p h t", h=H), ACT.Copy)
                    act.activation(XH[:, :, NEW:TOK], BK[2][:, H * TS:2 * H * TS].rearrange("p (h t) -> p h t", h=H),
                                   ACT.Copy).then_inc(pre2, 1)
                    act.activation(VHN[0:TS, :], AVS[0:TS, :], ACT.Copy).then_inc(vn, 1)
                    act.wait_ge(pre2, 1)
                    act.wait_ge(ini, 2)

                    def body(b, keys, values):
                        i = b - 1

                        def k_high(p):
                            for j in range(2):
                                act.wait_ge(tp, 2 * PAGES * b + 2 * p + j + 1)
                                act.activation(XH[:, 4 * j:4 * j + 4, p * P:(p + 1) * P],
                                               BK[j].rearrange("p (h t) -> p h t", h=4), ACT.Copy).then_inc(kh, 1)

                        def v_high(p):
                            act.wait_ge(v_ld[p % 4], 16 * (2 * i + p // 4 + 1))
                            wait(act, av, PAGES * i + max(p - 3, 0))
                            act.activation(VH[p % 4], VB[:, p % 4, :], ACT.Copy).then_inc(vh, 1)

                        def low_rows(s, r):
                            bank, n, at = S_RD[r]
                            act.wait_ge(sc, 4 * s + (2, 3, 4)[r])
                            act.activation(SX[0:64, at:at + n], bank[64:128, 0:n], ACT.Copy).then_inc(slo, 1)

                        def queries():
                            wait(act, sc, 4 * b)
                            for c in range(2):
                                rows = slice(DK * c, DK * c + DK)
                                dst = QZ.rearrange("p (h r) -> p h r", r=136)[rows, :, DS * c:DS * c + DS]
                                act.activation(dst, QS[rows, :, bass.ds(b * DS, DS)], ACT.Copy).then_inc(qh, 1)

                        def exponentials():
                            act.wait_ge(mxs, i + 1)
                            act.activation(SR[0:64, :], SR[0:64, :], ACT.Exp, scale=ATTN_SCALE, bias=nm[0:64, :],
                                           accum_out=sm[0:64, :]).then_inc(exd, 1)

                        def weights_high():
                            act.wait_ge(wr, i + 1)
                            ws = WS.rearrange("p (a c) -> p a c", a=NB)
                            act.activation(WTS[:, 0:PAGES, 0:TS], ws[:, 0:PAGES, :], ACT.Copy)
                            act.activation(WTS[0:TS, PAGES, 0:TS], ws[0:TS, PAGES, :], ACT.Copy).then_inc(whi, 1)

                        for step in ORDER:
                            if step[0] == "K" and keys:
                                k_high(int(step[1]))
                            elif step[0] == "R" and keys:
                                low_rows(b, int(step[1]))
                            elif step == "L" and keys:
                                low_rows(b, 2)
                            elif step == "Q" and keys:
                                queries()
                            elif step == "E" and values:
                                exponentials()
                            elif step == "W" and values:
                                weights_high()
                            elif step[0] == "V" and values:
                                v_high(int(step[1]))
                        if values:
                            act.wait_ge(avd, i + 1)
                            wait(act, d_avs, 16 * i)
                            for j in range(2):
                                last = act.activation(AVS[0:64, 512 * j:512 * j + 512], OUT[0:64, j, :], ACT.Copy)
                            last.then_inc(avc, 1)
                    sequences(act, body)

                @block.vector
                def _(dve):
                    v = nc.vector
                    links = Chain(dve, dch)
                    v.memset(QZ.bitcast(F32), 0.0).then_inc(ini, 1)
                    links.link(v.tensor_scalar(sgn[0:64, :], LAM[0:64, :], 1.0, None, ALU.subtract))
                    v.tensor_scalar(sgn[0:64, :], sgn[0:64, :], cst[0:64, C_C1:C_C1 + 1], 1.0, ALU.mult, ALU.add)\
                     .then_inc(ini, 1)
                    dve.wait_ge(ini, 2)
                    dve.wait_ge(pre2, 1)
                    v.tensor_tensor(XL[:, :, NEW:TOK], BK[2][:, H * TS:2 * H * TS].rearrange("p (h t) -> p h t", h=H),
                                    XH[:, :, NEW:TOK].bitcast(F32), ALU.subtract).then_inc(vn, 1)
                    dve.wait_ge(vn, 2)
                    v.tensor_tensor(VLN[0:TS, :], AVS[0:TS, :], VHN[0:TS, :].bitcast(F32), ALU.subtract).then_inc(vn, 1)

                    def body(b, keys, values):
                        i = b - 1

                        def k_low(p):
                            for j in range(2):
                                dve.wait_ge(kh, 2 * PAGES * b + 2 * p + j + 1)
                                cols = (slice(None), slice(4 * j, 4 * j + 4), slice(p * P, (p + 1) * P))
                                v.tensor_tensor(XL[cols], BK[j].rearrange("p (h t) -> p h t", h=4),
                                                XH[cols].bitcast(F32), ALU.subtract).then_inc(kl, 1)

                        def v_low(p):
                            dve.wait_ge(vh, PAGES * i + p + 1)
                            v.tensor_tensor(VL[p % 4], VB[:, p % 4, :], VH[p % 4].bitcast(F32),
                                            ALU.subtract).then_inc(vl, 1)

                        def add_rows(s, r):
                            bank, n, at = S_RD[r]
                            dve.wait_ge(slo, 3 * s + r + 1)
                            v.tensor_tensor(SR[0:64, at:at + n], bank[0:64, 0:n], SX[0:64, at:at + n], ALU.add)\
                             .then_inc(add, 1)

                        def maximum():
                            add_rows(b, 2)
                            dve.wait_ge(add, 3 * (b + 1))
                            mask = cst[0:64, bass.ds(C_NEW + b * TS, TS)]
                            links.link(v.tensor_tensor(SR[0:64, NEW:TOK], SR[0:64, NEW:TOK], mask, ALU.add))
                            links.link(v.tensor_reduce(mx[0:64, :], SR[0:64, :], AX, ALU.max, negate=True))
                            v.tensor_scalar(nm[0:64, :], mx[0:64, :], ATTN_SCALE, None, ALU.mult).then_inc(mxs, 1)

                        def queries():
                            for c in range(2):
                                rows = slice(DK * c, DK * c + DK)
                                z = QZ.rearrange("p (h r) -> p h r", r=136)[rows, :, :]
                                dve.wait_ge(qh, 2 * b + c + 1)
                                v.tensor_tensor(z[:, :, 64 + DS * c:64 + DS * c + DS], QS[rows, :, bass.ds(b * DS, DS)],
                                                z[:, :, DS * c:DS * c + DS].bitcast(F32), ALU.subtract).then_inc(ql, 1)

                        def shares():
                            dve.wait_ge(exd, i + 1)
                            links.link(v.reciprocal(rc[0:64, :], sm[0:64, :]))
                            links.link(v.tensor_tensor(cf[0:64, :], rc[0:64, :], sgn[0:64, :], ALU.mult))
                            v.tensor_scalar(SR[0:64, :], SR[0:64, :], cf[0:64, :], None, ALU.mult).then_inc(wd, 1)

                        def weights_low():
                            dve.wait_ge(wtp, i + 1)
                            v.tensor_reduce(WS[:, 0:PAGES * TS].rearrange("p (a q) -> p a q", q=DS),
                                            BK[7].rearrange("p (a c q) -> p a q c", c=2, q=DS), AX, ALU.add)
                            v.tensor_reduce(WS[0:TS, PAGES * TS:NB * TS].rearrange("p (a q) -> p a q", q=DS),
                                            BK[3][0:TS, G:G + 64].rearrange("p (a c q) -> p a q c", c=2, q=DS),
                                            AX, ALU.add).then_inc(wr, 1)
                            dve.wait_ge(whi, i + 1)
                            dve.wait_ge(wr, i + 1)
                            ws = WS.rearrange("p (a c) -> p a c", a=NB)
                            v.tensor_tensor(WTS[:, 0:PAGES, TS:2 * TS], ws[:, 0:PAGES, :],
                                            WTS[:, 0:PAGES, 0:TS].bitcast(F32), ALU.subtract)
                            v.tensor_tensor(WTS[0:TS, PAGES, TS:2 * TS], ws[0:TS, PAGES, :],
                                            WTS[0:TS, PAGES, 0:TS].bitcast(F32), ALU.subtract).then_inc(wlo, 1)

                        for step in ORDER:
                            if step[0] == "K" and keys:
                                k_low(int(step[1]))
                            elif step[0] == "R" and keys:
                                if step == "R0" and values:
                                    dve.wait_ge(wtp, i + 1)
                                add_rows(b, int(step[1]))
                            elif step == "L" and keys:
                                maximum()
                            elif step == "Q" and keys:
                                queries()
                            elif step == "E" and values:
                                shares()
                            elif step == "W" and values:
                                weights_low()
                            elif step[0] == "V" and values and int(step[1]) % 4 < 3:
                                v_low(int(step[1]))
                    sequences(dve, body, links, 4)

                @block.tensor
                def _(pe):
                    pe.wait_ge(d_in, 48)
                    for h in range(H):
                        nc.tensor.transpose(BK[2][:, h * TS:(h + 1) * TS],
                                            RAW[0:TS, 3 * D + h * P:3 * D + (h + 1) * P], ident[0:TS, 0:TS])
                    for h in range(H):
                        x = nc.tensor.transpose(BK[2][:, (H + h) * TS:(H + h + 1) * TS],
                                                RAW[0:TS, 4 * D + h * P:4 * D + (h + 1) * P], ident[0:TS, 0:TS])
                    x.then_inc(pre, 1)
                    pe.wait_ge(vn, 3)

                    def body(b, keys, values):
                        i = b - 1

                        def turn(p):
                            pe.wait_ge(k_ld[p % 4], 16 * (2 * b + p // 4 + 1))
                            for j in range(2):
                                wait(pe, kl, 2 * PAGES * b + (2 * p + j - 1))
                                for h in range(4):
                                    x = nc.tensor.transpose(BK[j][:, h * P:(h + 1) * P],
                                                            KB[:, p % 4, (4 * j + h) * P:(4 * j + h + 1) * P], ident)
                                x.then_inc(tp, 1)

                        def score(g):
                            bank, at, n = S_AT[g]
                            pe.wait_ge(kl, 2 * PAGES * b + 4 * (g + 1))
                            if g == 0:
                                pe.wait_ge(ql, 2 * b + 2)
                            wait(pe, add, 3 * i + (1, 1, 2, 3)[g])
                            m = 0
                            for h in range(H):
                                for k in (XH, XL):
                                    x = nc.tensor.matmul(bank[:, at:at + n], QZ[:, h * P:(h + 1) * P],
                                                         k[:, h, g * G:g * G + n], start=(m == 0), stop=(m == 2 * H - 1))
                                    m += 1
                            x.then_inc(sc, 1)

                        def weights():
                            pe.wait_ge(wd, i + 1)
                            apart(pe)
                            for p in range(PAGES):
                                nc.tensor.transpose(BK[7][:, p * 64:(p + 1) * 64], SR[0:64, p * P:(p + 1) * P],
                                                    ident[0:64, 0:64])
                            nc.tensor.transpose(BK[3][0:TS, G:G + 64], SR[0:64, NEW:TOK], ident[0:64, 0:64])\
                              .then_inc(wtp, 1)

                        def value(p):
                            if p % 4 == 3:
                                pe.wait_ge(vlp, 2 * i + p // 4 + 1)
                            else:
                                pe.wait_ge(vl, 6 * i + (p + 1 if p < 3 else p))
                            if p == 0:
                                pe.wait_ge(wlo, i + 1)
                                wait(pe, avc, i)
                            for j in range(2):
                                for w in (VH, VL):
                                    x = nc.tensor.matmul(OUT[0:64, j, :], WTS[:, p, :], w[p % 4][:, 512 * j:512 * j + 512],
                                                         start=(p == 0 and w is VH), stop=False)
                            x.then_inc(av, 1)

                        def new_value():
                            for j in range(2):
                                for w in (VHN, VLN):
                                    x = nc.tensor.matmul(OUT[0:64, j, :], WTS[0:TS, PAGES, :],
                                                         w[0:TS, 512 * j:512 * j + 512], start=False, stop=(w is VLN))
                            x.then_inc(avd, 1)

                        for step in PE_ORDER:
                            if step[0] == "T" and keys:
                                turn(int(step[1]))
                            elif step[0] == "S" and keys:
                                score(int(step[1]))
                            elif step[0] == "V" and values:
                                value(int(step[1]))
                            elif step == "W" and values:
                                weights()
                            elif step == "N" and values:
                                new_value()
                    sequences(pe, body)


        run(norm_phase)
        run(gates_phase)
        run(mlstm_phase)
        run(mlstm_sample_phase)
        run(out_phase, "oa", w_out_a, True)
        fresh_semaphores()
        run(attention_phase)
        run(decode_phase)
        run(out_phase, "ob", w_out_b, False)
        fresh_semaphores()



_INS = ['x_prompt', 'x_sample', 'cache_k', 'cache_v', 'state_C', 'state_n', 'state_m', 'page_table',
        'norm_g', 'w_in_a', 'b_i_a', 'b_f_a', 'hnorm_a', 'w_out_a', 'kv_norm_g', 'w_kv', 'w_in_b',
        'lam_q1', 'lam_k1', 'lam_q2', 'lam_k2', 'subln_b', 'w_out_b', 'final_norm_g']
_OUTS = [(1, SEQ, D), (DB, DS, D), (1, SEQ, H, 2, DK), (1, SEQ, H, P), (1, 1, H, P, P), (1, 1, H, P), (1, 1, H),
         (DB, DS, H, 2, DK), (DB, DS, H, P), (1, DB, H, P, P), (1, DB, H, P), (1, DB, H)]


def kernel(**inputs):
    import numpy as _np
    import concourse.bacc as _bacc
    from concourse import mybir as _mybir
    from concourse.bass_utils import run_bass_kernel_spmd as _run

    nc = _bacc.Bacc("TRN2", target_bir_lowering=False, num_devices=1)
    arrays, args = {}, []
    for name in _INS:
        a = _np.ascontiguousarray(inputs[name])
        arrays[f"in_{name}"] = a
        args.append(nc.dram_tensor(f"in_{name}", a.shape, _mybir.dt.from_np(a.dtype), kind="ExternalInput").ap())
    c = constants()
    arrays["in_consts"] = c
    args.append(nc.dram_tensor("in_consts", c.shape, _mybir.dt.float32, kind="ExternalInput").ap())
    for i, shape in enumerate(_OUTS):
        args.append(nc.dram_tensor(f"out_{i}", shape, _mybir.dt.float32, kind="ExternalOutput").ap())
    trunk_step(nc, *args)
    r = _run(nc, [arrays], core_ids=[0])
    return tuple(r.results[0][f"out_{i}"] for i in range(len(_OUTS)))
```
